# Optimizing a Trainium2 kernel written in Bass

```python
import math
import jax, jax.numpy as jnp
from jax import lax
import numpy as np

D_MODEL = 1024
BATCH = 1
SEQ = 512
DEPTH = 1
DEC_BATCH = 1
DEC_SEQ = 256
PAST_LEN = 128

N_META = 16
N_HEADS = 8
NOPE_DIM = 128
ROPE_DIM = 64
V_DIM = 128
Q_LORA = 512
KV_LORA = 256
ROPE_THETA = 10000.0
Q_BLOCK = 128
D_CONV = D_MODEL
CONV_WIDTH = 31
CONV_PAD = CONV_WIDTH // 2
D_FF = 4 * D_MODEL
N_GATE = 2 * D_MODEL
EPS = 1e-6
SPLITS = [Q_LORA, Q_LORA + KV_LORA, Q_LORA + KV_LORA + ROPE_DIM,
          Q_LORA + KV_LORA + ROPE_DIM + 2 * D_CONV]
N_IN = Q_LORA + KV_LORA + ROPE_DIM + 2 * D_CONV + N_GATE

kernel_name = "mla_conformer_gated_hybrid_encoder"

def _rms(x, g):
    xf = x.astype(jnp.float32)
    y = xf * lax.rsqrt(jnp.mean(xf * xf, axis=-1, keepdims=True) + EPS)
    return (y * g.astype(jnp.float32)).astype(x.dtype)

def _layernorm(x, g, b):
    xf = x.astype(jnp.float32)
    mu = jnp.mean(xf, axis=-1, keepdims=True)
    var = jnp.mean(jnp.square(xf - mu), axis=-1, keepdims=True)
    y = (xf - mu) * lax.rsqrt(var + EPS)
    return (y * g.astype(jnp.float32) + b.astype(jnp.float32)).astype(x.dtype)

def _rope_cs(L):
    inv = ROPE_THETA ** (-jnp.arange(0, ROPE_DIM, 2, dtype=jnp.float32) / ROPE_DIM)
    ang = jnp.arange(L, dtype=jnp.float32)[:, None] * inv[None, :]
    return jnp.cos(ang), jnp.sin(ang)

def _apply_rope(x, cos, sin):
    x1, x2 = jnp.split(x, 2, axis=-1)
    c = cos.astype(x.dtype)
    s = sin.astype(x.dtype)
    return jnp.concatenate([x1 * c - x2 * s, x2 * c + x1 * s], axis=-1)

def _mla_attention(q_n, q_r, k_n, k_r, v):
    B, L, H, _ = q_n.shape
    nblk = -(-L // Q_BLOCK)
    pad = nblk * Q_BLOCK - L
    scale = 1.0 / math.sqrt(NOPE_DIM + ROPE_DIM)

    def blocks(t):
        t = jnp.pad(t, ((0, 0), (0, pad), (0, 0), (0, 0)))
        return t.reshape(B, nblk, Q_BLOCK, H, t.shape[-1]).transpose(1, 0, 2, 3, 4)

    def one(args):
        qn_b, qr_b = args
        s = (jnp.einsum('bqhd,bkhd->bhqk', qn_b, k_n)
             + jnp.einsum('bqhr,bkr->bhqk', qr_b, k_r))
        p = jax.nn.softmax(s.astype(jnp.float32) * scale, axis=-1).astype(v.dtype)
        return jnp.einsum('bhqk,bkhd->bqhd', p, v)

    o = lax.map(one, (blocks(q_n), blocks(q_r)))
    o = o.transpose(1, 0, 2, 3, 4).reshape(B, nblk * Q_BLOCK, H, V_DIM)[:, :L]
    return o

def _encode(x, meta_tokens, norm_mix, w_in, b_gate, norm_q, w_uq, norm_kv, w_ukv,
            w_o_attn, conv_w, conv_b, conv_ln_g, conv_ln_b, w_conv_out, w_out,
            norm_mlp, w_mlp_in, w_mlp_out, norm_final):
    B = x.shape[0]
    meta = jnp.broadcast_to(meta_tokens.astype(x.dtype)[None], (B, N_META, D_MODEL))
    h = jnp.concatenate([meta, x], axis=1)
    L = h.shape[1]
    cos, sin = _rope_cs(L)
    for l in range(DEPTH):
        u = _rms(h, norm_mix[l])
        proj = u @ w_in[l]
        c_q, c_kv, k_r, conv_in, gate_logits = jnp.split(proj, SPLITS, axis=-1)

        q = (_rms(c_q, norm_q[l]) @ w_uq[l]).reshape(B, L, N_HEADS, NOPE_DIM + ROPE_DIM)
        q_n = q[..., :NOPE_DIM]
        q_r = _apply_rope(q[..., NOPE_DIM:], cos[:, None, :], sin[:, None, :])
        kv = (_rms(c_kv, norm_kv[l]) @ w_ukv[l]).reshape(B, L, N_HEADS, NOPE_DIM + V_DIM)
        k_n = kv[..., :NOPE_DIM]
        v = kv[..., NOPE_DIM:]
        k_r = _apply_rope(k_r, cos, sin)
        attn = _mla_attention(q_n, q_r, k_n, k_r, v).reshape(B, L, N_HEADS * V_DIM) @ w_o_attn[l]

        a, b = jnp.split(conv_in, 2, axis=-1)
        c = a * jax.nn.sigmoid(b)
        c = lax.conv_general_dilated(
            c, conv_w[l][:, None, :].astype(c.dtype), window_strides=(1,),
            padding=[(CONV_PAD, CONV_PAD)], dimension_numbers=('NWC', 'WIO', 'NWC'),
            feature_group_count=D_CONV) + conv_b[l]
        c = jax.nn.silu(_layernorm(c, conv_ln_g[l], conv_ln_b[l]))
        conv = c @ w_conv_out[l]

        g_a, g_c = jnp.split(jax.nn.sigmoid(gate_logits + b_gate[l]), 2, axis=-1)
        h = h + (g_a * attn + g_c * conv) @ w_out[l]

        u = _rms(h, norm_mlp[l])
        h = h + jnp.square(jax.nn.relu(u @ w_mlp_in[l])) @ w_mlp_out[l]
    return _rms(h, norm_final)[:, N_META:]

def setup_inputs(seed: int = 0) -> dict:
    key = jax.random.key(seed)
    ks = jax.random.split(key, 24)
    f32 = jnp.float32

    def nrm(k, shape, scale):
        return jax.random.normal(k, shape, f32) * scale

    def gain(k, shape):
        return 1.0 + 0.02 * jax.random.normal(k, shape, f32)

    return {
        "x_prompt": jax.random.normal(ks[0], (BATCH, SEQ, D_MODEL), f32),
        "x_sample": jax.random.normal(ks[1], (DEC_BATCH, DEC_SEQ, D_MODEL), f32),
        "meta_tokens": nrm(ks[2], (N_META, D_MODEL), 1.0),
        "norm_mix": gain(ks[3], (DEPTH, D_MODEL)),
        "w_in": nrm(ks[4], (DEPTH, D_MODEL, N_IN), D_MODEL ** -0.5),
        "b_gate": nrm(ks[5], (DEPTH, N_GATE), 0.01),
        "norm_q": gain(ks[6], (DEPTH, Q_LORA)),
        "w_uq": nrm(ks[7], (DEPTH, Q_LORA, N_HEADS * (NOPE_DIM + ROPE_DIM)), Q_LORA ** -0.5),
        "norm_kv": gain(ks[8], (DEPTH, KV_LORA)),
        "w_ukv": nrm(ks[9], (DEPTH, KV_LORA, N_HEADS * (NOPE_DIM + V_DIM)), KV_LORA ** -0.5),
        "w_o_attn": nrm(ks[10], (DEPTH, N_HEADS * V_DIM, D_MODEL), (N_HEADS * V_DIM) ** -0.5),
        "conv_w": nrm(ks[11], (DEPTH, CONV_WIDTH, D_CONV), CONV_WIDTH ** -0.5),
        "conv_b": nrm(ks[12], (DEPTH, D_CONV), 0.01),
        "conv_ln_g": gain(ks[13], (DEPTH, D_CONV)),
        "conv_ln_b": nrm(ks[14], (DEPTH, D_CONV), 0.01),
        "w_conv_out": nrm(ks[15], (DEPTH, D_CONV, D_MODEL), D_CONV ** -0.5),
        "w_out": nrm(ks[16], (DEPTH, D_MODEL, D_MODEL), D_MODEL ** -0.5),
        "norm_mlp": gain(ks[17], (DEPTH, D_MODEL)),
        "w_mlp_in": nrm(ks[18], (DEPTH, D_MODEL, D_FF), D_MODEL ** -0.5),
        "w_mlp_out": nrm(ks[19], (DEPTH, D_FF, D_MODEL), D_FF ** -0.5),
        "norm_final": gain(ks[20], (D_MODEL,)),
    }

def reference(x_prompt, x_sample, meta_tokens, norm_mix, w_in, b_gate, norm_q, w_uq,
              norm_kv, w_ukv, w_o_attn, conv_w, conv_b, conv_ln_g, conv_ln_b, w_conv_out,
              w_out, norm_mlp, w_mlp_in, w_mlp_out, norm_final):
    y_prompt = _encode(x_prompt, meta_tokens, norm_mix, w_in, b_gate, norm_q, w_uq, norm_kv,
                       w_ukv, w_o_attn, conv_w, conv_b, conv_ln_g, conv_ln_b, w_conv_out,
                       w_out, norm_mlp, w_mlp_in, w_mlp_out, norm_final)
    y_sample = _encode(x_sample, meta_tokens, norm_mix, w_in, b_gate, norm_q, w_uq, norm_kv,
                       w_ukv, w_o_attn, conv_w, conv_b, conv_ln_g, conv_ln_b, w_conv_out,
                       w_out, norm_mlp, w_mlp_in, w_mlp_out, norm_final)
    return (y_prompt, y_sample)


_drawn_inputs = setup_inputs


def setup_inputs(seed=0):
    import zlib

    import numpy as np

    out = dict(_drawn_inputs(seed))
    spreads = {}
    factors = {'norm_mix': 7.331,
     'b_gate': 34.289,
     'norm_q': 8.0,
     'norm_kv': 8.0,
     'conv_b': 46.656,
     'conv_ln_g': 31.578,
     'conv_ln_b': 64.0,
     'norm_mlp': 9.004,
     'norm_final': 8.82}
    for name, (base, spread) in spreads.items():
        noise = np.random.default_rng([zlib.crc32(name.encode()), seed]).standard_normal(out[name].shape)
        drawn = base * np.exp(spread * noise) if base else spread * noise
        out[name] = __import__('jax').numpy.asarray(drawn.astype(out[name].dtype))
    for name, factor in factors.items():
        out[name] = (out[name] * factor).astype(out[name].dtype)
    return out
```

```python
from contextlib import ExitStack

import numpy as np
import concourse.bass as bass
from concourse import mybir

F32 = mybir.dt.float32
F32R = mybir.dt.float32r
ALU = mybir.AluOpType
ACT = mybir.ActivationFunctionType
AX = mybir.AxisListType
ds = bass.ds

P = 128
D = 1024
KD = D // P
T_PROMPT, T_SAMPLE, T_META = 512, 256, 16
META0 = T_PROMPT
SAMP0 = T_PROMPT + T_META
TK = T_PROMPT + T_META + T_SAMPLE
TQ = T_PROMPT + T_SAMPLE
NT = TQ // P
HEADS, NOPE, ROPE, VD = 8, 128, 64, 128
PAIRS = HEADS // 2
Q_LORA, KV_LORA = 512, 256
KQ, KKV = Q_LORA // P, KV_LORA // P
TAPS, PAD = 31, 15
FF = 4 * D
KF = FF // P
EPS = 1e-6
SCALE = float((NOPE + ROPE) ** -0.5)
HALF = 512

C_Q, C_KV = 0, Q_LORA
C_KR = C_KV + KV_LORA
C_A = C_KR + ROPE
C_B = C_A + D
C_GATE = C_B + D

U_QKV = 0
U_CONV = 8
U_GATE = U_CONV + 2 * KD
U_ATT = U_GATE + 2 * KD
U_O = U_ATT + 4 * PAIRS
U_CO = U_O + KD
U_OUT = U_CO + KD
U_IN = U_OUT + KD
U_FF = U_IN + KF
U_END = U_FF + KF

VEC = {}
for _name, _rows in (("norm_mix", KD), ("norm_q", KQ), ("norm_kv", KKV), ("b_gate", 2 * KD),
                     ("conv_b", KD), ("conv_ln_g", KD), ("conv_ln_b", KD), ("norm_mlp", KD)):
    VEC[_name] = (sum(r for _, r in VEC.values()), _rows)
NVEC = sum(r for _, r in VEC.values())

CS_PROMPT = T_META
CS_GAP = CS_PROMPT + T_PROMPT
CS_META2 = CS_GAP + PAD
CS_SAMPLE = CS_META2 + T_META
CS_END = CS_SAMPLE + T_SAMPLE
CS_ALL = 832
SPAN = CS_END - CS_PROMPT
ACC_SAMPLE = CS_SAMPLE - CS_PROMPT

VTILES = [0, 128, 256, 384, META0, META0 + 128, SAMP0 - 128, TK - 128]
GROUPS = [
    dict(k0=0, nk=SAMP0, pieces=((0, SAMP0 // 2), (SAMP0 // 2, SAMP0 // 2)),
         tiles=((0, 0), (1, 128), (2, 256), (3, 384), (6, SAMP0 - 128))),
    dict(k0=META0, nk=TK - META0, pieces=((0, TK - META0),),
         tiles=((4, 0), (5, 128), (7, TK - META0 - 128))),
]

SB0 = 16512
Z0 = SB0 + 36352


def build(nc, t):
    with ExitStack() as ctx:
        def at(name, shape, dt, offset):
            return nc.alloc_sbuf_tensor_at(name, shape, dt, offset=offset)

        def sem(name):
            return ctx.enter_context(nc.semaphore(name))

        psum = ctx.enter_context(nc.psum_tensor("psum", [P, 4, 2 * HALF], F32))
        bank = psum[:].rearrange("p a (b n) -> p (a b) n", n=HALF)

        ident = at("ident", [P, P], F32, SB0)
        ones = at("ones", [P, P], F32, SB0 + 512)
        vec = at("vec", [P, NVEC], F32, SB0 + 1024)
        convw = at("convw", [P, KD, TAPS], F32, SB0 + 1280)
        eps = at("eps", [P, 1], F32, SB0 + 2272)
        tail_mask = at("tail_mask", [P, 1], F32, SB0 + 2304)
        sumsq = at("sumsq", [P, 8], F32, SB0 + 2336)
        root = at("root", [P, 8], F32, SB0 + 2368)
        rstd = at("rstd", [P, 8], F32, SB0 + 2400)
        negmax = at("negmax", [P, 4], F32, SB0 + 2432)
        psumexp = at("psumexp", [P, 4], F32, SB0 + 2464)
        rsum = at("rsum", [P, 4], F32, SB0 + 2496)
        raw = at("raw", [P, 4, D], F32, SB0 + 3584)
        whi = at("whi", [P, 2, D], F32R, SB0 + 3584 + 16384)
        wlo = at("wlo", [P, 2, D], F32R, SB0 + 3584 + 24576)

        cs = at("cs", [P, KD, CS_ALL], F32, Z0)
        acc = at("acc", [P, 2, 800], F32, Z0 + 26624)
        lnsum = at("lnsum", [P, TQ], F32, Z0 + 33024)
        qhi = at("qhi", [P, KQ, TQ], F32R, Z0 + 36096)
        qlo = at("qlo", [P, KQ, TQ], F32R, Z0 + 48384)
        kvhi = at("kvhi", [P, KKV, TK], F32R, Z0 + 60672)
        kvlo = at("kvlo", [P, KKV, TK], F32R, Z0 + 66944)
        kra = at("kra", [P, TK], F32R, Z0 + 73216)
        krb = at("krb", [P, TK], F32R, Z0 + 76352)
        rcos = at("rcos", [P, TK], F32, Z0 + 79488)
        rsin = at("rsin", [P, TK], F32, Z0 + 82624)
        V0 = Z0 + 85760
        xt = at("xt", [P, 7, D], F32, Z0)
        vecrows = at("vecrows", [P, P], F32, V0 + 50176)
        tapsrows = at("tapsrows", [32, D], F32, V0 + 50176 + 512)
        junk0 = at("junk0", [P, D], F32, V0 + 50176 + 4608)
        uhi = at("uhi", [P, KD, TK], F32R, V0)
        ulo = at("ulo", [P, KD, TK], F32R, V0 + 25088)
        qraw = at("qraw", [P, KQ, TQ], F32, V0 + 50176)
        kvraw = at("kvraw", [P, KKV, TK], F32, V0 + 62464)
        sqacc = at("sqacc", [P, 2, TK], F32, V0 + 68736)
        sqt = at("sqt", [P, 2, TK], F32, V0 + 75008)
        krsw = at("krsw", [P, TK], F32, V0 + 81280)
        krt = at("krt", [P, TK], F32, V0 + 84416)
        sg = at("sg", [P, 2, TK], F32, V0 + 75008)
        gout = at("gout", [P, 2, TQ], F32, V0 + 62464)
        qnhi = at("qnhi", [P, TQ], F32R, V0)
        qnlo = at("qnlo", [P, TQ], F32R, V0 + 3072)
        knhi = at("knhi", [P, TK], F32R, V0 + 6144)
        knlo = at("knlo", [P, TK], F32R, V0 + 9280)
        qrs = [at(f"qrs{e}", [P, TQ], F32R, V0 + 12416 + 3072 * e) for e in range(2)]
        qsw = at("qsw", [P, TQ], F32, V0 + 18560)
        qt = at("qt", [P, TQ], F32, V0 + 21632)
        vhi = at("vhi", [P, 8, 2 * VD], F32R, V0 + 24704)
        vlo = at("vlo", [P, 8, 2 * VD], F32R, V0 + 32896)
        prob = at("prob", [P, 2, SAMP0], F32, V0 + 41088)
        pthi = at("pthi", [P, 2, 5, 2 * P], F32R, V0 + 45312)
        ptlo = at("ptlo", [P, 2, 5, 2 * P], F32R, V0 + 55552)
        oraw = at("oraw", [P, HEADS, TQ], F32, V0 + 65792)
        ohi = at("ohi", [P, KD, TQ], F32R, Z0 + 36096)
        olo = at("olo", [P, KD, TQ], F32R, Z0 + 60672)
        gin = at("gin", [P, 2, TQ], F32, Z0 + 26624)
        zacc = at("zacc", [P, KD, TQ], F32, Z0 + 85760)
        chi = at("chi", [P, KD, TQ], F32R, Z0 + 110336)
        clo = at("clo", [P, KD, TQ], F32R, Z0 + 151552)
        mu = at("mu", [P, TQ], F32, Z0 + 134912)
        lnr = at("lnr", [P, TQ], F32, Z0 + 137984)
        lnsq = at("lnsq", [P, 2, TQ], F32, Z0 + 141056)
        lnacc = at("lnacc", [P, TQ], F32, Z0 + 147200)
        gconv = at("gconv", [P, TQ], F32, Z0 + 134912)
        zhi = at("zhi", [P, KD, TQ], F32R, Z0 + 36096)
        zlo = at("zlo", [P, KD, TQ], F32R, Z0 + 60672)
        h1 = at("h1", [P, NT, D], F32, Z0)
        hs1 = at("hs1", [P, NT, D], F32, Z0 + 85760)
        junk1 = at("junk1", [P, D], F32, Z0 + 110336)
        hid = at("hid", [P, KF, TQ], F32, Z0 + 24576)
        u2hi = at("u2hi", [P, KD, TQ], F32R, Z0 + 122880)
        u2lo = at("u2lo", [P, KD, TQ], F32R, Z0 + 147456)
        hidhi = at("hidhi", [P, 2, 2, TQ], F32R, Z0 + 122880)
        hidlo = at("hidlo", [P, 2, 2, TQ], F32R, Z0 + 135168)
        yout = at("yout", [P, NT, D], F32, Z0 + 147456)
        gfinal = at("gfinal", [P, D], F32, Z0 + 172032)
        junk2 = at("junk2", [P, D], F32, Z0 + 24576)

        gates = nc.dram_tensor("gates", [2 * KD, P, TQ], F32, kind="Internal").ap()

        raw_landed = [sem(f"raw_landed{s}") for s in range(4)]
        hi_ready, lo_ready, unit_used = sem("hi_ready"), sem("lo_ready"), sem("unit_used")
        dup_landed = [sem(f"dup_landed{e}") for e in range(2)]
        kw_landed = [sem(f"kw_landed{e}") for e in range(2)]
        x_landed = [sem(f"x_landed{i}") for i in range(7)]
        consts_landed, taps_landed, tables_landed = sem("consts_landed"), sem("taps_landed"), sem("tables_landed")
        setup, vec_clear, vec_t, vec_ready = sem("setup"), sem("vec_clear"), sem("vec_t"), sem("vec_ready")
        x_sq, x_root, x_rstd, x_scaled = sem("x_sq"), sem("x_root"), sem("x_rstd"), sem("x_scaled")
        ut_ready, uhi_ready, ulo_ready = sem("ut_ready"), sem("uhi_ready"), sem("ulo_ready")
        raw_q, q_sq, sq_sum = sem("raw_q"), sem("q_sq"), sem("sq_sum")
        ss_mm, ss_root, ss_rstd = sem("ss_mm"), sem("ss_root"), sem("ss_rstd")
        qkv_scaled, qkv_hi, qkv_lo = sem("qkv_scaled"), sem("qkv_hi"), sem("qkv_lo")
        kr_sw, kr_cos, kr_sin, kr_rot, kr_hi, kr_lo = (sem("kr_sw"), sem("kr_cos"), sem("kr_sin"),
                                                       sem("kr_rot"), sem("kr_hi"), sem("kr_lo"))
        pads_zero, sg_ready, glu_ready = sem("pads_zero"), sem("sg_ready"), sem("glu_ready")
        tap_done, conv_done, lnsum_done = sem("tap_done"), sem("conv_done"), sem("lnsum_done")
        gate_ready = sem("gate_ready")
        gate_stored = [sem(f"gate_stored{e}") for e in range(2)]
        v_mm, v_hi, v_lo = sem("v_mm"), sem("v_hi"), sem("v_lo")
        qr_sw, qr_cos, qr_sin, qr_rot, qr_hi, qr_lo = (sem("qr_sw"), sem("qr_cos"), sem("qr_sin"),
                                                       sem("qr_rot"), sem("qr_hi"), sem("qr_lo"))
        qn_mm, qn_hi, qn_lo, kn_hi, kn_lo = sem("qn_mm"), sem("qn_hi"), sem("qn_lo"), sem("kn_hi"), sem("kn_lo")
        s_ready, max_ready, exp_ready, rsum_ready, p_ready = (sem("s_ready"), sem("max_ready"),
                                                              sem("exp_ready"), sem("rsum_ready"), sem("p_ready"))
        pt_mm, pt_hi, pt_lo, av_mm, o_ready = sem("pt_mm"), sem("pt_hi"), sem("pt_lo"), sem("av_mm"), sem("o_ready")
        o_hi, o_lo = sem("o_hi"), sem("o_lo")
        gin_landed = [sem(f"gin_landed{e}") for e in range(2)]
        mean_mm, mu_ready, centred, ln_sq, ln_sqsum = (sem("mean_mm"), sem("mu_ready"), sem("centred"),
                                                       sem("ln_sq"), sem("ln_sqsum"))
        var_mm, ln_root, ln_rstd, ln_scaled, c_silu, c_hi, c_lo = (
            sem("var_mm"), sem("ln_root"), sem("ln_rstd"), sem("ln_scaled"), sem("c_silu"), sem("c_hi"), sem("c_lo"))
        merged, gated, z_hi, z_lo = sem("merged"), sem("gated"), sem("z_hi"), sem("z_lo")
        h_landed, h_ready = [sem(f"h_landed{i}") for i in range(2)], sem("h_ready")
        h_sq, h_root, h_rstd, h_scaled = sem("h_sq"), sem("h_root"), sem("h_rstd"), sem("h_scaled")
        u2t_ready, u2hi_ready, u2lo_ready = sem("u2t_ready"), sem("u2hi_ready"), sem("u2lo_ready")
        relu_ready, hid_ready = sem("relu_ready"), sem("hid_ready")
        hidhi_ready, hidlo_ready = sem("hidhi_ready"), sem("hidlo_ready")
        gfinal_landed, y_ready, y_sq, y_root, y_rstd, y_out, y_stored = (
            sem("gfinal_landed"), sem("y_ready"), sem("y_sq"), sem("y_root"), sem("y_rstd"), sem("y_out"), sem("y_stored"))

        waits_apart = sem("waits_apart")

        def wait(eng, s, value):
            if not isinstance(value, int) or value > 0:
                eng.wait_ge(s, value)

        def wait_apart(eng, s, value):
            wait(eng, s, value)
            if not isinstance(value, int):
                eng.sem_inc(waits_apart, 1)

        def rolled(eng, count, body, peel=1, last=0):
            for i in range(peel):
                body(i)
            if count - peel - last > 0:
                with eng.Fori(peel, count - last) as i:
                    body(i)
            for i in range(count - last, count):
                body(i)

        def hi_unit(act, base, i, c):
            act.wait_ge(raw_landed[c % 4], (i + (base // 4 + c // 4 + 1)) * 16)
            wait(act, unit_used, i * 4 + (base + c - 1))
            nc.scalar.activation(whi[:, c % 2], raw[:, c % 4], ACT.Copy).then_inc(hi_ready, 1)

        def lo_unit(gp, base, i, c):
            gp.wait_ge(hi_ready, i * 4 + (base + c + 1))
            gp.tensor_tensor(out=wlo[:, c % 2], in0=raw[:, c % 4], in1=whi[:, c % 2].bitcast(F32),
                             op=ALU.subtract).then_inc(lo_ready, 1)

        def weights(s, k, m=P):
            return (whi[:, s, 0:k * m].rearrange("p (k m) -> p k m", k=k),
                    wlo[:, s, 0:k * m].rearrange("p (k m) -> p k m", k=k))

        def products(out, lhs, rhs, k, segments, first, last):
            (lh, ll), (rh, rl) = lhs, rhs
            mm = None
            for step, (a, b) in enumerate(((lh, rh), (lh, rl), (ll, rh))):
                for o0, c0, n in segments:
                    mm = nc.tensor.matmul(out[:, o0:o0 + n], a, b[:, k, c0:c0 + n],
                                          start=first and step == 0, stop=last and step == 2)
            return mm

        KSEG = ((0, 0, HALF), (HALF, HALF, TK - HALF))
        QSEG = ((0, 0, T_PROMPT), (T_PROMPT, SAMP0, T_SAMPLE))
        ZSEG = ((0, 0, HALF), (HALF, HALF, TQ - HALF))

        def vcol(name, k):
            r = VEC[name][0]
            return vec[:, ds(k + r, 1)] if not isinstance(k, int) else vec[:, r + k:r + k + 1]

        def head_events(eng_list, handlers, p, hh):
            for kind, q in eng_list:
                handlers[kind](p, hh, q)

        def qtile(q):
            return (GROUPS[0] if q < 4 else GROUPS[1]), q * P

        def sum_squares(pe, a, w, count):
            pe.wait_ge(sq_sum, count)
            for c0, n in ((0, HALF), (HALF, w - HALF)):
                mm = nc.tensor.matmul(psum[:, 3, c0:c0 + n], ones[:, :], sqacc[:, a, c0:c0 + n], start=True, stop=True)
            mm.then_inc(ss_mm, 1)

        block = ctx.enter_context(nc.Block())

        @block.sync
        def _(sp):
            xs = [t["x_prompt"][0, i * P:(i + 1) * P, :] for i in range(4)]
            xs += [t["x_sample"][0, i * P:(i + 1) * P, :] for i in range(2)]
            for i in range(2):
                sp.dma_start(xt[:, i], xs[i]).then_inc(x_landed[i], 16)
            sp.dma_start(xt[0:T_META, 6], t["meta_tokens"]).then_inc(x_landed[6], 16)
            for i in range(2, 6):
                sp.dma_start(xt[:, i], xs[i]).then_inc(x_landed[i], 16)

            win = t["w_in"][0].rearrange("(k p) n -> p k n", p=P)

            def columns(w, n, base, i, c, col):
                wait_apart(sp, lo_ready, i * 4 + (base + c - 3))
                sp.dma_start(raw[:, c].rearrange("p (k m) -> p k m", k=KD), w[:, :, col]) \
                  .then_inc(raw_landed[c], 16)

            for n in range(6):
                col = n * P
                columns(win, n, 4 * (n // 4), 0, n % 4, slice(col, col + P))
            sp.dma_start(rcos[:, :], t["rope_cos"]).then_inc(tables_landed, 16)
            sp.dma_start(rsin[:, :], t["rope_sin"]).then_inc(tables_landed, 16)
            for e in range(2):
                sp.wait_ge(lo_ready, 6 + e - 3)
                r = raw[:, 2 + e, 0:4 * P].rearrange("p (k m) -> p k m", k=4)
                w = win[:, 4 * e:4 * e + 4, C_KR:C_KR + ROPE]
                sp.dma_start(r[:, :, 0:ROPE], w).then_inc(raw_landed[2 + e], 16)
                sp.dma_start(r[:, :, ROPE:P], w).then_inc(dup_landed[e], 16)

            def conv_units(i):
                for c in range(4):
                    first = C_B if c % 2 == 0 else C_A
                    columns(win, None, U_CONV, i, c, ds(i * (2 * P) + (first + (c // 2) * P), P))
            rolled(sp, 4, conv_units, peel=0)

            def gate_units(i):
                for c in range(4):
                    columns(win, None, U_GATE, i, c, ds(i * (4 * P) + (C_GATE + c * P), P))
            rolled(sp, 4, gate_units, peel=0)

            uq = t["w_uq"][0].rearrange("(k p) (a h e) -> p k a h e", p=P, h=2, e=NOPE + ROPE)
            ukv = t["w_ukv"][0].rearrange("(k p) (a h v d) -> p k a h v d", p=P, h=2, v=2, d=VD)

            def pair_units(i):
                wait_apart(sp, lo_ready, i * 4 + (U_ATT - 3))
                for h in range(2):
                    d = sp.dma_start(raw[:, 0, 0:KKV * 2 * VD].rearrange("p (k h d) -> p k h d", k=KKV, h=2)[:, :, h],
                                     ukv[:, :, ds(i, 1), h, 1].rearrange("p k a d -> p k (a d)"))
                    d.then_inc(raw_landed[0] if h == 0 else dup_landed[0], 16)
                wait_apart(sp, lo_ready, i * 4 + (U_ATT - 2))
                for h in range(2):
                    d = sp.dma_start(raw[:, 1, 0:KQ * P].rearrange("p (k h e) -> p k h e", k=KQ, h=2)[:, :, h],
                                     uq[:, :, ds(i, 1), h, NOPE:NOPE + ROPE].rearrange("p k a e -> p k (a e)"))
                    d.then_inc(raw_landed[1] if h == 0 else dup_landed[1], 16)
                for h in range(2):
                    wait_apart(sp, lo_ready, i * 4 + (U_ATT - 1 + h))
                    sp.dma_start(raw[:, 2 + h, 0:KQ * P].rearrange("p (k m) -> p k m", k=KQ),
                                 uq[:, :, ds(i, 1), h, 0:NOPE].rearrange("p k a e -> p k (a e)")) \
                      .then_inc(raw_landed[2 + h], 16)
                    sp.dma_start(raw[:, 2 + h, KQ * P:(KQ + KKV) * P].rearrange("p (k m) -> p k m", k=KKV),
                                 ukv[:, :, ds(i, 1), h, 0].rearrange("p k a d -> p k (a d)")) \
                      .then_inc(kw_landed[h], 16)
            rolled(sp, PAIRS, pair_units, peel=0)

            def gate_back(g):
                if g < 2:
                    sp.wait_ge(conv_done, KD)
                    for e in range(2):
                        sp.wait_ge(gate_stored[e], 16 * KD)
                wait(sp, merged, g - 1)
                sp.dma_start(gin[:, g % 2], gates[g]).then_inc(gin_landed[g % 2], 16)

            projections = [t[name][0].rearrange("(k p) n -> p k n", p=P) for name in ("w_o_attn", "w_conv_out")]
            for g in range(2 * KD + 3):
                m = g % KD
                if g < 2 * KD:
                    columns(projections[g // KD], None, U_O + g - g % 4, 0, g % 4, slice(m * P, (m + 1) * P))
                if g >= 3:
                    gate_back(g - 3)
            sp.wait_ge(c_lo, KD)
            for g, (name, t0, nt) in enumerate((("x_prompt", 0, 4), ("x_sample", 4, 2))):
                sp.dma_start(h1[:, t0:t0 + nt], t[name][0].rearrange("(t p) n -> p t n", p=P)) \
                  .then_inc(h_landed[g], 16)

            def row_units(w, base, half, k0):
                def body(i):
                    for c in range(4):
                        wait_apart(sp, lo_ready, i * 4 + (base + c - 3))
                        sp.dma_start(raw[:, c].rearrange("p (k n) -> p k n", k=2),
                                     w[:, ds(i * 4 + c, 1), :, half * HALF:(half + 1) * HALF]
                                     .rearrange("p u k n -> p (u k) n")).then_inc(raw_landed[c], 16)
                return body
            wo = t["w_out"][0].rearrange("(u k p) n -> p u k n", k=2, p=P)
            for half in range(2):
                rolled(sp, 1, row_units(wo, U_OUT + 4 * half, half, 0), peel=1)
            wi = t["w_mlp_in"][0].rearrange("(k p) n -> p k n", p=P)

            def in_units(i):
                for c in range(4):
                    columns(wi, None, U_IN, i, c, ds(i * (4 * P) + c * P, P))
            rolled(sp, KF // 4, in_units, peel=0)
            wm = t["w_mlp_out"][0].rearrange("(u k p) n -> p u k n", k=2, p=P)
            for half in range(2):
                rolled(sp, KF // 8, row_units(wm, U_FF + 16 * half, half, 0), peel=0)
            sp.wait_ge(u2lo_ready, KD)
            sp.dma_start(gfinal[:, :], t["norm_final"].rearrange("(a n) -> a n", a=1).to_broadcast([P, D])) \
              .then_inc(gfinal_landed, 16)
            for i in range(NT):
                sp.wait_ge(y_out, i + 1)
                dst = t["y_prompt"][0, i * P:(i + 1) * P, :] if i < 4 else t["y_sample"][0, (i - 4) * P:(i - 3) * P, :]
                sp.dma_start(dst, yout[:, i]).then_inc(y_stored, 16)
            sp.wait_ge(y_stored, 16 * NT)

        @block.scalar
        def _(act):
            act.wait_ge(vec_clear, 1)
            for name, (r, n) in VEC.items():
                src = t[name] if name != "b_gate" else t[name]
                act.dma_start(vecrows[r:r + n, :], src[0].rearrange("(k p) -> k p", p=P)).then_inc(consts_landed, 16)
            act.dma_start(tapsrows[0:TAPS, :], t["conv_w"][0]).then_inc(taps_landed, 16)

            act.wait_ge(setup, 7)
            for j, i in enumerate((0, 1, 6, 2, 3, 4, 5)):
                r = T_META if i == 6 else P
                act.wait_ge(x_landed[i], 16)
                wait(act, x_sq, j)
                nc.scalar.activation(junk0[0:r, :], xt[0:r, i], ACT.Square,
                                     accum_out=sumsq[0:r, i:i + 1]).then_inc(x_sq, 1)
            act.wait_ge(x_sq, 7)
            nc.scalar.activation(root[:, 0:7], sumsq[:, 0:7], ACT.Sqrt, bias=eps[:, 0:1],
                                 scale=1.0 / D).then_inc(x_root, 1)
            hi_unit(act, 0, 0, 0)
            act.wait_ge(vec_ready, 2)
            for k in range(KD):
                act.wait_ge(ut_ready, k + 1)
                nc.scalar.activation(uhi[:, k], psum[:, k % 4, 0:TK], ACT.Copy,
                                     scale=vcol("norm_mix", k)).then_inc(uhi_ready, 1)

            for n in range(8):
                if n in (5, 6):
                    act.wait_ge(dup_landed[n - 5], 16)
                hi_unit(act, 0, 0, n + 1) if n < 3 else hi_unit(act, 4, 0, n + 1 - 4)
                if n < 6:
                    act.wait_ge(raw_q, n + 1)
                    wait(act, sq_sum, n - 1)
                    src, w = (qraw[:, n], TQ) if n < 4 else (kvraw[:, n - 4], TK)
                    nc.scalar.activation(sqt[:, n % 2, 0:w], src, ACT.Square).then_inc(q_sq, 1)
                if n == 7:
                    act.wait_ge(unit_used, 8)
                    for b in range(4):
                        o = b ^ 1
                        ins = nc.scalar.activation(krsw[32 * o:32 * o + 32, :], psum[32 * b:32 * b + 32, 2, 0:TK], ACT.Copy)
                    ins.then_inc(kr_sw, 1)
            act.wait_ge(ss_mm, 1)
            nc.scalar.activation(sqacc[:, 0, 0:TQ], psum[:, 3, 0:TQ], ACT.Sqrt, bias=eps[:, 0:1],
                                 scale=1.0 / Q_LORA).then_inc(ss_root, 1)

            def kr_split():
                act.wait_ge(kr_rot, 1)
                nc.scalar.activation(kra[0:64, :], krt[0:64, :], ACT.Copy)
                nc.scalar.activation(krb[64:128, :], krt[64:128, :], ACT.Copy).then_inc(kr_hi, 1)

            def latent_hi(j):
                act.wait_ge(qkv_scaled, j + 1)
                dst, src = (qhi[:, j], qraw[:, j]) if j < 4 else (kvhi[:, j - 4], kvraw[:, j - 4])
                nc.scalar.activation(dst, src, ACT.Copy).then_inc(qkv_hi, 1)

            def conv_step(i, extras=()):
                for c in range(4):
                    hi_unit(act, U_CONV, i, c + 1)
                    if c % 2 == 0:
                        j = i * 2 + c // 2
                        act.wait_ge(unit_used, i * 4 + (U_CONV + c + 1))
                        wait(act, glu_ready, i * 2 + (c // 2 - 1))
                        if isinstance(i, int) and i == 0 and c == 0:
                            act.wait_ge(sq_sum, 6)
                        nc.scalar.activation(sg[:, c // 2], psum[:, 0, 0:TK], ACT.Sigmoid).then_inc(sg_ready, 1)
                    if extras and c < len(extras):
                        for f in extras[c]:
                            f()

            def kv_root():
                act.wait_ge(ss_mm, 2)
                nc.scalar.activation(sqacc[:, 1, :], psum[:, 3, 0:TK], ACT.Sqrt, bias=eps[:, 0:1],
                                     scale=1.0 / KV_LORA).then_inc(ss_root, 1)
            conv_step(0, ((kr_split,), (), (kv_root, lambda: latent_hi(0), lambda: latent_hi(1)),
                          (lambda: latent_hi(2), lambda: latent_hi(3))))
            conv_step(1, ((lambda: latent_hi(4), lambda: latent_hi(5)),))
            with act.Fori(2, 4) as i:
                conv_step(i)

            def gate_step(i):
                for c in range(4):
                    if isinstance(i, int) and i == 3 and c == 3:
                        act.wait_ge(dup_landed[0], 32)
                    hi_unit(act, U_GATE, i, c + 1)
                    act.wait_ge(unit_used, i * 4 + (U_GATE + c + 1))
                    wait(act, gate_stored[c % 2], i * 32 + 16 * (c // 2))
                    if isinstance(i, int) and i == 0 and c == 0:
                        act.wait_ge(qkv_lo, 6)
                    nc.scalar.activation(gout[:, c % 2], psum[:, c % 2, 0:TQ], ACT.Sigmoid,
                                         bias=vcol("b_gate", i * 4 + c)).then_inc(gate_ready, 1)
                    act.wait_ge(gate_ready, i * 4 + (c + 1))
                    dst = gates[ds(i * 4 + c, 1)].rearrange("a p n -> p (a n)") if not isinstance(i, int) else gates[i * 4 + c]
                    act.dma_start(dst, gout[:, c % 2]).then_inc(gate_stored[c % 2], 16)
            rolled(act, 4, gate_step, peel=1, last=1)

            for e in range(2):
                act.wait_ge(gate_stored[e], 16 * KD)

            def pair(p):
                act.wait_ge(dup_landed[1], p * 16 + 32)
                hi_unit(act, U_ATT, p, 1)
                act.wait_ge(v_mm, p + 1)
                nc.scalar.activation(vhi[:, 0:4], psum[:, 2, :].rearrange("p (t n) -> p t n", t=4), ACT.Copy).then_inc(v_hi, 1)
                act.wait_ge(unit_used, p * 4 + (U_ATT + 1))
                nc.scalar.activation(vhi[:, 4:6], psum[:, 3, 0:HALF].rearrange("p (t n) -> p t n", t=2), ACT.Copy).then_inc(v_hi, 1)
                nc.scalar.activation(vhi[:, 6:8], psum[:, 3, HALF:2 * HALF].rearrange("p (t n) -> p t n", t=2), ACT.Copy,
                                     scale=tail_mask[:, 0:1]).then_inc(v_hi, 1)
                act.wait_ge(kw_landed[0], p * 16 + 16)
                hi_unit(act, U_ATT, p, 2)
                act.wait_ge(unit_used, p * 4 + (U_ATT + 2))
                for b in range(4):
                    o = b ^ 1
                    ins = nc.scalar.activation(qsw[32 * o:32 * o + 32, :], psum[32 * b:32 * b + 32, 2, 0:TQ], ACT.Copy)
                ins.then_inc(qr_sw, 1)
                act.wait_ge(kw_landed[1], p * 16 + 16)
                hi_unit(act, U_ATT, p, 3)

                def proj(hh):
                    act.wait_ge(qn_mm, p * 2 + (hh + 1))
                    nc.scalar.activation(qnhi[:, :], psum[:, 3, 0:TQ], ACT.Copy, scale=SCALE).then_inc(qn_hi, 1)
                    act.wait_ge(unit_used, p * 4 + (U_ATT + 3 + hh))
                    nc.scalar.activation(knhi[:, :], psum[:, 2, 0:TK], ACT.Copy).then_inc(kn_hi, 1)
                proj(0)
                act.wait_ge(qr_rot, p + 1)
                nc.scalar.activation(qrs[0][0:64, :], qt[0:64, :], ACT.Copy, scale=SCALE)
                nc.scalar.activation(qrs[1][64:128, :], qt[64:128, :], ACT.Copy, scale=SCALE).then_inc(qr_hi, 1)
                return proj

            def head(p, hh, proj, before_end):
                def E(q):
                    g = p * 12 + (6 * hh + q)
                    grp, _ = qtile(q)
                    act.wait_ge(max_ready, g + 1)
                    wait(act, pt_mm, g - 1)
                    n = len(grp["pieces"])
                    src = psum[:, q % 2, :].rearrange("p (b n) -> p b n", b=2)[:, 0:n, 0:grp["pieces"][0][1]]
                    dst = prob[:, q % 2, 0:grp["nk"]].rearrange("p (b n) -> p b n", b=n)
                    nc.scalar.activation(dst, src, ACT.Exp, bias=negmax[:, q % 4:q % 4 + 1],
                                         accum_out=psumexp[:, q % 4:q % 4 + 1]).then_inc(exp_ready, 1)

                def H(q):
                    g = p * 12 + (6 * hh + q)
                    b = 3 * hh + q // 2
                    nt = len(qtile(q)[0]["tiles"])
                    act.wait_ge(pt_mm, g + 1)
                    wait(act, av_mm, p * 6 + (b - 1))
                    nc.scalar.activation(pthi[:, b % 2, 0:nt, (q % 2) * P:(q % 2 + 1) * P],
                                         psum[:, 3, 0:nt * P].rearrange("p (t n) -> p t n", t=nt),
                                         ACT.Copy).then_inc(pt_hi, 1)

                def O(b):
                    act.wait_ge(av_mm, p * 6 + (3 * hh + b + 1))
                    dst = oraw[:, ds(p * 2 + hh, 1), b * 2 * P:(b + 1) * 2 * P]
                    nc.scalar.activation(dst, psum[:, 2, 0:2 * P].rearrange("p (a n) -> p a n", a=1), ACT.Copy) \
                      .then_inc(o_ready, 1)
                E(0), E(1), E(2), H(0), E(3), H(1), O(0), E(4), H(2), E(5), H(3), O(1)
                if hh == 0:
                    proj(1)
                else:
                    before_end()
                H(4), H(5), O(2)

            def pair_step(p):
                proj = pair(p)
                head(p, 0, proj, None)
                nothing = lambda: None
                head(p, 1, proj, nothing)
                if not (isinstance(p, int) and p == PAIRS - 1):
                    act.wait_ge(dup_landed[0], p * 16 + 48)
                hi_unit(act, U_ATT, p, 4)
            rolled(act, PAIRS, pair_step, peel=1, last=1)

            act.wait_ge(o_ready, 3 * HEADS)
            for h in range(HEADS):
                nc.scalar.activation(ohi[:, h], oraw[:, h], ACT.Copy).then_inc(o_hi, 1)
                if h == 1:
                    hi_unit(act, U_O, 0, 1)
            hi_unit(act, U_O, 0, 2)
            hi_unit(act, U_O, 0, 3)
            act.wait_ge(mean_mm, 1)
            nc.scalar.activation(mu[:, :], psum[:, 2, 0:TQ], ACT.Copy, scale=1.0 / D).then_inc(mu_ready, 1)

            def ln_squares(js):
                for j in js:
                    act.wait_ge(centred, j + 1)
                    wait(act, ln_sqsum, j - 1)
                    nc.scalar.activation(lnsq[:, j % 2], cs[:, j, 0:TQ], ACT.Square).then_inc(ln_sq, 1)
            hi_unit(act, U_O, 0, 4)
            ln_squares(range(0, 3))
            hi_unit(act, U_O, 1, 1)
            ln_squares(range(3, 6))
            hi_unit(act, U_O, 1, 2)
            ln_squares(range(6, 8))
            hi_unit(act, U_O, 1, 3)
            act.wait_ge(var_mm, 1)
            nc.scalar.activation(lnacc[:, :], psum[:, 3, 0:TQ], ACT.Sqrt, bias=eps[:, 0:1],
                                 scale=1.0 / D).then_inc(ln_root, 1)
            hi_unit(act, U_O, 1, 4)
            for k in range(KD):
                act.wait_ge(ln_scaled, k + 1)
                nc.scalar.activation(cs[:, k, 0:TQ], cs[:, k, 0:TQ], ACT.Silu,
                                     bias=vcol("conv_ln_b", k)).then_inc(c_silu, 1)
                act.wait_ge(c_silu, k + 1)
                nc.scalar.activation(chi[:, k], cs[:, k, 0:TQ], ACT.Copy).then_inc(c_hi, 1)
                if k == 3:
                    hi_unit(act, U_CO, 0, 1)

            for m in range(KD):
                if m > 0:
                    hi_unit(act, U_CO, m // 4, m % 4 + 1)
                act.wait_ge(merged, KD + m + 1)
                nc.scalar.activation(zhi[:, m], zacc[:, m], ACT.Copy).then_inc(z_hi, 1)
            for n in range(8):
                hi_unit(act, U_OUT, n // 4, n % 4 + 1)

            for i in range(NT):
                act.wait_ge(h_ready, NT + i + 1)
                wait(act, h_sq, i)
                nc.scalar.activation(junk1[:, :], h1[:, i], ACT.Square, accum_out=sumsq[:, i:i + 1]).then_inc(h_sq, 1)
            act.wait_ge(h_sq, NT)
            nc.scalar.activation(root[:, 0:NT], sumsq[:, 0:NT], ACT.Sqrt, bias=eps[:, 0:1], scale=1.0 / D).then_inc(h_root, 1)
            for k in range(KD):
                act.wait_ge(u2t_ready, k + 1)
                nc.scalar.activation(u2hi[:, k], psum[:, k % 4, 0:TQ], ACT.Copy, scale=vcol("norm_mlp", k)).then_inc(u2hi_ready, 1)

            def in_step(i):
                for c in range(4):
                    hi_unit(act, U_IN, i, c + 1)
                    act.wait_ge(unit_used, i * 4 + (U_IN + c + 1))
                    nc.scalar.activation(hid[:, ds(i * 4 + c, 1), :], psum[:, c % 2, 0:TQ].rearrange("p (a n) -> p a n", a=1),
                                         ACT.Relu).then_inc(relu_ready, 1)
            rolled(act, KF // 4, in_step, peel=0)

            def hid_hi(i, c, half):
                n = i * 4 + (U_FF + 16 * half + c)
                act.wait_ge(unit_used, n - 1)
                nc.scalar.activation(hidhi[:, c % 2], hid[:, ds(i * 8 + 2 * c, 2), :], ACT.Copy).then_inc(hidhi_ready, 1)
            act.wait_ge(hid_ready, KF)
            hid_hi(0, 0, 0)

            def ff_step(half, last):
                def body(i):
                    for c in range(4):
                        end = isinstance(i, int) and i == 3 and c == 3
                        if end and half == 1:
                            continue
                        hi_unit(act, U_FF + 16 * half, i, c + 1)
                        if end:
                            hid_hi(0, 0, 1)
                        elif c < 3:
                            hid_hi(i, c + 1, half)
                        else:
                            hid_hi(i + 1, 0, half)
                return body
            rolled(act, 4, ff_step(0, False), peel=0, last=1)
            rolled(act, 4, ff_step(1, True), peel=0, last=1)

            for i in range(NT):
                act.wait_ge(y_ready, NT + i + 1)
                wait(act, y_sq, i)
                nc.scalar.activation(junk2[:, :], h1[:, i], ACT.Square, accum_out=sumsq[:, i:i + 1]).then_inc(y_sq, 1)
                act.wait_ge(y_sq, i + 1)
                nc.scalar.activation(root[:, i:i + 1], sumsq[:, i:i + 1], ACT.Sqrt, bias=eps[:, 0:1], scale=1.0 / D).then_inc(y_root, 1)

        @block.vector
        def _(dve):
            dve.wait_ge(x_root, 1)
            nc.vector.reciprocal(rstd[:, 0:7], root[:, 0:7]).then_inc(x_rstd, 1)
            dve.wait_ge(x_rstd, 1)
            for i in range(7):
                r = T_META if i == 6 else P
                nc.vector.tensor_scalar(xt[0:r, i], xt[0:r, i], rstd[0:r, i:i + 1], None, ALU.mult).then_inc(x_scaled, 1)
            dve.wait_ge(vec_t, 1)
            nc.vector.tensor_copy(vec[:, :], psum[:, 0, 0:NVEC]).then_inc(vec_ready, 1)
            dve.wait_ge(vec_t, 2)
            nc.vector.tensor_copy(convw[:, :, :], psum[:, 1, 0:KD * 32].rearrange("p (k n) -> p k n", k=KD)[:, :, 0:TAPS]).then_inc(vec_ready, 1)
            dve.wait_ge(vec_ready, 2)
            for k in range(KD):
                dve.wait_ge(uhi_ready, k + 1)
                nc.vector.scalar_tensor_tensor(out=ulo[:, k], in0=psum[:, k % 4, 0:TK], scalar=vcol("norm_mix", k),
                                               in1=uhi[:, k].bitcast(F32), op0=ALU.mult, op1=ALU.subtract).then_inc(ulo_ready, 1)

            for n in range(6):
                dve.wait_ge(unit_used, n + 1)
                dst, w = (qraw[:, n], TQ) if n < 4 else (kvraw[:, n - 4], TK)
                nc.vector.tensor_copy(dst, psum[:, n % 2, 0:w]).then_inc(raw_q, 1)
            dve.wait_ge(tables_landed, 32)
            dve.wait_ge(kr_sw, 1)
            nc.vector.tensor_tensor(out=krt[:, :], in0=psum[:, 2, 0:TK], in1=rcos[:, :], op=ALU.mult).then_inc(kr_cos, 1)
            dve.wait_ge(kr_cos, 1)
            dve.wait_ge(kr_sin, 1)
            nc.vector.tensor_tensor(out=krt[:, :], in0=krt[:, :], in1=krsw[:, :], op=ALU.add).then_inc(kr_rot, 1)

            def kr_los():
                dve.wait_ge(kr_hi, 1)
                dve.wait_ge(kr_rot, 1)
                nc.vector.tensor_tensor(out=kra[64:128, :], in0=krt[64:128, :], in1=krb[64:128, :].bitcast(F32), op=ALU.subtract)
                nc.vector.tensor_tensor(out=krb[0:64, :], in0=krt[0:64, :], in1=kra[0:64, :].bitcast(F32), op=ALU.subtract).then_inc(kr_lo, 1)

            def recip_q():
                dve.wait_ge(ss_root, 1)
                nc.vector.reciprocal(sqacc[:, 0, 0:TQ], sqacc[:, 0, 0:TQ]).then_inc(ss_rstd, 1)

            def recip_kv():
                dve.wait_ge(ss_root, 2)
                nc.vector.reciprocal(sqacc[:, 1, :], sqacc[:, 1, :]).then_inc(ss_rstd, 1)

            def latent_scale(j):
                dve.wait_ge(ss_rstd, 1 if j < 4 else 2)
                src, g, r = ((qraw[:, j], vcol("norm_q", j), sqacc[:, 0, 0:TQ]) if j < 4 else
                             (kvraw[:, j - 4], vcol("norm_kv", j - 4), sqacc[:, 1, :]))
                nc.vector.scalar_tensor_tensor(out=src, in0=src, scalar=g, in1=r, op0=ALU.mult, op1=ALU.mult).then_inc(qkv_scaled, 1)

            def latent_lo(j):
                dve.wait_ge(qkv_hi, j + 1)
                dst, src, h = ((qlo[:, j], qraw[:, j], qhi[:, j]) if j < 4 else
                               (kvlo[:, j - 4], kvraw[:, j - 4], kvhi[:, j - 4]))
                nc.vector.tensor_tensor(out=dst, in0=src, in1=h.bitcast(F32), op=ALU.subtract).then_inc(qkv_lo, 1)

            def tap(tile, k, before, r=None):
                half = (k if isinstance(k, int) else r) % 2
                a = acc[:, half, 0:SPAN]
                j = tile if isinstance(tile, int) else None
                def pick(x, lo_, n_):
                    return x[:, ds(tile, 1), lo_:lo_ + n_] if j is None else x[:, j:j + 1, lo_:lo_ + n_]
                if isinstance(k, int):
                    src = pick(cs, 1 + k, SPAN).rearrange("p a n -> p (a n)")
                    w = pick(convw, k, 1).rearrange("p a n -> p (a n)")
                else:
                    src = cs[:, j, ds(k + 1, SPAN)]
                    w = convw[:, j, ds(k, 1)]
                if isinstance(k, int) and k == 0:
                    b = vcol("conv_b", tile)
                    ins = nc.vector.tensor_scalar(a, src, w, b, ALU.mult, ALU.add)
                elif isinstance(k, int) and k == 1:
                    ins = nc.vector.tensor_scalar(a, src, w, None, ALU.mult)
                else:
                    dve.wait_ge(tap_done, before - 1)
                    ins = nc.vector.scalar_tensor_tensor(out=a, in0=src, scalar=w, in1=a, op0=ALU.mult, op1=ALU.add)
                ins.then_inc(tap_done, 1)

            def combine(tile, done):
                dve.wait_ge(tap_done, done)
                def out(lo_, n_):
                    return (cs[:, ds(tile, 1), lo_:lo_ + n_].rearrange("p a n -> p (a n)") if not isinstance(tile, int)
                            else cs[:, tile, lo_:lo_ + n_])
                nc.vector.tensor_tensor(out=out(0, T_PROMPT), in0=acc[:, 0, 0:T_PROMPT], in1=acc[:, 1, 0:T_PROMPT], op=ALU.add)
                nc.vector.tensor_tensor(out=out(T_PROMPT, T_SAMPLE), in0=acc[:, 0, ACC_SAMPLE:ACC_SAMPLE + T_SAMPLE],
                                        in1=acc[:, 1, ACC_SAMPLE:ACC_SAMPLE + T_SAMPLE], op=ALU.add).then_inc(conv_done, 1)

            def conv_part(tile, c):
                if c == 0:
                    wait(dve, conv_done, tile)
                for k in range(8 * c, min(8 * c + 8, TAPS)):
                    tap(tile, k, tile * TAPS + k)
                if c == 3:
                    combine(tile, tile * TAPS + TAPS)

            def glu(i, c):
                j = i * 2 + c // 2
                dve.wait_ge(sg_ready, i * 2 + (c // 2 + 1))
                dve.wait_ge(unit_used, i * 4 + (U_CONV + c + 1))
                def dst(lo_, n_):
                    return cs[:, ds(j, 1), lo_:lo_ + n_].rearrange("p a n -> p (a n)") if not isinstance(j, int) else cs[:, j, lo_:lo_ + n_]
                s = sg[:, c // 2]
                for o, c0, n in ((CS_PROMPT, 0, T_PROMPT), (CS_META2, META0, T_META + T_SAMPLE), (0, META0, T_META)):
                    ins = nc.vector.tensor_tensor(out=dst(o, n), in0=psum[:, 1, c0:c0 + n], in1=s[:, c0:c0 + n], op=ALU.mult)
                ins.then_inc(glu_ready, 1)

            dve.wait_ge(pads_zero, 2)
            extras0 = {0: [kr_los, recip_q], 1: [], 2: [lambda: latent_scale(0), lambda: latent_scale(1),
                                                       lambda: latent_scale(2), lambda: latent_scale(3), lambda: latent_lo(0)],
                       3: [lambda: latent_lo(1), lambda: latent_lo(2), lambda: latent_lo(3), recip_kv,
                           lambda: latent_scale(4), lambda: latent_scale(5)]}
            for c in range(4):
                if c % 2:
                    glu(0, c)
                for f in extras0[c]:
                    f()

            def conv_step(i):
                dve.wait_ge(glu_ready, i * 2)
                for c in range(4):
                    if c % 2:
                        glu(i, c)
                    conv_part(i - 1, c)
            conv_step(1)
            latent_lo(4)
            latent_lo(5)
            with dve.Fori(2, 4) as i:
                conv_step(i)

            dve.wait_ge(glu_ready, KD)
            with dve.Fori(3, 7) as tile:
                for c in range(4):
                    conv_part(tile, c)

            LAST = KD - 1
            dve.wait_ge(conv_done, LAST)
            tap(LAST, 0, LAST * TAPS)
            tap(LAST, 1, LAST * TAPS + 1)

            def pair_step(p):
                dve.wait_ge(v_hi, p * 3 + 1)
                nc.vector.tensor_tensor(out=vlo[:, 0:4], in0=psum[:, 2, :].rearrange("p (t n) -> p t n", t=4),
                                        in1=vhi[:, 0:4].bitcast(F32), op=ALU.subtract).then_inc(v_lo, 1)
                dve.wait_ge(v_hi, p * 3 + 3)
                nc.vector.tensor_tensor(out=vlo[:, 4:6], in0=psum[:, 3, 0:HALF].rearrange("p (t n) -> p t n", t=2),
                                        in1=vhi[:, 4:6].bitcast(F32), op=ALU.subtract).then_inc(v_lo, 1)
                nc.vector.scalar_tensor_tensor(out=vlo[:, 6:8].rearrange("p t n -> p (t n)"), in0=psum[:, 3, HALF:2 * HALF], scalar=tail_mask[:, 0:1],
                                               in1=vhi[:, 6:8].rearrange("p t n -> p (t n)").bitcast(F32), op0=ALU.mult, op1=ALU.subtract).then_inc(v_lo, 1)

                def taps(a, b):
                    for r in range(a, b):
                        tap(LAST, p * 6 + (2 + r), p * 6 + (LAST * TAPS + 2 + r), r)
                taps(0, 3)
                dve.wait_ge(qr_sw, p + 1)
                nc.vector.tensor_tensor(out=qt[:, 0:T_PROMPT], in0=psum[:, 2, 0:T_PROMPT], in1=rcos[:, 0:T_PROMPT], op=ALU.mult)
                nc.vector.tensor_tensor(out=qt[:, T_PROMPT:TQ], in0=psum[:, 2, T_PROMPT:TQ], in1=rcos[:, SAMP0:TK], op=ALU.mult).then_inc(qr_cos, 1)
                dve.wait_ge(qr_cos, p + 1)
                dve.wait_ge(qr_sin, p + 1)
                nc.vector.tensor_tensor(out=qt[:, :], in0=qt[:, :], in1=qsw[:, :], op=ALU.add).then_inc(qr_rot, 1)

                def proj(hh):
                    dve.wait_ge(qn_hi, p * 2 + (hh + 1))
                    nc.vector.scalar_tensor_tensor(out=qnlo[:, :], in0=psum[:, 3, 0:TQ], scalar=SCALE, in1=qnhi[:, :].bitcast(F32),
                                                   op0=ALU.mult, op1=ALU.subtract).then_inc(qn_lo, 1)
                    dve.wait_ge(kn_hi, p * 2 + (hh + 1))
                    nc.vector.tensor_tensor(out=knlo[:, :], in0=psum[:, 2, 0:TK], in1=knhi[:, :].bitcast(F32),
                                            op=ALU.subtract).then_inc(kn_lo, 1)
                proj(0)
                dve.wait_ge(qr_hi, p + 1)
                dve.wait_ge(qr_rot, p + 1)
                nc.vector.scalar_tensor_tensor(out=qrs[0][64:128, :], in0=qt[0:64, :], scalar=SCALE, in1=qrs[0][0:64, :].bitcast(F32),
                                               op0=ALU.mult, op1=ALU.subtract)
                nc.vector.scalar_tensor_tensor(out=qrs[1][0:64, :], in0=qt[64:128, :], scalar=SCALE, in1=qrs[1][64:128, :].bitcast(F32),
                                               op0=ALU.mult, op1=ALU.subtract).then_inc(qr_lo, 1)
                for hh in range(2):
                    def M(q):
                        g = p * 12 + (6 * hh + q)
                        grp, _ = qtile(q)
                        n = len(grp["pieces"])
                        dve.wait_ge(s_ready, g + 1)
                        src = psum[:, q % 2, :].rearrange("p (b n) -> p b n", b=2)[:, 0:n, 0:grp["pieces"][0][1]]
                        nc.vector.tensor_reduce(out=negmax[:, q % 4:q % 4 + 1], in_=src, axis=AX.XY, op=ALU.max,
                                                negate=True).then_inc(max_ready, 1)

                    def R(q):
                        g = p * 12 + (6 * hh + q)
                        dve.wait_ge(exp_ready, g + 1)
                        nc.vector.reciprocal(rsum[:, q % 4:q % 4 + 1], psumexp[:, q % 4:q % 4 + 1]).then_inc(rsum_ready, 1)

                    def L(q):
                        g = p * 12 + (6 * hh + q)
                        b = 3 * hh + q // 2
                        nt = len(qtile(q)[0]["tiles"])
                        sl = (slice(None), b % 2, slice(0, nt), slice((q % 2) * P, (q % 2 + 1) * P))
                        dve.wait_ge(pt_hi, g + 1)
                        nc.vector.tensor_tensor(out=ptlo[sl], in0=psum[:, 3, 0:nt * P].rearrange("p (t n) -> p t n", t=nt),
                                                in1=pthi[sl].bitcast(F32), op=ALU.subtract).then_inc(pt_lo, 1)
                    M(0), M(1), R(0), M(2), R(1), L(0), M(3), R(2), L(1), M(4), R(3), L(2), M(5), R(4), L(3), R(5)
                    if hh == 0:
                        proj(1)
                        taps(3, 6)
                    L(4), L(5)
            rolled(dve, PAIRS, pair_step, peel=1)

            for h in range(HEADS):
                dve.wait_ge(o_hi, h + 1)
                nc.vector.tensor_tensor(out=olo[:, h], in0=oraw[:, h], in1=ohi[:, h].bitcast(F32), op=ALU.subtract).then_inc(o_lo, 1)
            for k in range(26, TAPS):
                tap(LAST, k, LAST * TAPS + k)
            combine(LAST, KD * TAPS)

            def gate_attn(m):
                dve.wait_ge(unit_used, U_O + m + 1)
                dve.wait_ge(gin_landed[m % 2], 16 * (m // 2 + 1))
                nc.vector.tensor_tensor(out=zacc[:, m], in0=psum[:, m % 2, 0:TQ], in1=gin[:, m % 2], op=ALU.mult).then_inc(merged, 1)

            def centre(js):
                dve.wait_ge(mu_ready, 1)
                for j in js:
                    dve.wait_ge(conv_done, KD)
                    nc.vector.tensor_tensor(out=cs[:, j, 0:TQ], in0=cs[:, j, 0:TQ], in1=mu[:, :], op=ALU.subtract).then_inc(centred, 1)

            def ln_scale(k):
                dve.wait_ge(ln_rstd, 1)
                nc.vector.scalar_tensor_tensor(out=cs[:, k, 0:TQ], in0=cs[:, k, 0:TQ], scalar=vcol("conv_ln_g", k), in1=lnr[:, :],
                                               op0=ALU.mult, op1=ALU.mult).then_inc(ln_scaled, 1)

            def c_low(k):
                dve.wait_ge(c_hi, k + 1)
                nc.vector.tensor_tensor(out=clo[:, k], in0=cs[:, k, 0:TQ], in1=chi[:, k].bitcast(F32), op=ALU.subtract).then_inc(c_lo, 1)
            gate_attn(0), gate_attn(1)
            centre(range(0, 3))
            gate_attn(2)
            centre(range(3, 6))
            gate_attn(3)
            centre(range(6, 8))
            gate_attn(4), gate_attn(5)
            dve.wait_ge(ln_root, 1)
            dve.wait_ge(centred, KD)
            nc.vector.reciprocal(lnr[:, :], lnacc[:, :]).then_inc(ln_rstd, 1)
            gate_attn(6)
            ln_scale(0), ln_scale(1), c_low(0), ln_scale(2), c_low(1)
            gate_attn(7)
            ln_scale(3), c_low(2), ln_scale(4), c_low(3), ln_scale(5), c_low(4), ln_scale(6), c_low(5), ln_scale(7), c_low(6), c_low(7)

            for m in range(KD):
                dve.wait_ge(unit_used, U_CO + m + 1)
                dve.wait_ge(gin_landed[m % 2], 16 * ((KD + m) // 2 + 1))
                nc.vector.tensor_tensor(out=gconv[:, :], in0=psum[:, m % 2, 0:TQ], in1=gin[:, m % 2], op=ALU.mult).then_inc(gated, 1)
                dve.wait_ge(gated, m + 1)
                dve.wait_ge(merged, KD + m)
                nc.vector.tensor_tensor(out=zacc[:, m], in0=zacc[:, m], in1=gconv[:, :], op=ALU.add).then_inc(merged, 1)
                dve.wait_ge(z_hi, m + 1)
                nc.vector.tensor_tensor(out=zlo[:, m], in0=zacc[:, m], in1=zhi[:, m].bitcast(F32), op=ALU.subtract).then_inc(z_lo, 1)

            for half in range(2):
                for i in range(NT):
                    dve.wait_ge(unit_used, U_OUT + 4 * (half + 1))
                    dve.wait_ge(h_landed[0 if i < 4 else 1], 16)
                    hx = h1[:, i, half * HALF:(half + 1) * HALF]
                    nc.vector.tensor_tensor(out=hx, in0=bank[:, (6 * half + i) % 8], in1=hx, op=ALU.add).then_inc(h_ready, 1)
            dve.wait_ge(h_root, 1)
            nc.vector.reciprocal(rstd[:, 0:NT], root[:, 0:NT]).then_inc(h_rstd, 1)
            dve.wait_ge(h_rstd, 1)
            for i in range(NT):
                nc.vector.tensor_scalar(hs1[:, i], h1[:, i], rstd[:, i:i + 1], None, ALU.mult).then_inc(h_scaled, 1)
            for k in range(KD):
                dve.wait_ge(u2hi_ready, k + 1)
                nc.vector.scalar_tensor_tensor(out=u2lo[:, k], in0=psum[:, k % 4, 0:TQ], scalar=vcol("norm_mlp", k),
                                               in1=u2hi[:, k].bitcast(F32), op0=ALU.mult, op1=ALU.subtract).then_inc(u2lo_ready, 1)

            def in_step(i):
                for c in range(4):
                    dve.wait_ge(relu_ready, i * 4 + (c + 1))
                    r = hid[:, ds(i * 4 + c, 1), :]
                    nc.vector.tensor_tensor(out=r, in0=r, in1=r, op=ALU.mult).then_inc(hid_ready, 1)
            rolled(dve, KF // 4, in_step, peel=0)

            def add_ff(half):
                dve.wait_ge(unit_used, U_FF + 16 * (half + 1))
                for i in range(NT):
                    hx = h1[:, i, half * HALF:(half + 1) * HALF]
                    nc.vector.tensor_tensor(out=hx, in0=bank[:, (6 * half + i) % 8], in1=hx, op=ALU.add).then_inc(y_ready, 1)

            for half in range(2):
                def ff_step(i):
                    for c in range(4):
                        if half == 1 and c == 2 and isinstance(i, int):
                            add_ff(0)
                        dve.wait_ge(hidhi_ready, i * 4 + (16 * half + c + 1))
                        nc.vector.tensor_tensor(out=hidlo[:, c % 2], in0=hid[:, ds(i * 8 + 2 * c, 2), :],
                                                in1=hidhi[:, c % 2].bitcast(F32), op=ALU.subtract).then_inc(hidlo_ready, 1)
                rolled(dve, 4, ff_step, peel=half)
            dve.wait_ge(gfinal_landed, 16)
            add_ff(1)
            dve.wait_ge(y_ready, 2 * NT)
            for i in range(NT):
                dve.wait_ge(y_root, i + 1)
                nc.vector.reciprocal(rstd[:, i:i + 1], root[:, i:i + 1]).then_inc(y_rstd, 1)
                dve.wait_ge(y_rstd, i + 1)
                nc.vector.scalar_tensor_tensor(out=yout[:, i], in0=h1[:, i], scalar=rstd[:, i:i + 1], in1=gfinal[:, :],
                                               op0=ALU.mult, op1=ALU.mult).then_inc(y_out, 1)

        @block.gpsimd
        def _(gp):
            gp.memset(tapsrows[:, :], 0.0).then_inc(vec_clear, 1)
            gp.memset(sumsq[:, :], 1.0).then_inc(setup, 1)
            gp.memset(ident[:, :], 0.0).then_inc(setup, 1)
            gp.memset(ones[:, :], 1.0).then_inc(setup, 1)
            gp.memset(eps[:, :], EPS).then_inc(setup, 1)
            gp.memset(tail_mask[:, :], 0.0).then_inc(setup, 1)
            gp.wait_ge(setup, 5)
            gp.affine_select(out=ident[:, :], in_=ident[:, :], compare_op=ALU.not_equal, fill=1.0, base=0,
                             pattern=[[-1, P]], channel_multiplier=1).then_inc(setup, 1)
            gp.affine_select(out=tail_mask[:, :], in_=tail_mask[:, :], compare_op=ALU.is_gt, fill=1.0,
                             base=P - T_META, pattern=[[0, 1]], channel_multiplier=-1).then_inc(setup, 1)
            gp.memset(lnsum[:, :], 0.0).then_inc(lnsum_done, 1)
            lo_unit(gp, 0, 0, 0)
            gp.wait_ge(ut_ready, KD)
            gp.memset(cs[:, :, CS_GAP:CS_META2], 0.0).then_inc(pads_zero, 1)
            gp.memset(cs[:, :, CS_END:CS_END + PAD], 0.0).then_inc(pads_zero, 1)

            for n in range(8):
                lo_unit(gp, 0, 0, n + 1) if n < 3 else lo_unit(gp, 4, 0, n + 1 - 4)
                if n < 6:
                    gp.wait_ge(q_sq, n + 1)
                    w, a = (TQ, 0) if n < 4 else (TK, 1)
                    if n in (0, 4):
                        gp.tensor_scalar(sqacc[:, a, 0:w], sqt[:, n % 2, 0:w], 1.0, 1.0, ALU.mult, ALU.mult).then_inc(sq_sum, 1)
                    else:
                        gp.wait_ge(sq_sum, n)
                        gp.tensor_tensor(out=sqacc[:, a, 0:w], in0=sqacc[:, a, 0:w], in1=sqt[:, n % 2, 0:w], op=ALU.add).then_inc(sq_sum, 1)
            gp.wait_ge(kr_sw, 1)
            gp.wait_ge(tables_landed, 32)
            gp.tensor_tensor(out=krsw[:, :], in0=krsw[:, :], in1=rsin[:, :], op=ALU.mult).then_inc(kr_sin, 1)

            def conv_step(i):
                for c in range(4):
                    lo_unit(gp, U_CONV, i, c + 1)
            rolled(gp, 4, conv_step, peel=0)

            def ln_add(tile):
                gp.wait_ge(conv_done, tile + 1)
                gp.wait_ge(lnsum_done, tile + 1)
                src = cs[:, ds(tile, 1), 0:TQ].rearrange("p a n -> p (a n)") if not isinstance(tile, int) else cs[:, tile, 0:TQ]
                gp.tensor_tensor(out=lnsum[:, :], in0=lnsum[:, :], in1=src, op=ALU.add).then_inc(lnsum_done, 1)

            def gate_step(i):
                for c in range(4):
                    lo_unit(gp, U_GATE, i, c + 1)
                    if c == 1 and not (isinstance(i, int) and i == 0):
                        ln_add(i - 1)
            rolled(gp, 4, gate_step, peel=1)

            def pair_step(p):
                lo_unit(gp, U_ATT, p, 1)
                lo_unit(gp, U_ATT, p, 2)
                gp.wait_ge(qr_sw, p + 1)
                gp.tensor_tensor(out=qsw[:, 0:T_PROMPT], in0=qsw[:, 0:T_PROMPT], in1=rsin[:, 0:T_PROMPT], op=ALU.mult)
                gp.tensor_tensor(out=qsw[:, T_PROMPT:TQ], in0=qsw[:, T_PROMPT:TQ], in1=rsin[:, SAMP0:TK], op=ALU.mult).then_inc(qr_sin, 1)
                lo_unit(gp, U_ATT, p, 3)
                for hh in range(2):
                    for q in range(6):
                        g = p * 12 + (6 * hh + q)
                        n = qtile(q)[0]["nk"]
                        wait_apart(gp, rsum_ready, g + 1)
                        gp.tensor_scalar(prob[:, q % 2, 0:n], prob[:, q % 2, 0:n], rsum[:, q % 4:q % 4 + 1], 1.0,
                                         ALU.mult, ALU.mult).then_inc(p_ready, 1)
                    if hh == 0:
                        ln_add(p + 3)
                lo_unit(gp, U_ATT, p, 4)
            rolled(gp, PAIRS, pair_step, peel=1)

            for c in range(3):
                lo_unit(gp, U_O, 0, c + 1)
                if c == 0:
                    ln_add(KD - 1)

            def ln_sq_add(js):
                for j in js:
                    gp.wait_ge(ln_sq, j + 1)
                    if j == 0:
                        gp.tensor_scalar(lnacc[:, :], lnsq[:, 0], 1.0, 1.0, ALU.mult, ALU.mult).then_inc(ln_sqsum, 1)
                    else:
                        gp.wait_ge(ln_sqsum, j)
                        gp.tensor_tensor(out=lnacc[:, :], in0=lnacc[:, :], in1=lnsq[:, j % 2], op=ALU.add).then_inc(ln_sqsum, 1)
            lo_unit(gp, U_O, 0, 4)
            ln_sq_add(range(0, 3))
            lo_unit(gp, U_O, 1, 1)
            ln_sq_add(range(3, 6))
            lo_unit(gp, U_O, 1, 2)
            ln_sq_add(range(6, 8))
            lo_unit(gp, U_O, 1, 3)
            for n in range(U_O + KD, U_IN + 1):
                lo_unit(gp, n - n % 4, 0, n % 4)

            def in_step(i):
                for c in range(4):
                    lo_unit(gp, U_IN, i, c + 1)
            rolled(gp, KF // 4, in_step, peel=0)
            with gp.Fori(0, 7) as i:
                for c in range(4):
                    lo_unit(gp, U_FF, i, c + 1)
            for c in range(3):
                lo_unit(gp, U_FF, 7, c + 1)

        @block.tensor
        def _(pe):
            pe.wait_ge(setup, 7)
            pe.wait_ge(consts_landed, 16 * len(VEC))
            nc.tensor.transpose(psum[:, 0, 0:NVEC], vecrows[0:NVEC, :], ident[0:NVEC, 0:NVEC]).then_inc(vec_t, 1)
            pe.wait_ge(taps_landed, 16)
            for k in range(KD):
                mm = nc.tensor.transpose(psum[:, 1, k * 32:(k + 1) * 32], tapsrows[:, k * P:(k + 1) * P], ident[0:32, 0:32])
            mm.then_inc(vec_t, 1)
            pe.wait_ge(vec_ready, 2)

            pe.wait_ge(x_scaled, 7)
            COLS = [0, 128, 256, 384, SAMP0, SAMP0 + 128, META0]
            for k in range(KD):
                wait(pe, ulo_ready, k - 3)
                for i in range(7):
                    r = T_META if i == 6 else P
                    mm = nc.tensor.transpose(psum[:, k % 4, COLS[i]:COLS[i] + r], xt[0:r, i, k * P:(k + 1) * P], ident[0:r, 0:r])
                mm.then_inc(ut_ready, 1)

            u = (uhi, ulo)

            def unit(base, i, c, pair, rhs, segments, k_tiles=range(KD), first=True, last=True, rhs_ready=None):
                pe.wait_ge(lo_ready, i * 4 + (base + c + 1))
                wh, wl = weights(c % 2, len(k_tiles))
                for j, k in enumerate(k_tiles):
                    if rhs_ready is not None:
                        rhs_ready(k)
                    mm = products(psum[:, pair], (wh[:, j], wl[:, j]), rhs, k, segments,
                                  first and j == 0, last and j == len(k_tiles) - 1)
                mm.then_inc(unit_used, 1)

            for n in range(6):
                wait(pe, raw_q, n - 1)
                unit(4 * (n // 4), 0, n % 4, n % 2, u, QSEG if n < 4 else KSEG,
                     rhs_ready=(lambda k: pe.wait_ge(ulo_ready, max(k + 1, 5))) if n == 0 else
                     ((lambda k: pe.wait_ge(ulo_ready, KD)) if n == 1 else None))
            for e in range(2):
                unit(4, 0, 2 + e, 2, u, KSEG, k_tiles=range(4 * e, 4 * e + 4), first=e == 0, last=e == 1)
                if e == 0:
                    sum_squares(pe, 0, TQ, 4)
            pe.wait_ge(raw_q, 6)

            def conv_step(i):
                for c in range(4):
                    if c % 2 == 0:
                        wait(pe, sg_ready, i * 2 + c // 2)
                    else:
                        wait(pe, glu_ready, i * 2 + c // 2)
                    unit(U_CONV, i, c, c % 2, u, KSEG)
                    if isinstance(i, int) and i == 0 and c == 0:
                        pe.wait_ge(ss_root, 1)
                        sum_squares(pe, 1, TK, 6)
            rolled(pe, 4, conv_step, peel=1)

            def gate_step(i):
                for c in range(4):
                    if isinstance(i, int) and i == 0 and c < 2:
                        pe.wait_ge(sg_ready if c == 0 else glu_ready, KD)
                    wait(pe, gate_ready, i * 4 + (c - 1))
                    unit(U_GATE, i, c, c % 2, u, QSEG)
            rolled(pe, 4, gate_step, peel=1)

            pe.wait_ge(gate_ready, 2 * KD)
            pe.wait_ge(qkv_lo, KQ + KKV)
            pe.wait_ge(kr_lo, 1)
            pe.wait_ge(kr_rot, 1)

            def pair_step(p):
                pe.wait_ge(lo_ready, p * 4 + (U_ATT + 1))
                wh, wl = weights(0, KKV, 2 * VD)
                for j, c0 in enumerate(VTILES):
                    out = psum[:, 2 + j // 4, (j % 4) * 2 * VD:(j % 4 + 1) * 2 * VD]
                    if j == 0:
                        wait(pe, o_ready, p * 6)
                    if j == 4:
                        wait(pe, pt_lo, p * 12)
                    for k in range(KKV):
                        for step, (a, b) in enumerate(((kvhi, wh), (kvlo, wh), (kvhi, wl))):
                            mm = nc.tensor.matmul(out, a[:, k, c0:c0 + P], b[:, k, :],
                                                  start=k == 0 and step == 0, stop=k == KKV - 1 and step == 2)
                    if j == 3:
                        mm.then_inc(v_mm, 1)
                mm.then_inc(unit_used, 1)
                pe.wait_ge(v_lo, p * 3 + 1)
                unit_q(p, 1, 2, range(KQ), (qhi, qlo), ZSEG)

                def proj(hh):
                    pe.wait_ge(lo_ready, p * 4 + (U_ATT + 3 + hh))
                    wh, wl = weights(hh, KQ + KKV)
                    if hh == 0:
                        pe.wait_ge(v_lo, p * 3 + 3)
                    else:
                        pe.wait_ge(pt_lo, p * 12 + 4)
                    for k in range(KQ):
                        mm = products(psum[:, 3], (wh[:, k], wl[:, k]), (qhi, qlo), k, ZSEG, k == 0, k == KQ - 1)
                    mm.then_inc(qn_mm, 1)
                    if hh == 0:
                        pe.wait_ge(qr_cos, p + 1)
                    else:
                        pe.wait_ge(o_ready, p * 6 + 2)
                    for k in range(KKV):
                        mm = products(psum[:, 2], (wh[:, KQ + k], wl[:, KQ + k]), (kvhi, kvlo), k, KSEG, k == 0, k == KKV - 1)
                    mm.then_inc(unit_used, 1)
                proj(0)
                pe.wait_ge(qr_lo, p + 1)
                for hh in range(2):
                    pe.wait_ge(qn_lo, p * 2 + (hh + 1))
                    pe.wait_ge(kn_lo, p * 2 + (hh + 1))

                    def S(q):
                        g = p * 12 + (6 * hh + q)
                        grp, c0 = qtile(q)
                        wait(pe, exp_ready, g - 1)
                        ops = [(qnhi, knhi), (qnhi, knlo), (qnlo, knhi), (qrs[hh], kra), (qrs[hh], krb)]
                        for step, (a, b) in enumerate(ops):
                            for e, (k0, n) in enumerate(grp["pieces"]):
                                mm = nc.tensor.matmul(psum[:, q % 2, e * HALF:e * HALF + n], a[:, c0:c0 + P],
                                                      b[:, grp["k0"] + k0:grp["k0"] + k0 + n],
                                                      start=step == 0, stop=step == len(ops) - 1)
                        mm.then_inc(s_ready, 1)

                    def T(q):
                        g = p * 12 + (6 * hh + q)
                        pe.wait_ge(p_ready, g + 1)
                        wait(pe, pt_lo, g)
                        for e, (_, k0) in enumerate(qtile(q)[0]["tiles"]):
                            mm = nc.tensor.transpose(psum[:, 3, e * P:(e + 1) * P], prob[:, q % 2, k0:k0 + P], ident[:, :])
                        mm.then_inc(pt_mm, 1)

                    def A(b):
                        blk = 3 * hh + b
                        pe.wait_ge(pt_lo, p * 12 + (6 * hh + 2 * b + 2))
                        wait(pe, o_ready, p * 6 + blk)
                        tiles = qtile(2 * b)[0]["tiles"]
                        for e, (vt, _) in enumerate(tiles):
                            for step, (a, r) in enumerate(((vhi, pthi), (vhi, ptlo), (vlo, pthi))):
                                mm = nc.tensor.matmul(psum[:, 2, 0:2 * P], a[:, vt, hh * VD:(hh + 1) * VD], r[:, blk % 2, e, :],
                                                      start=e == 0 and step == 0, stop=e == len(tiles) - 1 and step == 2)
                        mm.then_inc(av_mm, 1)
                    S(0), S(1), S(2), T(0), S(3), T(1), A(0), S(4), T(2), S(5), T(3), A(1)
                    if hh == 0:
                        proj(1)
                        pe.wait_ge(qn_lo, p * 2 + 2)
                        pe.wait_ge(kn_lo, p * 2 + 2)
                    T(4), T(5), A(2)

            def unit_q(p, c, pair, k_tiles, rhs, segments):
                unit(U_ATT, p, c, pair, rhs, segments, k_tiles=k_tiles)
            rolled(pe, PAIRS, pair_step, peel=1)

            pe.wait_ge(o_ready, 3 * HEADS)
            o = (ohi, olo)
            for m in range(KD):
                wait(pe, merged, m - 1)
                unit(U_O, m // 4, m % 4, m % 2, o, ZSEG,
                     rhs_ready=(lambda k: pe.wait_ge(o_lo, k + 1)) if m == 0 else None)
                if m == 1:
                    pe.wait_ge(lnsum_done, KD + 1)
                    for c0, n in ((0, HALF), (HALF, TQ - HALF)):
                        mm = nc.tensor.matmul(psum[:, 2, c0:c0 + n], ones[:, :], lnsum[:, c0:c0 + n], start=True, stop=True)
                    mm.then_inc(mean_mm, 1)
                if m == 5:
                    pe.wait_ge(ln_sqsum, KD)
                    for c0, n in ((0, HALF), (HALF, TQ - HALF)):
                        mm = nc.tensor.matmul(psum[:, 3, c0:c0 + n], ones[:, :], lnacc[:, c0:c0 + n], start=True, stop=True)
                    mm.then_inc(var_mm, 1)
            for m in range(KD):
                pe.wait_ge(merged, KD + m - 1)
                unit(U_CO, m // 4, m % 4, m % 2, (chi, clo), ZSEG,
                     rhs_ready=(lambda k: pe.wait_ge(c_lo, k + 1)) if m == 0 else None)

            def token_major(base, half, i, units, n_k, lhs, lhs_ready, free):
                for c in range(4):
                    pe.wait_ge(lo_ready, i * 4 + (base + c + 1))
                    wh, wl = weights(c % 2, 2, HALF)
                    lhs_ready(i, c)
                    for kk in range(2):
                        for tt in range(NT):
                            first = isinstance(i, int) and i == 0 and c == 0 and kk == 0
                            last = isinstance(i, int) and i == units // 4 - 1 and c == 3 and kk == 1
                            if first:
                                free(tt)
                            out = bank[:, (6 * half + tt) % 8]
                            a_hi, a_lo = lhs(i, c, kk, tt)
                            for step, (a, b) in enumerate(((a_hi, wh), (a_hi, wl), (a_lo, wh))):
                                mm = nc.tensor.matmul(out, a, b[:, kk, :], start=first and step == 0, stop=last and step == 2)
                    mm.then_inc(unit_used, 1)

            pe.wait_ge(merged, 2 * KD)
            for half in range(2):
                token_major(U_OUT + 4 * half, half, 0, 4, KD,
                            lambda i, c, kk, tt: (zhi[:, 2 * c + kk, tt * P:(tt + 1) * P], zlo[:, 2 * c + kk, tt * P:(tt + 1) * P]),
                            (lambda i, c: pe.wait_ge(z_lo, 2 * c + 2)) if half == 0 else (lambda i, c: None),
                            (lambda tt: None) if half == 0 else (lambda tt: wait(pe, h_ready, tt - 1)))

            pe.wait_ge(h_ready, 2 * NT)
            pe.wait_ge(h_scaled, NT)
            for k in range(KD):
                wait(pe, u2lo_ready, k - 3)
                for i in range(NT):
                    mm = nc.tensor.transpose(psum[:, k % 4, i * P:(i + 1) * P], hs1[:, i, k * P:(k + 1) * P], ident[:, :])
                mm.then_inc(u2t_ready, 1)

            def in_step(i):
                for c in range(4):
                    if isinstance(i, int) and i == 0:
                        pe.wait_ge(u2lo_ready, KD)
                    wait(pe, relu_ready, i * 4 + (c - 1))
                    unit(U_IN, i, c, c % 2, (u2hi, u2lo), ZSEG)
            rolled(pe, KF // 4, in_step, peel=1)

            pe.wait_ge(relu_ready, KF)
            for half in range(2):
                rolled(pe, 4, lambda i: token_major(
                    U_FF + 16 * half, half, i, 16, KF,
                    lambda i, c, kk, tt: (hidhi[:, c % 2, kk, tt * P:(tt + 1) * P], hidlo[:, c % 2, kk, tt * P:(tt + 1) * P]),
                    lambda i, c: pe.wait_ge(hidlo_ready, i * 4 + (16 * half + c + 1)),
                    (lambda tt: None) if half == 0 else (lambda tt: wait(pe, y_ready, tt - 1))), peel=1, last=1)


_INS = ["x_prompt", "x_sample", "meta_tokens", "norm_mix", "w_in", "b_gate", "norm_q", "w_uq", "norm_kv", "w_ukv",
        "w_o_attn", "conv_w", "conv_b", "conv_ln_g", "conv_ln_b", "w_conv_out", "w_out", "norm_mlp", "w_mlp_in",
        "w_mlp_out", "norm_final"]
_OUTS = [("y_prompt", (1, T_PROMPT, D)), ("y_sample", (1, T_SAMPLE, D))]


def rope_tables():
    pos = np.concatenate([T_META + np.arange(T_PROMPT), np.arange(T_META), T_META + np.arange(T_SAMPLE)]).astype(np.float32)
    inv = np.float32(10000.0) ** (-np.arange(0, ROPE, 2, dtype=np.float32) / np.float32(ROPE))
    ang = (inv[:, None] * pos[None, :]).astype(np.float32)
    c, s = np.cos(ang), np.sin(ang)
    return (np.ascontiguousarray(np.concatenate([c, c, c, c]), np.float32),
            np.ascontiguousarray(np.concatenate([-s, s, -s, s]), np.float32))


def kernel(**inputs):
    import concourse.bacc as _bacc
    from concourse.bass_utils import run_bass_kernel_spmd as _run

    nc = _bacc.Bacc("TRN2", target_bir_lowering=False, num_devices=1)
    arrays, t = {}, {}
    for name in _INS:
        a = np.ascontiguousarray(inputs[name])
        arrays[f"in_{name}"] = a
        t[name] = nc.dram_tensor(f"in_{name}", a.shape, F32, kind="ExternalInput").ap()
    for name, a in zip(("rope_cos", "rope_sin"), rope_tables()):
        arrays[name] = a
        t[name] = nc.dram_tensor(name, a.shape, F32, kind="ExternalInput").ap()
    for name, shape in _OUTS:
        t[name] = nc.dram_tensor(f"out_{name}", shape, F32, kind="ExternalOutput").ap()
    build(nc, t)
    r = _run(nc, [arrays], core_ids=[0])
    return tuple(r.results[0][f"out_{name}"] for name, _ in _OUTS)
```

```python
from contextlib import ExitStack

import numpy as np
import concourse.bass as bass
from concourse import mybir

F32 = mybir.dt.float32
F32R = mybir.dt.float32r
ALU = mybir.AluOpType
ACT = mybir.ActivationFunctionType
AX = mybir.AxisListType
ds = bass.ds

P = 128
D = 1024
KD = D // P
T_PROMPT, T_SAMPLE, T_META = 512, 256, 16
META0 = T_PROMPT
SAMP0 = T_PROMPT + T_META
TK = T_PROMPT + T_META + T_SAMPLE
TQ = T_PROMPT + T_SAMPLE
NT = TQ // P
HEADS, NOPE, ROPE, VD = 8, 128, 64, 128
PAIRS = HEADS // 2
Q_LORA, KV_LORA = 512, 256
KQ, KKV = Q_LORA // P, KV_LORA // P
TAPS, PAD = 31, 15
FF = 4 * D
KF = FF // P
EPS = 1e-6
SCALE = float((NOPE + ROPE) ** -0.5)
HALF = 512

C_Q, C_KV = 0, Q_LORA
C_KR = C_KV + KV_LORA
C_A = C_KR + ROPE
C_B = C_A + D
C_GATE = C_B + D

U_QKV = 0
U_CONV = 8
U_GATE = U_CONV + 2 * KD
U_ATT = U_GATE + 2 * KD
U_O = U_ATT + 4 * PAIRS
U_CO = U_O + KD
U_OUT = U_CO + KD
U_IN = U_OUT + KD
U_FF = U_IN + KF
U_END = U_FF + KF

VEC = {}
for _name, _rows in (("norm_mix", KD), ("norm_q", KQ), ("norm_kv", KKV), ("b_gate", 2 * KD),
                     ("conv_b", KD), ("conv_ln_g", KD), ("conv_ln_b", KD), ("norm_mlp", KD)):
    VEC[_name] = (sum(r for _, r in VEC.values()), _rows)
NVEC = sum(r for _, r in VEC.values())

CS_PROMPT = T_META
CS_GAP = CS_PROMPT + T_PROMPT
CS_META2 = CS_GAP + PAD
CS_SAMPLE = CS_META2 + T_META
CS_END = CS_SAMPLE + T_SAMPLE
CS_ALL = 832
SPAN = CS_END - CS_PROMPT
ACC_SAMPLE = CS_SAMPLE - CS_PROMPT

VTILES = [0, 128, 256, 384, META0, META0 + 128, SAMP0 - 128, TK - 128]
GROUPS = [
    dict(k0=0, nk=SAMP0, pieces=((0, SAMP0 // 2), (SAMP0 // 2, SAMP0 // 2)),
         tiles=((0, 0), (1, 128), (2, 256), (3, 384), (6, SAMP0 - 128))),
    dict(k0=META0, nk=TK - META0, pieces=((0, TK - META0),),
         tiles=((4, 0), (5, 128), (7, TK - META0 - 128))),
]

W_QR, W_QK, W_V = KQ * P, (KQ + KKV) * P, KKV * 2 * VD
PAIR_W = (W_QR, W_QK, W_V, W_QK)
TAIL = 4

SB0 = 16512
Z0 = SB0 + 36352


def build(nc, t):
    with ExitStack() as ctx:
        def at(name, shape, dt, offset):
            return nc.alloc_sbuf_tensor_at(name, shape, dt, offset=offset)

        def sem(name):
            return ctx.enter_context(nc.semaphore(name))

        psum = ctx.enter_context(nc.psum_tensor("psum", [P, 4, 2 * HALF], F32))
        bank = psum[:].rearrange("p a (b n) -> p (a b) n", n=HALF)

        ident = at("ident", [P, P], F32, SB0)
        ones = at("ones", [P, P], F32, SB0 + 512)
        vec = at("vec", [P, NVEC], F32, SB0 + 1024)
        convw = at("convw", [P, KD, TAPS], F32, SB0 + 1280)
        eps = at("eps", [P, 1], F32, SB0 + 2272)
        tail_mask = at("tail_mask", [P, 1], F32, SB0 + 2304)
        sumsq = at("sumsq", [P, 8], F32, SB0 + 2336)
        root = at("root", [P, 8], F32, SB0 + 2368)
        rstd = at("rstd", [P, 8], F32, SB0 + 2400)
        negmax = at("negmax", [P, 4], F32, SB0 + 2432)
        psumexp = at("psumexp", [P, 4], F32, SB0 + 2464)
        rsum = at("rsum", [P, 4], F32, SB0 + 2496)
        raw = at("raw", [P, 4, D], F32, SB0 + 3584)
        whi = at("whi", [P, 2, D], F32R, SB0 + 3584 + 16384)
        wlo = at("wlo", [P, 2, D], F32R, SB0 + 3584 + 24576)

        cs = at("cs", [P, KD, CS_ALL], F32, Z0)
        acc = at("acc", [P, 2, 800], F32, Z0 + 26624)
        lnsum = at("lnsum", [P, TQ], F32, Z0 + 33024)
        qhi = at("qhi", [P, KQ, TQ], F32R, Z0 + 36096)
        qlo = at("qlo", [P, KQ, TQ], F32R, Z0 + 48384)
        kvhi = at("kvhi", [P, KKV, TK], F32R, Z0 + 60672)
        kvlo = at("kvlo", [P, KKV, TK], F32R, Z0 + 66944)
        kra = at("kra", [P, TK], F32R, Z0 + 73216)
        krb = at("krb", [P, TK], F32R, Z0 + 76352)
        rcos = at("rcos", [P, TK], F32, Z0 + 79488)
        rsin = at("rsin", [P, TK], F32, Z0 + 82624)
        V0 = Z0 + 85760
        xt = at("xt", [P, 7, D], F32, Z0)
        vecrows = at("vecrows", [P, P], F32, V0 + 50176)
        tapsrows = at("tapsrows", [32, D], F32, V0 + 50176 + 512)
        junk0 = at("junk0", [P, D], F32, V0 + 50176 + 4608)
        uhi = at("uhi", [P, KD, TK], F32R, V0)
        ulo = at("ulo", [P, KD, TK], F32R, V0 + 25088)
        qraw = at("qraw", [P, KQ, TQ], F32, V0 + 50176)
        kvraw = at("kvraw", [P, KKV, TK], F32, V0 + 62464)
        sqacc = at("sqacc", [P, 2, TK], F32, V0 + 68736)
        sqt = at("sqt", [P, 2, TK], F32, V0 + 75008)
        krsw = at("krsw", [P, TK], F32, V0 + 81280)
        krt = at("krt", [P, TK], F32, V0 + 84416)
        sg = at("sg", [P, 2, TK], F32, V0 + 75008)
        gout = at("gout", [P, 2, TQ], F32, V0 + 62464)
        qnhi = at("qnhi", [P, TQ], F32R, V0)
        qnlo = at("qnlo", [P, TQ], F32R, V0 + 3072)
        knhi = at("knhi", [P, TK], F32R, V0 + 6144)
        knlo = at("knlo", [P, TK], F32R, V0 + 9280)
        qrs = [at(f"qrs{e}", [P, TQ], F32R, V0 + 12416 + 3072 * e) for e in range(2)]
        qsw = at("qsw", [P, TQ], F32, V0 + 18560)
        qt = at("qt", [P, TQ], F32, V0 + 21632)
        vhi = at("vhi", [P, 8, 2 * VD], F32R, V0 + 24704)
        vlo = at("vlo", [P, 8, 2 * VD], F32R, V0 + 32896)
        prob = at("prob", [P, 2, SAMP0], F32, V0 + 41088)
        pthi = at("pthi", [P, 2, 5, 2 * P], F32R, V0 + 45312)
        ptlo = at("ptlo", [P, 2, 5, 2 * P], F32R, V0 + 55552)
        oraw = at("oraw", [P, HEADS, TQ], F32, V0 + 65792)
        ohi = at("ohi", [P, KD, TQ], F32R, Z0 + 36096)
        olo = at("olo", [P, KD, TQ], F32R, Z0 + 60672)
        gin = at("gin", [P, 2, TQ], F32, Z0 + 26624)
        zacc = at("zacc", [P, KD, TQ], F32, Z0 + 85760)
        chi = at("chi", [P, KD, TQ], F32R, Z0 + 110336)
        clo = at("clo", [P, KD, TQ], F32R, Z0 + 151552)
        mu = at("mu", [P, TQ], F32, Z0 + 134912)
        lnr = at("lnr", [P, TQ], F32, Z0 + 137984)
        lnsq = at("lnsq", [P, 2, TQ], F32, Z0 + 141056)
        lnacc = at("lnacc", [P, TQ], F32, Z0 + 147200)
        gconv = at("gconv", [P, TQ], F32, Z0 + 134912)
        zhi = at("zhi", [P, KD, TQ], F32R, Z0 + 36096)
        zlo = at("zlo", [P, KD, TQ], F32R, Z0 + 60672)
        h1 = at("h1", [P, NT, D], F32, Z0)
        hs1 = at("hs1", [P, NT, D], F32, Z0 + 85760)
        junk1 = at("junk1", [P, D], F32, Z0 + 110336)
        hid = at("hid", [P, KF, TQ], F32, Z0 + 24576)
        u2hi = at("u2hi", [P, KD, TQ], F32R, Z0 + 122880)
        u2lo = at("u2lo", [P, KD, TQ], F32R, Z0 + 147456)
        hidhi = at("hidhi", [P, 2, 2, TQ], F32R, Z0 + 122880)
        hidlo = at("hidlo", [P, 2, 2, TQ], F32R, Z0 + 135168)
        yout = at("yout", [P, NT, D], F32, Z0 + 147456)
        gfinal = at("gfinal", [P, D], F32, Z0 + 172032)
        junk2 = at("junk2", [P, D], F32, Z0 + 24576)

        gates = nc.dram_tensor("gates", [2 * KD, P, TQ], F32, kind="Internal").ap()

        raw_landed = [sem(f"raw_landed{s}") for s in range(4)]
        hi_ready, lo_ready, unit_used = sem("hi_ready"), sem("lo_ready"), sem("unit_used")
        dup_landed = [sem(f"dup_landed{e}") for e in range(2)]
        kw_landed = [sem(f"kw_landed{e}") for e in range(2)]
        x_landed = [sem(f"x_landed{i}") for i in range(7)]
        consts_landed, taps_landed, tables_landed = sem("consts_landed"), sem("taps_landed"), sem("tables_landed")
        setup, vec_clear, vec_t, vec_ready = sem("setup"), sem("vec_clear"), sem("vec_t"), sem("vec_ready")
        x_sq, x_root, x_rstd, x_scaled = sem("x_sq"), sem("x_root"), sem("x_rstd"), sem("x_scaled")
        ut_ready, uhi_ready, ulo_ready = sem("ut_ready"), sem("uhi_ready"), sem("ulo_ready")
        raw_q, q_sq, sq_sum = sem("raw_q"), sem("q_sq"), sem("sq_sum")
        ss_mm, ss_root, ss_rstd = sem("ss_mm"), sem("ss_root"), sem("ss_rstd")
        qkv_scaled, qkv_hi, qkv_lo = sem("qkv_scaled"), sem("qkv_hi"), sem("qkv_lo")
        kr_sw, kr_cos, kr_sin, kr_rot, kr_hi, kr_lo = (sem("kr_sw"), sem("kr_cos"), sem("kr_sin"),
                                                       sem("kr_rot"), sem("kr_hi"), sem("kr_lo"))
        pads_zero, sg_ready, glu_ready = sem("pads_zero"), sem("sg_ready"), sem("glu_ready")
        tap_done, conv_done, lnsum_done = sem("tap_done"), sem("conv_done"), sem("lnsum_done")
        gate_ready = sem("gate_ready")
        gate_stored = [sem(f"gate_stored{e}") for e in range(2)]
        v_mm, v_hi, v_lo = sem("v_mm"), sem("v_hi"), sem("v_lo")
        qr_sw, qr_cos, qr_sin, qr_rot, qr_hi, qr_lo = (sem("qr_sw"), sem("qr_cos"), sem("qr_sin"),
                                                       sem("qr_rot"), sem("qr_hi"), sem("qr_lo"))
        qn_mm, qn_hi, qn_lo, kn_hi, kn_lo = sem("qn_mm"), sem("qn_hi"), sem("qn_lo"), sem("kn_hi"), sem("kn_lo")
        s_ready, max_ready, exp_ready, rsum_ready, p_ready = (sem("s_ready"), sem("max_ready"),
                                                              sem("exp_ready"), sem("rsum_ready"), sem("p_ready"))
        tail_lo = sem("tail_lo")
        pt_mm, pt_hi, pt_lo, av_mm, o_ready = sem("pt_mm"), sem("pt_hi"), sem("pt_lo"), sem("av_mm"), sem("o_ready")
        o_hi, o_lo = sem("o_hi"), sem("o_lo")
        gin_landed = [sem(f"gin_landed{e}") for e in range(2)]
        mean_mm, mu_ready, centred, ln_sq, ln_sqsum = (sem("mean_mm"), sem("mu_ready"), sem("centred"),
                                                       sem("ln_sq"), sem("ln_sqsum"))
        var_mm, ln_root, ln_rstd, ln_scaled, c_silu, c_hi, c_lo = (
            sem("var_mm"), sem("ln_root"), sem("ln_rstd"), sem("ln_scaled"), sem("c_silu"), sem("c_hi"), sem("c_lo"))
        merged, gated, z_hi, z_lo = sem("merged"), sem("gated"), sem("z_hi"), sem("z_lo")
        h_landed, h_ready = [sem(f"h_landed{i}") for i in range(2)], sem("h_ready")
        h_sq, h_root, h_rstd, h_scaled = sem("h_sq"), sem("h_root"), sem("h_rstd"), sem("h_scaled")
        u2t_ready, u2hi_ready, u2lo_ready = sem("u2t_ready"), sem("u2hi_ready"), sem("u2lo_ready")
        relu_ready, hid_ready = sem("relu_ready"), sem("hid_ready")
        hidhi_ready, hidlo_ready = sem("hidhi_ready"), sem("hidlo_ready")
        gfinal_landed, y_ready, y_sq, y_root, y_rstd, y_out, y_stored = (
            sem("gfinal_landed"), sem("y_ready"), sem("y_sq"), sem("y_root"), sem("y_rstd"), sem("y_out"), sem("y_stored"))

        waits_apart = sem("waits_apart")

        def wait(eng, s, value):
            if not isinstance(value, int) or value > 0:
                eng.wait_ge(s, value)

        def wait_apart(eng, s, value):
            wait(eng, s, value)
            if not isinstance(value, int):
                eng.sem_inc(waits_apart, 1)

        def rolled(eng, count, body, peel=1, last=0):
            for i in range(peel):
                body(i)
            if count - peel - last > 0:
                with eng.Fori(peel, count - last) as i:
                    body(i)
            for i in range(count - last, count):
                body(i)

        def hi_unit(act, base, i, c, w=D):
            act.wait_ge(raw_landed[c % 4], (i + (base // 4 + c // 4 + 1)) * 16)
            wait(act, unit_used, i * 4 + (base + c - 1))
            nc.scalar.activation(whi[:, c % 2, 0:w], raw[:, c % 4, 0:w], ACT.Copy).then_inc(hi_ready, 1)

        def lo_unit(gp, base, i, c, w=D):
            gp.wait_ge(hi_ready, i * 4 + (base + c + 1))
            gp.tensor_tensor(out=wlo[:, c % 2, 0:w], in0=raw[:, c % 4, 0:w], in1=whi[:, c % 2, 0:w].bitcast(F32),
                             op=ALU.subtract).then_inc(lo_ready, 1)

        def weights(s, k, m=P):
            return (whi[:, s, 0:k * m].rearrange("p (k m) -> p k m", k=k),
                    wlo[:, s, 0:k * m].rearrange("p (k m) -> p k m", k=k))

        def products(out, lhs, rhs, k, segments, first, last):
            (lh, ll), (rh, rl) = lhs, rhs
            mm = None
            for step, (a, b) in enumerate(((lh, rh), (lh, rl), (ll, rh))):
                for o0, c0, n in segments:
                    mm = nc.tensor.matmul(out[:, o0:o0 + n], a, b[:, k, c0:c0 + n],
                                          start=first and step == 0, stop=last and step == 2)
            return mm

        KSEG = ((0, 0, HALF), (HALF, HALF, TK - HALF))
        QSEG = ((0, 0, T_PROMPT), (T_PROMPT, SAMP0, T_SAMPLE))
        ZSEG = ((0, 0, HALF), (HALF, HALF, TQ - HALF))

        def vcol(name, k):
            r = VEC[name][0]
            return vec[:, ds(k + r, 1)] if not isinstance(k, int) else vec[:, r + k:r + k + 1]

        def qtile(q):
            return (GROUPS[0] if q < 4 else GROUPS[1]), q * P

        def main_tiles(q):
            return 4 if q < 4 else 3

        def sum_squares(pe, a, w, count):
            pe.wait_ge(sq_sum, count)
            for c0, n in ((0, HALF), (HALF, w - HALF)):
                mm = nc.tensor.matmul(psum[:, 3, c0:c0 + n], ones[:, :], sqacc[:, a, c0:c0 + n], start=True, stop=True)
            mm.then_inc(ss_mm, 1)

        block = ctx.enter_context(nc.Block())

        @block.sync
        def _(sp):
            xs = [t["x_prompt"][0, i * P:(i + 1) * P, :] for i in range(4)]
            xs += [t["x_sample"][0, i * P:(i + 1) * P, :] for i in range(2)]
            for i in range(2):
                sp.dma_start(xt[:, i], xs[i]).then_inc(x_landed[i], 16)
            sp.dma_start(xt[0:T_META, 6], t["meta_tokens"]).then_inc(x_landed[6], 16)
            for i in range(2, 6):
                sp.dma_start(xt[:, i], xs[i]).then_inc(x_landed[i], 16)

            win = t["w_in"][0].rearrange("(k p) n -> p k n", p=P)

            def columns(w, n, base, i, c, col):
                wait_apart(sp, lo_ready, i * 4 + (base + c - 3))
                sp.dma_start(raw[:, c].rearrange("p (k m) -> p k m", k=KD), w[:, :, col]) \
                  .then_inc(raw_landed[c], 16)

            for n in range(6):
                col = n * P
                columns(win, n, 4 * (n // 4), 0, n % 4, slice(col, col + P))
            sp.dma_start(rcos[:, :], t["rope_cos"]).then_inc(tables_landed, 16)
            sp.dma_start(rsin[:, :], t["rope_sin"]).then_inc(tables_landed, 16)
            for e in range(2):
                sp.wait_ge(lo_ready, 6 + e - 3)
                r = raw[:, 2 + e, 0:4 * P].rearrange("p (k m) -> p k m", k=4)
                w = win[:, 4 * e:4 * e + 4, C_KR:C_KR + ROPE]
                sp.dma_start(r[:, :, 0:ROPE], w).then_inc(raw_landed[2 + e], 16)
                sp.dma_start(r[:, :, ROPE:P], w).then_inc(dup_landed[e], 16)

            def conv_units(i):
                for c in range(4):
                    first = C_B if c % 2 == 0 else C_A
                    columns(win, None, U_CONV, i, c, ds(i * (2 * P) + (first + (c // 2) * P), P))
            rolled(sp, 4, conv_units, peel=0)

            def gate_units(i):
                for c in range(4):
                    columns(win, None, U_GATE, i, c, ds(i * (4 * P) + (C_GATE + c * P), P))
            rolled(sp, 4, gate_units, peel=0)

            uq = t["w_uq"][0].rearrange("(k p) (a h e) -> p k a h e", p=P, h=2, e=NOPE + ROPE)
            ukv = t["w_ukv"][0].rearrange("(k p) (a h v d) -> p k a h v d", p=P, h=2, v=2, d=VD)

            def pair_units(i):
                def head_halves(c, wait_value, dst, src, second):
                    wait_apart(sp, lo_ready, wait_value)
                    for h in range(2):
                        sp.dma_start(dst[:, :, h], src(h)).then_inc(raw_landed[c] if h == 0 else second, 16)

                def queries_keys(c, h, wait_value):
                    wait_apart(sp, lo_ready, wait_value)
                    sp.dma_start(raw[:, c, 0:KQ * P].rearrange("p (k m) -> p k m", k=KQ),
                                 uq[:, :, ds(i, 1), h, 0:NOPE].rearrange("p k a e -> p k (a e)")) \
                      .then_inc(raw_landed[c], 16)
                    sp.dma_start(raw[:, c, KQ * P:(KQ + KKV) * P].rearrange("p (k m) -> p k m", k=KKV),
                                 ukv[:, :, ds(i, 1), h, 0].rearrange("p k a d -> p k (a d)")) \
                      .then_inc(kw_landed[h], 16)
                head_halves(0, i * 4 + (U_ATT - 3), raw[:, 0, 0:W_QR].rearrange("p (k h e) -> p k h e", k=KQ, h=2),
                            lambda h: uq[:, :, ds(i, 1), h, NOPE:NOPE + ROPE].rearrange("p k a e -> p k (a e)"), dup_landed[0])
                queries_keys(1, 0, i * 4 + (U_ATT - 2))
                head_halves(2, i * 4 + (U_ATT - 1), raw[:, 2, 0:W_V].rearrange("p (k h d) -> p k h d", k=KKV, h=2),
                            lambda h: ukv[:, :, ds(i, 1), h, 1].rearrange("p k a d -> p k (a d)"), dup_landed[1])
                queries_keys(3, 1, i * 4 + U_ATT)
            rolled(sp, PAIRS, pair_units, peel=0)

            def gate_back(g):
                if g < 2:
                    sp.wait_ge(conv_done, KD)
                    for e in range(2):
                        sp.wait_ge(gate_stored[e], 16 * KD)
                wait(sp, merged, g - 1)
                sp.dma_start(gin[:, g % 2], gates[g]).then_inc(gin_landed[g % 2], 16)

            projections = [t[name][0].rearrange("(k p) n -> p k n", p=P) for name in ("w_o_attn", "w_conv_out")]
            for g in range(2 * KD + 3):
                m = g % KD
                if g < 2 * KD:
                    columns(projections[g // KD], None, U_O + g - g % 4, 0, g % 4, slice(m * P, (m + 1) * P))
                if g >= 3:
                    gate_back(g - 3)
            sp.wait_ge(c_lo, KD)
            for g, (name, t0, nt) in enumerate((("x_prompt", 0, 4), ("x_sample", 4, 2))):
                sp.dma_start(h1[:, t0:t0 + nt], t[name][0].rearrange("(t p) n -> p t n", p=P)) \
                  .then_inc(h_landed[g], 16)

            def row_units(w, base, half, k0):
                def body(i):
                    for c in range(4):
                        wait_apart(sp, lo_ready, i * 4 + (base + c - 3))
                        sp.dma_start(raw[:, c].rearrange("p (k n) -> p k n", k=2),
                                     w[:, ds(i * 4 + c, 1), :, half * HALF:(half + 1) * HALF]
                                     .rearrange("p u k n -> p (u k) n")).then_inc(raw_landed[c], 16)
                return body
            wo = t["w_out"][0].rearrange("(u k p) n -> p u k n", k=2, p=P)
            for half in range(2):
                rolled(sp, 1, row_units(wo, U_OUT + 4 * half, half, 0), peel=1)
            wi = t["w_mlp_in"][0].rearrange("(k p) n -> p k n", p=P)

            def in_units(i):
                for c in range(4):
                    columns(wi, None, U_IN, i, c, ds(i * (4 * P) + c * P, P))
            rolled(sp, KF // 4, in_units, peel=0)
            wm = t["w_mlp_out"][0].rearrange("(u k p) n -> p u k n", k=2, p=P)
            for half in range(2):
                rolled(sp, KF // 8, row_units(wm, U_FF + 16 * half, half, 0), peel=0)
            sp.wait_ge(u2lo_ready, KD)
            sp.dma_start(gfinal[:, :], t["norm_final"].rearrange("(a n) -> a n", a=1).to_broadcast([P, D])) \
              .then_inc(gfinal_landed, 16)
            for i in range(NT):
                sp.wait_ge(y_out, i + 1)
                dst = t["y_prompt"][0, i * P:(i + 1) * P, :] if i < 4 else t["y_sample"][0, (i - 4) * P:(i - 3) * P, :]
                sp.dma_start(dst, yout[:, i]).then_inc(y_stored, 16)
            sp.wait_ge(y_stored, 16 * NT)

        @block.scalar
        def _(act):
            act.wait_ge(vec_clear, 1)
            for name, (r, n) in VEC.items():
                src = t[name] if name != "b_gate" else t[name]
                act.dma_start(vecrows[r:r + n, :], src[0].rearrange("(k p) -> k p", p=P)).then_inc(consts_landed, 16)
            act.dma_start(tapsrows[0:TAPS, :], t["conv_w"][0]).then_inc(taps_landed, 16)

            act.wait_ge(setup, 7)
            for j, i in enumerate((0, 1, 6, 2, 3, 4, 5)):
                r = T_META if i == 6 else P
                act.wait_ge(x_landed[i], 16)
                wait(act, x_sq, j)
                nc.scalar.activation(junk0[0:r, :], xt[0:r, i], ACT.Square,
                                     accum_out=sumsq[0:r, i:i + 1]).then_inc(x_sq, 1)
            act.wait_ge(x_sq, 7)
            nc.scalar.activation(root[:, 0:7], sumsq[:, 0:7], ACT.Sqrt, bias=eps[:, 0:1],
                                 scale=1.0 / D).then_inc(x_root, 1)
            hi_unit(act, 0, 0, 0)
            act.wait_ge(vec_ready, 2)
            for k in range(KD):
                act.wait_ge(ut_ready, k + 1)
                nc.scalar.activation(uhi[:, k], psum[:, k % 4, 0:TK], ACT.Copy,
                                     scale=vcol("norm_mix", k)).then_inc(uhi_ready, 1)

            for n in range(8):
                if n in (5, 6):
                    act.wait_ge(dup_landed[n - 5], 16)
                hi_unit(act, 0, 0, n + 1) if n < 3 else hi_unit(act, 4, 0, n + 1 - 4)
                if n < 6:
                    act.wait_ge(raw_q, n + 1)
                    wait(act, sq_sum, n - 1)
                    src, w = (qraw[:, n], TQ) if n < 4 else (kvraw[:, n - 4], TK)
                    nc.scalar.activation(sqt[:, n % 2, 0:w], src, ACT.Square).then_inc(q_sq, 1)
                if n == 7:
                    act.wait_ge(unit_used, 8)
                    for b in range(4):
                        o = b ^ 1
                        ins = nc.scalar.activation(krsw[32 * o:32 * o + 32, :], psum[32 * b:32 * b + 32, 2, 0:TK], ACT.Copy)
                    ins.then_inc(kr_sw, 1)
            act.wait_ge(ss_mm, 1)
            nc.scalar.activation(sqacc[:, 0, 0:TQ], psum[:, 3, 0:TQ], ACT.Sqrt, bias=eps[:, 0:1],
                                 scale=1.0 / Q_LORA).then_inc(ss_root, 1)

            def kr_split():
                act.wait_ge(kr_rot, 1)
                nc.scalar.activation(kra[0:64, :], krt[0:64, :], ACT.Copy)
                nc.scalar.activation(krb[64:128, :], krt[64:128, :], ACT.Copy).then_inc(kr_hi, 1)

            def latent_hi(j):
                act.wait_ge(qkv_scaled, j + 1)
                dst, src = (qhi[:, j], qraw[:, j]) if j < 4 else (kvhi[:, j - 4], kvraw[:, j - 4])
                nc.scalar.activation(dst, src, ACT.Copy).then_inc(qkv_hi, 1)

            def conv_step(i, extras=()):
                for c in range(4):
                    hi_unit(act, U_CONV, i, c + 1)
                    if c % 2 == 0:
                        j = i * 2 + c // 2
                        act.wait_ge(unit_used, i * 4 + (U_CONV + c + 1))
                        wait(act, glu_ready, i * 2 + (c // 2 - 1))
                        if isinstance(i, int) and i == 0 and c == 0:
                            act.wait_ge(sq_sum, 6)
                        nc.scalar.activation(sg[:, c // 2], psum[:, 0, 0:TK], ACT.Sigmoid).then_inc(sg_ready, 1)
                    if extras and c < len(extras):
                        for f in extras[c]:
                            f()

            def kv_root():
                act.wait_ge(ss_mm, 2)
                nc.scalar.activation(sqacc[:, 1, :], psum[:, 3, 0:TK], ACT.Sqrt, bias=eps[:, 0:1],
                                     scale=1.0 / KV_LORA).then_inc(ss_root, 1)
            conv_step(0, ((kr_split,), (), (kv_root, lambda: latent_hi(0), lambda: latent_hi(1)),
                          (lambda: latent_hi(2), lambda: latent_hi(3))))
            conv_step(1, ((lambda: latent_hi(4), lambda: latent_hi(5)),))
            with act.Fori(2, 4) as i:
                conv_step(i)

            def gate_step(i):
                for c in range(4):
                    end = isinstance(i, int) and i == 3 and c == 3
                    if end:
                        act.wait_ge(dup_landed[0], 32)
                    hi_unit(act, U_GATE, i, c + 1, W_QR if end else D)
                    act.wait_ge(unit_used, i * 4 + (U_GATE + c + 1))
                    wait(act, gate_stored[c % 2], i * 32 + 16 * (c // 2))
                    if isinstance(i, int) and i == 0 and c == 0:
                        act.wait_ge(qkv_lo, 6)
                    nc.scalar.activation(gout[:, c % 2], psum[:, c % 2, 0:TQ], ACT.Sigmoid,
                                         bias=vcol("b_gate", i * 4 + c)).then_inc(gate_ready, 1)
                    act.wait_ge(gate_ready, i * 4 + (c + 1))
                    dst = gates[ds(i * 4 + c, 1)].rearrange("a p n -> p (a n)") if not isinstance(i, int) else gates[i * 4 + c]
                    act.dma_start(dst, gout[:, c % 2]).then_inc(gate_stored[c % 2], 16)
            rolled(act, 4, gate_step, peel=1, last=1)

            def E(p, hh, q):
                g = p * 12 + (6 * hh + q)
                grp, _ = qtile(q)
                act.wait_ge(max_ready, g + 1)
                wait(act, pt_mm, g - 1)
                n = len(grp["pieces"])
                src = psum[:, q % 2, :].rearrange("p (b n) -> p b n", b=2)[:, 0:n, 0:grp["pieces"][0][1]]
                dst = prob[:, q % 2, 0:grp["nk"]].rearrange("p (b n) -> p b n", b=n)
                nc.scalar.activation(dst, src, ACT.Exp, bias=negmax[:, q % 4:q % 4 + 1],
                                     accum_out=psumexp[:, q % 4:q % 4 + 1]).then_inc(exp_ready, 1)

            def H(p, hh, q):
                g, b = p * 12 + (6 * hh + q), 3 * hh + q // 2
                act.wait_ge(pt_mm, g + 1)
                wait(act, av_mm, p * 6 + (b - 1))
                if q in (1, 3):
                    nc.scalar.activation(pthi[:, b % 2, TAIL], bank[:, 6, 0:2 * P], ACT.Copy)
                nc.scalar.activation(pthi[:, b % 2, 0:main_tiles(q), (q % 2) * P:(q % 2 + 1) * P],
                                     bank[:, 4 + q % 2, 0:main_tiles(q) * P].rearrange("p (t n) -> p t n", n=P),
                                     ACT.Copy).then_inc(pt_hi, 1)

            def O(p, hh, b):
                act.wait_ge(av_mm, p * 6 + (3 * hh + b + 1))
                dst = oraw[:, ds(p * 2 + hh, 1), b * 2 * P:(b + 1) * 2 * P]
                nc.scalar.activation(dst, bank[:, 7, 0:2 * P].rearrange("p (a n) -> p a n", a=1), ACT.Copy) \
                  .then_inc(o_ready, 1)

            def q_hi(p, hh, pair):
                act.wait_ge(qn_mm, p * 2 + (hh + 1))
                nc.scalar.activation(qnhi[:, :], psum[:, pair, 0:TQ], ACT.Copy, scale=SCALE).then_inc(qn_hi, 1)

            def k_hi(p, hh, pair):
                act.wait_ge(unit_used, p * 4 + (U_ATT + 2 + 2 * hh))
                nc.scalar.activation(knhi[:, :], psum[:, pair, 0:TK], ACT.Copy).then_inc(kn_hi, 1)

            def rotary_swap(p):
                act.wait_ge(unit_used, p * 4 + (U_ATT + 1))
                for b in range(4):
                    o = b ^ 1
                    ins = nc.scalar.activation(qsw[32 * o:32 * o + 32, :], psum[32 * b:32 * b + 32, 0, 0:TQ], ACT.Copy)
                ins.then_inc(qr_sw, 1)

            def rotary_hi(p):
                act.wait_ge(qr_rot, p + 1)
                nc.scalar.activation(qrs[0][0:64, :], qt[0:64, :], ACT.Copy, scale=SCALE)
                nc.scalar.activation(qrs[1][64:128, :], qt[64:128, :], ACT.Copy, scale=SCALE).then_inc(qr_hi, 1)

            def v_hi_first(p):
                act.wait_ge(v_mm, p + 1)
                nc.scalar.activation(vhi[:, 0:4], psum[:, 2, :].rearrange("p (t n) -> p t n", t=4), ACT.Copy).then_inc(v_hi, 1)

            def v_hi_rest(p):
                act.wait_ge(unit_used, p * 4 + (U_ATT + 3))
                nc.scalar.activation(vhi[:, 4:6], bank[:, 6].rearrange("p (t n) -> p t n", t=2), ACT.Copy).then_inc(v_hi, 1)
                nc.scalar.activation(vhi[:, 6:8], bank[:, 7].rearrange("p (t n) -> p t n", t=2), ACT.Copy,
                                     scale=tail_mask[:, 0:1]).then_inc(v_hi, 1)

            def start_pair(n, between=lambda step: None):
                rotary_swap(n)
                between(0)
                act.wait_ge(dup_landed[1], n * 16 + 32)
                hi_unit(act, U_ATT, n, 2, W_V)
                q_hi(n, 0, 1)
                rotary_hi(n)
                between(1)
                k_hi(n, 0, 0)
                act.wait_ge(kw_landed[1], n * 16 + 16)
                hi_unit(act, U_ATT, n, 3, W_QK)
                between(2)
                v_hi_first(n)

            def pair_step(p):
                final = isinstance(p, int) and p == PAIRS - 1
                for hh in range(2):
                    E(p, hh, 0), E(p, hh, 1)
                    v_hi_rest(p) if hh == 0 else O(p, 0, 2)
                    E(p, hh, 2)
                    if isinstance(p, int) and p == 0 and hh == 0:
                        for e in range(2):
                            act.wait_ge(gate_stored[e], 16 * KD)
                    H(p, hh, 0)
                    if hh == 0:
                        if not final:
                            act.wait_ge(dup_landed[0], p * 16 + 48)
                        hi_unit(act, U_ATT, p, 4, D if final else W_QR)
                    else:
                        if not final:
                            act.wait_ge(kw_landed[0], p * 16 + 32)
                        hi_unit(act, U_ATT, p, 5, D if final else W_QK)
                    E(p, hh, 3), H(p, hh, 1), E(p, hh, 4), H(p, hh, 2), O(p, hh, 0), E(p, hh, 5), H(p, hh, 3), H(p, hh, 4)
                    if hh == 0:
                        q_hi(p, 1, 0), H(p, hh, 5), k_hi(p, 1, 1), O(p, hh, 1)
                    elif not final:
                        rest = (lambda: H(p, 1, 5), lambda: O(p, 1, 1), lambda: O(p, 1, 2))
                        start_pair(p + 1, lambda step: rest[step]())
                    else:
                        O(p, hh, 1), H(p, hh, 5), O(p, hh, 2)
            act.wait_ge(kw_landed[0], 16)
            hi_unit(act, U_ATT, 0, 1, W_QK)
            start_pair(0)
            rolled(act, PAIRS, pair_step, peel=1, last=1)

            act.wait_ge(o_ready, 3 * HEADS)
            for h in range(HEADS):
                nc.scalar.activation(ohi[:, h], oraw[:, h], ACT.Copy).then_inc(o_hi, 1)
            hi_unit(act, U_O, 0, 2)
            hi_unit(act, U_O, 0, 3)
            act.wait_ge(mean_mm, 1)
            nc.scalar.activation(mu[:, :], psum[:, 2, 0:TQ], ACT.Copy, scale=1.0 / D).then_inc(mu_ready, 1)

            def ln_squares(js):
                for j in js:
                    act.wait_ge(centred, j + 1)
                    wait(act, ln_sqsum, j - 1)
                    nc.scalar.activation(lnsq[:, j % 2], cs[:, j, 0:TQ], ACT.Square).then_inc(ln_sq, 1)
            hi_unit(act, U_O, 0, 4)
            ln_squares(range(0, 3))
            hi_unit(act, U_O, 1, 1)
            ln_squares(range(3, 6))
            hi_unit(act, U_O, 1, 2)
            ln_squares(range(6, 8))
            hi_unit(act, U_O, 1, 3)
            act.wait_ge(var_mm, 1)
            nc.scalar.activation(lnacc[:, :], psum[:, 3, 0:TQ], ACT.Sqrt, bias=eps[:, 0:1],
                                 scale=1.0 / D).then_inc(ln_root, 1)
            hi_unit(act, U_O, 1, 4)
            for k in range(KD):
                act.wait_ge(ln_scaled, k + 1)
                nc.scalar.activation(cs[:, k, 0:TQ], cs[:, k, 0:TQ], ACT.Silu,
                                     bias=vcol("conv_ln_b", k)).then_inc(c_silu, 1)
                act.wait_ge(c_silu, k + 1)
                nc.scalar.activation(chi[:, k], cs[:, k, 0:TQ], ACT.Copy).then_inc(c_hi, 1)
                if k == 3:
                    hi_unit(act, U_CO, 0, 1)

            for m in range(KD):
                if m > 0:
                    hi_unit(act, U_CO, m // 4, m % 4 + 1)
                act.wait_ge(merged, KD + m + 1)
                nc.scalar.activation(zhi[:, m], zacc[:, m], ACT.Copy).then_inc(z_hi, 1)
            for n in range(8):
                hi_unit(act, U_OUT, n // 4, n % 4 + 1)

            for i in range(NT):
                act.wait_ge(h_ready, NT + i + 1)
                wait(act, h_sq, i)
                nc.scalar.activation(junk1[:, :], h1[:, i], ACT.Square, accum_out=sumsq[:, i:i + 1]).then_inc(h_sq, 1)
            act.wait_ge(h_sq, NT)
            nc.scalar.activation(root[:, 0:NT], sumsq[:, 0:NT], ACT.Sqrt, bias=eps[:, 0:1], scale=1.0 / D).then_inc(h_root, 1)
            for k in range(KD):
                act.wait_ge(u2t_ready, k + 1)
                nc.scalar.activation(u2hi[:, k], psum[:, k % 4, 0:TQ], ACT.Copy, scale=vcol("norm_mlp", k)).then_inc(u2hi_ready, 1)

            def in_step(i):
                for c in range(4):
                    hi_unit(act, U_IN, i, c + 1)
                    act.wait_ge(unit_used, i * 4 + (U_IN + c + 1))
                    nc.scalar.activation(hid[:, ds(i * 4 + c, 1), :], psum[:, c % 2, 0:TQ].rearrange("p (a n) -> p a n", a=1),
                                         ACT.Relu).then_inc(relu_ready, 1)
            rolled(act, KF // 4, in_step, peel=0)

            def hid_hi(i, c, half):
                n = i * 4 + (U_FF + 16 * half + c)
                act.wait_ge(unit_used, n - 1)
                nc.scalar.activation(hidhi[:, c % 2], hid[:, ds(i * 8 + 2 * c, 2), :], ACT.Copy).then_inc(hidhi_ready, 1)
            act.wait_ge(hid_ready, KF)
            hid_hi(0, 0, 0)

            def ff_step(half, last):
                def body(i):
                    for c in range(4):
                        end = isinstance(i, int) and i == 3 and c == 3
                        if end and half == 1:
                            continue
                        hi_unit(act, U_FF + 16 * half, i, c + 1)
                        if end:
                            hid_hi(0, 0, 1)
                        elif c < 3:
                            hid_hi(i, c + 1, half)
                        else:
                            hid_hi(i + 1, 0, half)
                return body
            rolled(act, 4, ff_step(0, False), peel=0, last=1)
            rolled(act, 4, ff_step(1, True), peel=0, last=1)

            for i in range(NT):
                act.wait_ge(y_ready, NT + i + 1)
                wait(act, y_sq, i)
                nc.scalar.activation(junk2[:, :], h1[:, i], ACT.Square, accum_out=sumsq[:, i:i + 1]).then_inc(y_sq, 1)
                act.wait_ge(y_sq, i + 1)
                nc.scalar.activation(root[:, i:i + 1], sumsq[:, i:i + 1], ACT.Sqrt, bias=eps[:, 0:1], scale=1.0 / D).then_inc(y_root, 1)

        @block.vector
        def _(dve):
            dve.wait_ge(x_root, 1)
            nc.vector.reciprocal(rstd[:, 0:7], root[:, 0:7]).then_inc(x_rstd, 1)
            dve.wait_ge(x_rstd, 1)
            for i in range(7):
                r = T_META if i == 6 else P
                nc.vector.tensor_scalar(xt[0:r, i], xt[0:r, i], rstd[0:r, i:i + 1], None, ALU.mult).then_inc(x_scaled, 1)
            dve.wait_ge(vec_t, 1)
            nc.vector.tensor_copy(vec[:, :], psum[:, 0, 0:NVEC]).then_inc(vec_ready, 1)
            dve.wait_ge(vec_t, 2)
            nc.vector.tensor_copy(convw[:, :, :], psum[:, 1, 0:KD * 32].rearrange("p (k n) -> p k n", k=KD)[:, :, 0:TAPS]).then_inc(vec_ready, 1)
            dve.wait_ge(vec_ready, 2)
            for k in range(KD):
                dve.wait_ge(uhi_ready, k + 1)
                nc.vector.scalar_tensor_tensor(out=ulo[:, k], in0=psum[:, k % 4, 0:TK], scalar=vcol("norm_mix", k),
                                               in1=uhi[:, k].bitcast(F32), op0=ALU.mult, op1=ALU.subtract).then_inc(ulo_ready, 1)

            for n in range(6):
                dve.wait_ge(unit_used, n + 1)
                dst, w = (qraw[:, n], TQ) if n < 4 else (kvraw[:, n - 4], TK)
                nc.vector.tensor_copy(dst, psum[:, n % 2, 0:w]).then_inc(raw_q, 1)
            dve.wait_ge(tables_landed, 32)
            dve.wait_ge(kr_sw, 1)
            nc.vector.tensor_tensor(out=krt[:, :], in0=psum[:, 2, 0:TK], in1=rcos[:, :], op=ALU.mult).then_inc(kr_cos, 1)
            dve.wait_ge(kr_cos, 1)
            dve.wait_ge(kr_sin, 1)
            nc.vector.tensor_tensor(out=krt[:, :], in0=krt[:, :], in1=krsw[:, :], op=ALU.add).then_inc(kr_rot, 1)

            def kr_los():
                dve.wait_ge(kr_hi, 1)
                dve.wait_ge(kr_rot, 1)
                nc.vector.tensor_tensor(out=kra[64:128, :], in0=krt[64:128, :], in1=krb[64:128, :].bitcast(F32), op=ALU.subtract)
                nc.vector.tensor_tensor(out=krb[0:64, :], in0=krt[0:64, :], in1=kra[0:64, :].bitcast(F32), op=ALU.subtract).then_inc(kr_lo, 1)

            def recip_q():
                dve.wait_ge(ss_root, 1)
                nc.vector.reciprocal(sqacc[:, 0, 0:TQ], sqacc[:, 0, 0:TQ]).then_inc(ss_rstd, 1)

            def recip_kv():
                dve.wait_ge(ss_root, 2)
                nc.vector.reciprocal(sqacc[:, 1, :], sqacc[:, 1, :]).then_inc(ss_rstd, 1)

            def latent_scale(j):
                dve.wait_ge(ss_rstd, 1 if j < 4 else 2)
                src, g, r = ((qraw[:, j], vcol("norm_q", j), sqacc[:, 0, 0:TQ]) if j < 4 else
                             (kvraw[:, j - 4], vcol("norm_kv", j - 4), sqacc[:, 1, :]))
                nc.vector.scalar_tensor_tensor(out=src, in0=src, scalar=g, in1=r, op0=ALU.mult, op1=ALU.mult).then_inc(qkv_scaled, 1)

            def latent_lo(j):
                dve.wait_ge(qkv_hi, j + 1)
                dst, src, h = ((qlo[:, j], qraw[:, j], qhi[:, j]) if j < 4 else
                               (kvlo[:, j - 4], kvraw[:, j - 4], kvhi[:, j - 4]))
                nc.vector.tensor_tensor(out=dst, in0=src, in1=h.bitcast(F32), op=ALU.subtract).then_inc(qkv_lo, 1)

            def tap(tile, k, before, r=None):
                half = (k if isinstance(k, int) else r) % 2
                a = acc[:, half, 0:SPAN]
                j = tile if isinstance(tile, int) else None
                def pick(x, lo_, n_):
                    return x[:, ds(tile, 1), lo_:lo_ + n_] if j is None else x[:, j:j + 1, lo_:lo_ + n_]
                if isinstance(k, int):
                    src = pick(cs, 1 + k, SPAN).rearrange("p a n -> p (a n)")
                    w = pick(convw, k, 1).rearrange("p a n -> p (a n)")
                else:
                    src = cs[:, j, ds(k + 1, SPAN)]
                    w = convw[:, j, ds(k, 1)]
                if isinstance(k, int) and k == 0:
                    b = vcol("conv_b", tile)
                    ins = nc.vector.tensor_scalar(a, src, w, b, ALU.mult, ALU.add)
                elif isinstance(k, int) and k == 1:
                    ins = nc.vector.tensor_scalar(a, src, w, None, ALU.mult)
                else:
                    dve.wait_ge(tap_done, before - 1)
                    ins = nc.vector.scalar_tensor_tensor(out=a, in0=src, scalar=w, in1=a, op0=ALU.mult, op1=ALU.add)
                ins.then_inc(tap_done, 1)

            def combine(tile, done):
                dve.wait_ge(tap_done, done)
                def out(lo_, n_):
                    return (cs[:, ds(tile, 1), lo_:lo_ + n_].rearrange("p a n -> p (a n)") if not isinstance(tile, int)
                            else cs[:, tile, lo_:lo_ + n_])
                nc.vector.tensor_tensor(out=out(0, T_PROMPT), in0=acc[:, 0, 0:T_PROMPT], in1=acc[:, 1, 0:T_PROMPT], op=ALU.add)
                nc.vector.tensor_tensor(out=out(T_PROMPT, T_SAMPLE), in0=acc[:, 0, ACC_SAMPLE:ACC_SAMPLE + T_SAMPLE],
                                        in1=acc[:, 1, ACC_SAMPLE:ACC_SAMPLE + T_SAMPLE], op=ALU.add).then_inc(conv_done, 1)

            def conv_part(tile, c):
                if c == 0:
                    wait(dve, conv_done, tile)
                for k in range(8 * c, min(8 * c + 8, TAPS)):
                    tap(tile, k, tile * TAPS + k)
                if c == 3:
                    combine(tile, tile * TAPS + TAPS)

            def glu(i, c):
                j = i * 2 + c // 2
                dve.wait_ge(sg_ready, i * 2 + (c // 2 + 1))
                dve.wait_ge(unit_used, i * 4 + (U_CONV + c + 1))
                def dst(lo_, n_):
                    return cs[:, ds(j, 1), lo_:lo_ + n_].rearrange("p a n -> p (a n)") if not isinstance(j, int) else cs[:, j, lo_:lo_ + n_]
                s = sg[:, c // 2]
                for o, c0, n in ((CS_PROMPT, 0, T_PROMPT), (CS_META2, META0, T_META + T_SAMPLE), (0, META0, T_META)):
                    ins = nc.vector.tensor_tensor(out=dst(o, n), in0=psum[:, 1, c0:c0 + n], in1=s[:, c0:c0 + n], op=ALU.mult)
                ins.then_inc(glu_ready, 1)

            dve.wait_ge(pads_zero, 2)
            extras0 = {0: [kr_los, recip_q], 1: [], 2: [lambda: latent_scale(0), lambda: latent_scale(1),
                                                       lambda: latent_scale(2), lambda: latent_scale(3), lambda: latent_lo(0)],
                       3: [lambda: latent_lo(1), lambda: latent_lo(2), lambda: latent_lo(3), recip_kv,
                           lambda: latent_scale(4), lambda: latent_scale(5)]}
            for c in range(4):
                if c % 2:
                    glu(0, c)
                for f in extras0[c]:
                    f()

            def conv_step(i):
                dve.wait_ge(glu_ready, i * 2)
                for c in range(4):
                    if c % 2:
                        glu(i, c)
                    conv_part(i - 1, c)
            conv_step(1)
            latent_lo(4)
            latent_lo(5)
            with dve.Fori(2, 4) as i:
                conv_step(i)

            dve.wait_ge(glu_ready, KD)
            with dve.Fori(3, 7) as tile:
                for c in range(4):
                    conv_part(tile, c)

            LAST = KD - 1
            dve.wait_ge(conv_done, LAST)
            tap(LAST, 0, LAST * TAPS)
            tap(LAST, 1, LAST * TAPS + 1)

            def M(p, hh, q):
                g = p * 12 + (6 * hh + q)
                grp, _ = qtile(q)
                n = len(grp["pieces"])
                dve.wait_ge(s_ready, g + 1)
                src = psum[:, q % 2, :].rearrange("p (b n) -> p b n", b=2)[:, 0:n, 0:grp["pieces"][0][1]]
                nc.vector.tensor_reduce(out=negmax[:, q % 4:q % 4 + 1], in_=src, axis=AX.XY, op=ALU.max,
                                        negate=True).then_inc(max_ready, 1)

            def R(p, hh, q):
                g = p * 12 + (6 * hh + q)
                dve.wait_ge(exp_ready, g + 1)
                nc.vector.reciprocal(rsum[:, q % 4:q % 4 + 1], psumexp[:, q % 4:q % 4 + 1]).then_inc(rsum_ready, 1)

            def L(p, hh, q):
                g, b = p * 12 + (6 * hh + q), 3 * hh + q // 2
                dve.wait_ge(pt_hi, g + 1)
                if q in (1, 3):
                    nc.vector.tensor_tensor(out=ptlo[:, b % 2, TAIL], in0=bank[:, 6, 0:2 * P],
                                            in1=pthi[:, b % 2, TAIL].bitcast(F32), op=ALU.subtract).then_inc(tail_lo, 1)
                sl = (slice(None), b % 2, slice(0, main_tiles(q)), slice((q % 2) * P, (q % 2 + 1) * P))
                nc.vector.tensor_tensor(out=ptlo[sl], in0=bank[:, 4 + q % 2, 0:main_tiles(q) * P].rearrange("p (t n) -> p t n", n=P),
                                        in1=pthi[sl].bitcast(F32), op=ALU.subtract).then_inc(pt_lo, 1)

            def q_lo(p, hh, pair):
                dve.wait_ge(qn_hi, p * 2 + (hh + 1))
                nc.vector.scalar_tensor_tensor(out=qnlo[:, :], in0=psum[:, pair, 0:TQ], scalar=SCALE, in1=qnhi[:, :].bitcast(F32),
                                               op0=ALU.mult, op1=ALU.subtract).then_inc(qn_lo, 1)

            def k_lo(p, hh, pair):
                dve.wait_ge(kn_hi, p * 2 + (hh + 1))
                nc.vector.tensor_tensor(out=knlo[:, :], in0=psum[:, pair, 0:TK], in1=knhi[:, :].bitcast(F32),
                                        op=ALU.subtract).then_inc(kn_lo, 1)

            def rotary_cos(p):
                dve.wait_ge(qr_sw, p + 1)
                nc.vector.tensor_tensor(out=qt[:, 0:T_PROMPT], in0=psum[:, 0, 0:T_PROMPT], in1=rcos[:, 0:T_PROMPT], op=ALU.mult)
                nc.vector.tensor_tensor(out=qt[:, T_PROMPT:TQ], in0=psum[:, 0, T_PROMPT:TQ], in1=rcos[:, SAMP0:TK], op=ALU.mult).then_inc(qr_cos, 1)

            def rotary_sum_lo(p):
                dve.wait_ge(qr_cos, p + 1)
                dve.wait_ge(qr_sin, p + 1)
                nc.vector.tensor_tensor(out=qt[:, :], in0=qt[:, :], in1=qsw[:, :], op=ALU.add).then_inc(qr_rot, 1)
                dve.wait_ge(qr_hi, p + 1)
                dve.wait_ge(qr_rot, p + 1)
                nc.vector.scalar_tensor_tensor(out=qrs[0][64:128, :], in0=qt[0:64, :], scalar=SCALE, in1=qrs[0][0:64, :].bitcast(F32),
                                               op0=ALU.mult, op1=ALU.subtract)
                nc.vector.scalar_tensor_tensor(out=qrs[1][0:64, :], in0=qt[64:128, :], scalar=SCALE, in1=qrs[1][64:128, :].bitcast(F32),
                                               op0=ALU.mult, op1=ALU.subtract).then_inc(qr_lo, 1)

            def v_lo_first(p):
                dve.wait_ge(v_hi, p * 3 + 1)
                nc.vector.tensor_tensor(out=vlo[:, 0:4], in0=psum[:, 2, :].rearrange("p (t n) -> p t n", t=4),
                                        in1=vhi[:, 0:4].bitcast(F32), op=ALU.subtract).then_inc(v_lo, 1)

            def v_lo_rest(p):
                dve.wait_ge(v_hi, p * 3 + 3)
                nc.vector.tensor_tensor(out=vlo[:, 4:6], in0=bank[:, 6].rearrange("p (t n) -> p t n", t=2),
                                        in1=vhi[:, 4:6].bitcast(F32), op=ALU.subtract).then_inc(v_lo, 1)
                nc.vector.scalar_tensor_tensor(out=vlo[:, 6:8].rearrange("p t n -> p (t n)"), in0=bank[:, 7], scalar=tail_mask[:, 0:1],
                                               in1=vhi[:, 6:8].rearrange("p t n -> p (t n)").bitcast(F32), op0=ALU.mult, op1=ALU.subtract).then_inc(v_lo, 1)

            def start_pair(n, between=lambda step: None):
                rotary_cos(n)
                between(0)
                q_lo(n, 0, 1)
                rotary_sum_lo(n)
                k_lo(n, 0, 0)
                between(1)
                v_lo_first(n)

            def pair_step(p):
                final = isinstance(p, int) and p == PAIRS - 1

                def taps(a, b):
                    for r in range(a, b):
                        tap(LAST, p * 6 + (2 + r), p * 6 + (LAST * TAPS + 2 + r), r)
                for hh in range(2):
                    M(p, hh, 0), M(p, hh, 1), R(p, hh, 0), R(p, hh, 1), M(p, hh, 2)
                    if hh == 0:
                        v_lo_rest(p)
                    R(p, hh, 2), M(p, hh, 3), L(p, hh, 0)
                    R(p, hh, 3), M(p, hh, 4), L(p, hh, 1)
                    R(p, hh, 4), M(p, hh, 5), L(p, hh, 2)
                    R(p, hh, 5), L(p, hh, 3), L(p, hh, 4)
                    taps(2 * hh, 2 * hh + 2)
                    if hh == 0:
                        q_lo(p, 1, 0), L(p, hh, 5), k_lo(p, 1, 1)
                    elif not final:
                        rest = (lambda: L(p, 1, 5), lambda: taps(4, 6))
                        start_pair(p + 1, lambda step: rest[step]())
                    else:
                        L(p, hh, 5)
                        taps(4, 6)
            start_pair(0)
            rolled(dve, PAIRS, pair_step, peel=1, last=1)

            for h in range(HEADS):
                dve.wait_ge(o_hi, h + 1)
                nc.vector.tensor_tensor(out=olo[:, h], in0=oraw[:, h], in1=ohi[:, h].bitcast(F32), op=ALU.subtract).then_inc(o_lo, 1)
            for k in range(26, TAPS):
                tap(LAST, k, LAST * TAPS + k)
            combine(LAST, KD * TAPS)

            def gate_attn(m):
                dve.wait_ge(unit_used, U_O + m + 1)
                dve.wait_ge(gin_landed[m % 2], 16 * (m // 2 + 1))
                nc.vector.tensor_tensor(out=zacc[:, m], in0=psum[:, m % 2, 0:TQ], in1=gin[:, m % 2], op=ALU.mult).then_inc(merged, 1)

            def centre(js):
                dve.wait_ge(mu_ready, 1)
                for j in js:
                    dve.wait_ge(conv_done, KD)
                    nc.vector.tensor_tensor(out=cs[:, j, 0:TQ], in0=cs[:, j, 0:TQ], in1=mu[:, :], op=ALU.subtract).then_inc(centred, 1)

            def ln_scale(k):
                dve.wait_ge(ln_rstd, 1)
                nc.vector.scalar_tensor_tensor(out=cs[:, k, 0:TQ], in0=cs[:, k, 0:TQ], scalar=vcol("conv_ln_g", k), in1=lnr[:, :],
                                               op0=ALU.mult, op1=ALU.mult).then_inc(ln_scaled, 1)

            def c_low(k):
                dve.wait_ge(c_hi, k + 1)
                nc.vector.tensor_tensor(out=clo[:, k], in0=cs[:, k, 0:TQ], in1=chi[:, k].bitcast(F32), op=ALU.subtract).then_inc(c_lo, 1)
            gate_attn(0), gate_attn(1)
            centre(range(0, 3))
            gate_attn(2)
            centre(range(3, 6))
            gate_attn(3)
            centre(range(6, 8))
            gate_attn(4), gate_attn(5)
            dve.wait_ge(ln_root, 1)
            dve.wait_ge(centred, KD)
            nc.vector.reciprocal(lnr[:, :], lnacc[:, :]).then_inc(ln_rstd, 1)
            gate_attn(6)
            ln_scale(0), ln_scale(1), c_low(0), ln_scale(2), c_low(1)
            gate_attn(7)
            ln_scale(3), c_low(2), ln_scale(4), c_low(3), ln_scale(5), c_low(4), ln_scale(6), c_low(5), ln_scale(7), c_low(6), c_low(7)

            for m in range(KD):
                dve.wait_ge(unit_used, U_CO + m + 1)
                dve.wait_ge(gin_landed[m % 2], 16 * ((KD + m) // 2 + 1))
                nc.vector.tensor_tensor(out=gconv[:, :], in0=psum[:, m % 2, 0:TQ], in1=gin[:, m % 2], op=ALU.mult).then_inc(gated, 1)
                dve.wait_ge(gated, m + 1)
                dve.wait_ge(merged, KD + m)
                nc.vector.tensor_tensor(out=zacc[:, m], in0=zacc[:, m], in1=gconv[:, :], op=ALU.add).then_inc(merged, 1)
                dve.wait_ge(z_hi, m + 1)
                nc.vector.tensor_tensor(out=zlo[:, m], in0=zacc[:, m], in1=zhi[:, m].bitcast(F32), op=ALU.subtract).then_inc(z_lo, 1)

            for half in range(2):
                for i in range(NT):
                    dve.wait_ge(unit_used, U_OUT + 4 * (half + 1))
                    dve.wait_ge(h_landed[0 if i < 4 else 1], 16)
                    hx = h1[:, i, half * HALF:(half + 1) * HALF]
                    nc.vector.tensor_tensor(out=hx, in0=bank[:, (6 * half + i) % 8], in1=hx, op=ALU.add).then_inc(h_ready, 1)
            dve.wait_ge(h_root, 1)
            nc.vector.reciprocal(rstd[:, 0:NT], root[:, 0:NT]).then_inc(h_rstd, 1)
            dve.wait_ge(h_rstd, 1)
            for i in range(NT):
                nc.vector.tensor_scalar(hs1[:, i], h1[:, i], rstd[:, i:i + 1], None, ALU.mult).then_inc(h_scaled, 1)
            for k in range(KD):
                dve.wait_ge(u2hi_ready, k + 1)
                nc.vector.scalar_tensor_tensor(out=u2lo[:, k], in0=psum[:, k % 4, 0:TQ], scalar=vcol("norm_mlp", k),
                                               in1=u2hi[:, k].bitcast(F32), op0=ALU.mult, op1=ALU.subtract).then_inc(u2lo_ready, 1)

            def in_step(i):
                for c in range(4):
                    dve.wait_ge(relu_ready, i * 4 + (c + 1))
                    r = hid[:, ds(i * 4 + c, 1), :]
                    nc.vector.tensor_tensor(out=r, in0=r, in1=r, op=ALU.mult).then_inc(hid_ready, 1)
            rolled(dve, KF // 4, in_step, peel=0)

            def add_ff(half):
                dve.wait_ge(unit_used, U_FF + 16 * (half + 1))
                for i in range(NT):
                    hx = h1[:, i, half * HALF:(half + 1) * HALF]
                    nc.vector.tensor_tensor(out=hx, in0=bank[:, (6 * half + i) % 8], in1=hx, op=ALU.add).then_inc(y_ready, 1)

            for half in range(2):
                def ff_step(i):
                    for c in range(4):
                        if half == 1 and c == 2 and isinstance(i, int):
                            add_ff(0)
                        dve.wait_ge(hidhi_ready, i * 4 + (16 * half + c + 1))
                        nc.vector.tensor_tensor(out=hidlo[:, c % 2], in0=hid[:, ds(i * 8 + 2 * c, 2), :],
                                                in1=hidhi[:, c % 2].bitcast(F32), op=ALU.subtract).then_inc(hidlo_ready, 1)
                rolled(dve, 4, ff_step, peel=half)
            dve.wait_ge(gfinal_landed, 16)
            add_ff(1)
            dve.wait_ge(y_ready, 2 * NT)
            for i in range(NT):
                dve.wait_ge(y_root, i + 1)
                nc.vector.reciprocal(rstd[:, i:i + 1], root[:, i:i + 1]).then_inc(y_rstd, 1)
                dve.wait_ge(y_rstd, i + 1)
                nc.vector.scalar_tensor_tensor(out=yout[:, i], in0=h1[:, i], scalar=rstd[:, i:i + 1], in1=gfinal[:, :],
                                               op0=ALU.mult, op1=ALU.mult).then_inc(y_out, 1)

        @block.gpsimd
        def _(gp):
            gp.memset(tapsrows[:, :], 0.0).then_inc(vec_clear, 1)
            gp.memset(sumsq[:, :], 1.0).then_inc(setup, 1)
            gp.memset(ident[:, :], 0.0).then_inc(setup, 1)
            gp.memset(ones[:, :], 1.0).then_inc(setup, 1)
            gp.memset(eps[:, :], EPS).then_inc(setup, 1)
            gp.memset(tail_mask[:, :], 0.0).then_inc(setup, 1)
            gp.wait_ge(setup, 5)
            gp.affine_select(out=ident[:, :], in_=ident[:, :], compare_op=ALU.not_equal, fill=1.0, base=0,
                             pattern=[[-1, P]], channel_multiplier=1).then_inc(setup, 1)
            gp.affine_select(out=tail_mask[:, :], in_=tail_mask[:, :], compare_op=ALU.is_gt, fill=1.0,
                             base=P - T_META, pattern=[[0, 1]], channel_multiplier=-1).then_inc(setup, 1)
            gp.memset(lnsum[:, :], 0.0).then_inc(lnsum_done, 1)
            lo_unit(gp, 0, 0, 0)
            gp.wait_ge(ut_ready, KD)
            gp.memset(cs[:, :, CS_GAP:CS_META2], 0.0).then_inc(pads_zero, 1)
            gp.memset(cs[:, :, CS_END:CS_END + PAD], 0.0).then_inc(pads_zero, 1)

            for n in range(8):
                lo_unit(gp, 0, 0, n + 1) if n < 3 else lo_unit(gp, 4, 0, n + 1 - 4)
                if n < 6:
                    gp.wait_ge(q_sq, n + 1)
                    w, a = (TQ, 0) if n < 4 else (TK, 1)
                    if n in (0, 4):
                        gp.tensor_scalar(sqacc[:, a, 0:w], sqt[:, n % 2, 0:w], 1.0, 1.0, ALU.mult, ALU.mult).then_inc(sq_sum, 1)
                    else:
                        gp.wait_ge(sq_sum, n)
                        gp.tensor_tensor(out=sqacc[:, a, 0:w], in0=sqacc[:, a, 0:w], in1=sqt[:, n % 2, 0:w], op=ALU.add).then_inc(sq_sum, 1)
            gp.wait_ge(kr_sw, 1)
            gp.wait_ge(tables_landed, 32)
            gp.tensor_tensor(out=krsw[:, :], in0=krsw[:, :], in1=rsin[:, :], op=ALU.mult).then_inc(kr_sin, 1)

            def conv_step(i):
                for c in range(4):
                    lo_unit(gp, U_CONV, i, c + 1)
            rolled(gp, 4, conv_step, peel=0)

            def ln_add(tile):
                gp.wait_ge(conv_done, tile + 1)
                gp.wait_ge(lnsum_done, tile + 1)
                src = cs[:, ds(tile, 1), 0:TQ].rearrange("p a n -> p (a n)") if not isinstance(tile, int) else cs[:, tile, 0:TQ]
                gp.tensor_tensor(out=lnsum[:, :], in0=lnsum[:, :], in1=src, op=ALU.add).then_inc(lnsum_done, 1)

            def gate_step(i):
                for c in range(4):
                    lo_unit(gp, U_GATE, i, c + 1, W_QR if isinstance(i, int) and i == 3 and c == 3 else D)
                    if c == 1 and not (isinstance(i, int) and i == 0):
                        ln_add(i - 1)
            rolled(gp, 4, gate_step, peel=1, last=1)

            def start_pair(n):
                gp.wait_ge(qr_sw, n + 1)
                gp.tensor_tensor(out=qsw[:, 0:T_PROMPT], in0=qsw[:, 0:T_PROMPT], in1=rsin[:, 0:T_PROMPT], op=ALU.mult)
                gp.tensor_tensor(out=qsw[:, T_PROMPT:TQ], in0=qsw[:, T_PROMPT:TQ], in1=rsin[:, SAMP0:TK], op=ALU.mult).then_inc(qr_sin, 1)
                lo_unit(gp, U_ATT, n, 2, W_V)
                lo_unit(gp, U_ATT, n, 3, W_QK)

            def pair_step(p):
                final = isinstance(p, int) and p == PAIRS - 1
                for hh in range(2):
                    for q in range(6):
                        g = p * 12 + (6 * hh + q)
                        n = qtile(q)[0]["nk"]
                        wait_apart(gp, rsum_ready, g + 1)
                        gp.tensor_scalar(prob[:, q % 2, 0:n], prob[:, q % 2, 0:n], rsum[:, q % 4:q % 4 + 1], 1.0,
                                         ALU.mult, ALU.mult).then_inc(p_ready, 1)
                    lo_unit(gp, U_ATT, p, 4 + hh, D if final else (W_QR, W_QK)[hh])
                    if hh == 0:
                        ln_add(p + 3)
                if not final:
                    start_pair(p + 1)
            lo_unit(gp, U_ATT, 0, 1, W_QK)
            start_pair(0)
            rolled(gp, PAIRS, pair_step, peel=1, last=1)

            ln_add(KD - 1)
            lo_unit(gp, U_O, 0, 2)
            lo_unit(gp, U_O, 0, 3)

            def ln_sq_add(js):
                for j in js:
                    gp.wait_ge(ln_sq, j + 1)
                    if j == 0:
                        gp.tensor_scalar(lnacc[:, :], lnsq[:, 0], 1.0, 1.0, ALU.mult, ALU.mult).then_inc(ln_sqsum, 1)
                    else:
                        gp.wait_ge(ln_sqsum, j)
                        gp.tensor_tensor(out=lnacc[:, :], in0=lnacc[:, :], in1=lnsq[:, j % 2], op=ALU.add).then_inc(ln_sqsum, 1)
            lo_unit(gp, U_O, 0, 4)
            ln_sq_add(range(0, 3))
            lo_unit(gp, U_O, 1, 1)
            ln_sq_add(range(3, 6))
            lo_unit(gp, U_O, 1, 2)
            ln_sq_add(range(6, 8))
            lo_unit(gp, U_O, 1, 3)
            for n in range(U_O + KD, U_IN + 1):
                lo_unit(gp, n - n % 4, 0, n % 4)

            def in_step(i):
                for c in range(4):
                    lo_unit(gp, U_IN, i, c + 1)
            rolled(gp, KF // 4, in_step, peel=0)
            with gp.Fori(0, 7) as i:
                for c in range(4):
                    lo_unit(gp, U_FF, i, c + 1)
            for c in range(3):
                lo_unit(gp, U_FF, 7, c + 1)

        @block.tensor
        def _(pe):
            pe.wait_ge(setup, 7)
            pe.wait_ge(consts_landed, 16 * len(VEC))
            nc.tensor.transpose(psum[:, 0, 0:NVEC], vecrows[0:NVEC, :], ident[0:NVEC, 0:NVEC]).then_inc(vec_t, 1)
            pe.wait_ge(taps_landed, 16)
            for k in range(KD):
                mm = nc.tensor.transpose(psum[:, 1, k * 32:(k + 1) * 32], tapsrows[:, k * P:(k + 1) * P], ident[0:32, 0:32])
            mm.then_inc(vec_t, 1)
            pe.wait_ge(vec_ready, 2)

            pe.wait_ge(x_scaled, 7)
            COLS = [0, 128, 256, 384, SAMP0, SAMP0 + 128, META0]
            for k in range(KD):
                wait(pe, ulo_ready, k - 3)
                for i in range(7):
                    r = T_META if i == 6 else P
                    mm = nc.tensor.transpose(psum[:, k % 4, COLS[i]:COLS[i] + r], xt[0:r, i, k * P:(k + 1) * P], ident[0:r, 0:r])
                mm.then_inc(ut_ready, 1)

            u = (uhi, ulo)

            def unit(base, i, c, pair, rhs, segments, k_tiles=range(KD), first=True, last=True, rhs_ready=None):
                pe.wait_ge(lo_ready, i * 4 + (base + c + 1))
                wh, wl = weights(c % 2, len(k_tiles))
                for j, k in enumerate(k_tiles):
                    if rhs_ready is not None:
                        rhs_ready(k)
                    mm = products(psum[:, pair], (wh[:, j], wl[:, j]), rhs, k, segments,
                                  first and j == 0, last and j == len(k_tiles) - 1)
                mm.then_inc(unit_used, 1)

            for n in range(6):
                wait(pe, raw_q, n - 1)
                unit(4 * (n // 4), 0, n % 4, n % 2, u, QSEG if n < 4 else KSEG,
                     rhs_ready=(lambda k: pe.wait_ge(ulo_ready, max(k + 1, 5))) if n == 0 else
                     ((lambda k: pe.wait_ge(ulo_ready, KD)) if n == 1 else None))
            for e in range(2):
                unit(4, 0, 2 + e, 2, u, KSEG, k_tiles=range(4 * e, 4 * e + 4), first=e == 0, last=e == 1)
                if e == 0:
                    sum_squares(pe, 0, TQ, 4)
            pe.wait_ge(raw_q, 6)

            def conv_step(i):
                for c in range(4):
                    if c % 2 == 0:
                        wait(pe, sg_ready, i * 2 + c // 2)
                    else:
                        wait(pe, glu_ready, i * 2 + c // 2)
                    unit(U_CONV, i, c, c % 2, u, KSEG)
                    if isinstance(i, int) and i == 0 and c == 0:
                        pe.wait_ge(ss_root, 1)
                        sum_squares(pe, 1, TK, 6)
            rolled(pe, 4, conv_step, peel=1)

            def gate_step(i):
                for c in range(4):
                    if isinstance(i, int) and i == 0 and c < 2:
                        pe.wait_ge(sg_ready if c == 0 else glu_ready, KD)
                    wait(pe, gate_ready, i * 4 + (c - 1))
                    unit(U_GATE, i, c, c % 2, u, QSEG)
            rolled(pe, 4, gate_step, peel=1)

            pe.wait_ge(qkv_lo, KQ + KKV)
            pe.wait_ge(kr_lo, 1)
            pe.wait_ge(kr_rot, 1)

            def values(p, js):
                pe.wait_ge(lo_ready, p * 4 + (U_ATT + 3))
                wh, wl = weights(0, KKV, 2 * VD)
                for j in js:
                    out = bank[:, 4 + j // 2, (j % 2) * 2 * VD:(j % 2 + 1) * 2 * VD]
                    if j == 0:
                        wait(pe, pt_lo, p * 12)
                    if j == 4:
                        wait(pe, tail_lo, p * 4)
                    if j == 6:
                        wait(pe, o_ready, p * 6)
                    for k in range(KKV):
                        for step, (a, b) in enumerate(((kvhi, wh), (kvlo, wh), (kvhi, wl))):
                            mm = nc.tensor.matmul(out, a[:, k, VTILES[j]:VTILES[j] + P], b[:, k, :],
                                                  start=k == 0 and step == 0, stop=k == KKV - 1 and step == 2)
                mm.then_inc(v_mm if js[0] == 0 else unit_used, 1)

            def rotary_queries(p):
                unit(U_ATT, p, 0, 0, (qhi, qlo), ZSEG, k_tiles=range(KQ))

            def queries(p, hh, pair):
                pe.wait_ge(lo_ready, p * 4 + (U_ATT + 2 + 2 * hh))
                wh, wl = weights(1, KQ + KKV)
                for k in range(KQ):
                    mm = products(psum[:, pair], (wh[:, k], wl[:, k]), (qhi, qlo), k, ZSEG, k == 0, k == KQ - 1)
                mm.then_inc(qn_mm, 1)

            def keys(hh, pair):
                wh, wl = weights(1, KQ + KKV)
                for k in range(KKV):
                    mm = products(psum[:, pair], (wh[:, KQ + k], wl[:, KQ + k]), (kvhi, kvlo), k, KSEG, k == 0, k == KKV - 1)
                mm.then_inc(unit_used, 1)

            def S(p, hh, q):
                g = p * 12 + (6 * hh + q)
                grp, c0 = qtile(q)
                wait(pe, exp_ready, g - 1)
                ops = [(qnhi, knhi), (qnhi, knlo), (qnlo, knhi), (qrs[hh], kra), (qrs[hh], krb)]
                for step, (a, b) in enumerate(ops):
                    for e, (k0, n) in enumerate(grp["pieces"]):
                        mm = nc.tensor.matmul(psum[:, q % 2, e * HALF:e * HALF + n], a[:, c0:c0 + P],
                                              b[:, grp["k0"] + k0:grp["k0"] + k0 + n],
                                              start=step == 0, stop=step == len(ops) - 1)
                mm.then_inc(s_ready, 1)

            def T(p, hh, q):
                g = p * 12 + (6 * hh + q)
                pe.wait_ge(p_ready, g + 1)
                wait(pe, pt_lo, g - 1)
                if hh == 0 and q == 0:
                    pe.wait_ge(v_lo, p * 3 + 3)
                for e, (_, k0) in enumerate(qtile(q)[0]["tiles"]):
                    if e == TAIL:
                        if q % 2 == 0:
                            wait(pe, tail_lo, p * 4 + (2 * hh + q // 2))
                        out = bank[:, 6, (q % 2) * P:(q % 2 + 1) * P]
                    else:
                        out = bank[:, 4 + q % 2, e * P:(e + 1) * P]
                    mm = nc.tensor.transpose(out, prob[:, q % 2, k0:k0 + P], ident[:, :])
                mm.then_inc(pt_mm, 1)

            def A(p, hh, b):
                blk = 3 * hh + b
                pe.wait_ge(pt_lo, p * 12 + (6 * hh + 2 * b + 2))
                wait(pe, o_ready, p * 6 + blk)
                tiles = qtile(2 * b)[0]["tiles"]
                for e, (vt, _) in enumerate(tiles):
                    for step, (a, r) in enumerate(((vhi, pthi), (vhi, ptlo), (vlo, pthi))):
                        mm = nc.tensor.matmul(bank[:, 7, 0:2 * P], a[:, vt, hh * VD:(hh + 1) * VD], r[:, blk % 2, e, :],
                                              start=e == 0 and step == 0, stop=e == len(tiles) - 1 and step == 2)
                mm.then_inc(av_mm, 1)

            def pair_step(p):
                final = isinstance(p, int) and p == PAIRS - 1
                pe.wait_ge(qr_lo, p + 1)
                for hh in range(2):
                    pe.wait_ge(qn_lo, p * 2 + (hh + 1))
                    pe.wait_ge(kn_lo, p * 2 + (hh + 1))
                    S(p, hh, 0), S(p, hh, 1)
                    values(p, range(4, 8)) if hh == 0 else A(p, 0, 2)
                    S(p, hh, 2), T(p, hh, 0), S(p, hh, 3), T(p, hh, 1), S(p, hh, 4), T(p, hh, 2), S(p, hh, 5)
                    A(p, hh, 0), T(p, hh, 3), T(p, hh, 4)
                    done = p * 12 + 6 * hh
                    if hh == 0:
                        pe.wait_ge(exp_ready, done + 5)
                        queries(p, 1, 0)
                        T(p, hh, 5)
                        pe.wait_ge(exp_ready, done + 6)
                        keys(1, 1)
                        A(p, hh, 1)
                    elif not final:
                        pe.wait_ge(exp_ready, done + 5)
                        rotary_queries(p + 1)
                        T(p, hh, 5)
                        pe.wait_ge(exp_ready, done + 6)
                        queries(p + 1, 0, 1)
                        A(p, hh, 1)
                        pe.wait_ge(qr_cos, p + 2)
                        keys(0, 0)
                        A(p, hh, 2)
                        values(p + 1, range(4))
                    else:
                        A(p, hh, 1), T(p, hh, 5), A(p, hh, 2)
            pe.wait_ge(gate_ready, 2 * KD - 1)
            rotary_queries(0)
            pe.wait_ge(gate_ready, 2 * KD)
            queries(0, 0, 1)
            values(0, range(4))
            pe.wait_ge(qr_cos, 1)
            keys(0, 0)
            rolled(pe, PAIRS, pair_step, peel=1, last=1)

            pe.wait_ge(o_ready, 3 * HEADS)
            o = (ohi, olo)
            for m in range(KD):
                wait(pe, merged, m - 1)
                unit(U_O, m // 4, m % 4, m % 2, o, ZSEG,
                     rhs_ready=(lambda k: pe.wait_ge(o_lo, k + 1)) if m == 0 else None)
                if m == 1:
                    pe.wait_ge(lnsum_done, KD + 1)
                    for c0, n in ((0, HALF), (HALF, TQ - HALF)):
                        mm = nc.tensor.matmul(psum[:, 2, c0:c0 + n], ones[:, :], lnsum[:, c0:c0 + n], start=True, stop=True)
                    mm.then_inc(mean_mm, 1)
                if m == 5:
                    pe.wait_ge(ln_sqsum, KD)
                    for c0, n in ((0, HALF), (HALF, TQ - HALF)):
                        mm = nc.tensor.matmul(psum[:, 3, c0:c0 + n], ones[:, :], lnacc[:, c0:c0 + n], start=True, stop=True)
                    mm.then_inc(var_mm, 1)
            for m in range(KD):
                pe.wait_ge(merged, KD + m - 1)
                unit(U_CO, m // 4, m % 4, m % 2, (chi, clo), ZSEG,
                     rhs_ready=(lambda k: pe.wait_ge(c_lo, k + 1)) if m == 0 else None)

            def token_major(base, half, i, units, n_k, lhs, lhs_ready, free):
                for c in range(4):
                    pe.wait_ge(lo_ready, i * 4 + (base + c + 1))
                    wh, wl = weights(c % 2, 2, HALF)
                    lhs_ready(i, c)
                    for kk in range(2):
                        for tt in range(NT):
                            first = isinstance(i, int) and i == 0 and c == 0 and kk == 0
                            last = isinstance(i, int) and i == units // 4 - 1 and c == 3 and kk == 1
                            if first:
                                free(tt)
                            out = bank[:, (6 * half + tt) % 8]
                            a_hi, a_lo = lhs(i, c, kk, tt)
                            for step, (a, b) in enumerate(((a_hi, wh), (a_hi, wl), (a_lo, wh))):
                                mm = nc.tensor.matmul(out, a, b[:, kk, :], start=first and step == 0, stop=last and step == 2)
                    mm.then_inc(unit_used, 1)

            pe.wait_ge(merged, 2 * KD)
            for half in range(2):
                token_major(U_OUT + 4 * half, half, 0, 4, KD,
                            lambda i, c, kk, tt: (zhi[:, 2 * c + kk, tt * P:(tt + 1) * P], zlo[:, 2 * c + kk, tt * P:(tt + 1) * P]),
                            (lambda i, c: pe.wait_ge(z_lo, 2 * c + 2)) if half == 0 else (lambda i, c: None),
                            (lambda tt: None) if half == 0 else (lambda tt: wait(pe, h_ready, tt - 1)))

            pe.wait_ge(h_ready, 2 * NT)
            pe.wait_ge(h_scaled, NT)
            for k in range(KD):
                wait(pe, u2lo_ready, k - 3)
                for i in range(NT):
                    mm = nc.tensor.transpose(psum[:, k % 4, i * P:(i + 1) * P], hs1[:, i, k * P:(k + 1) * P], ident[:, :])
                mm.then_inc(u2t_ready, 1)

            def in_step(i):
                for c in range(4):
                    if isinstance(i, int) and i == 0:
                        pe.wait_ge(u2lo_ready, KD)
                    wait(pe, relu_ready, i * 4 + (c - 1))
                    unit(U_IN, i, c, c % 2, (u2hi, u2lo), ZSEG)
            rolled(pe, KF // 4, in_step, peel=1)

            pe.wait_ge(relu_ready, KF)
            for half in range(2):
                rolled(pe, 4, lambda i: token_major(
                    U_FF + 16 * half, half, i, 16, KF,
                    lambda i, c, kk, tt: (hidhi[:, c % 2, kk, tt * P:(tt + 1) * P], hidlo[:, c % 2, kk, tt * P:(tt + 1) * P]),
                    lambda i, c: pe.wait_ge(hidlo_ready, i * 4 + (16 * half + c + 1)),
                    (lambda tt: None) if half == 0 else (lambda tt: wait(pe, y_ready, tt - 1))), peel=1, last=1)


_INS = ["x_prompt", "x_sample", "meta_tokens", "norm_mix", "w_in", "b_gate", "norm_q", "w_uq", "norm_kv", "w_ukv",
        "w_o_attn", "conv_w", "conv_b", "conv_ln_g", "conv_ln_b", "w_conv_out", "w_out", "norm_mlp", "w_mlp_in",
        "w_mlp_out", "norm_final"]
_OUTS = [("y_prompt", (1, T_PROMPT, D)), ("y_sample", (1, T_SAMPLE, D))]


def rope_tables():
    pos = np.concatenate([T_META + np.arange(T_PROMPT), np.arange(T_META), T_META + np.arange(T_SAMPLE)]).astype(np.float32)
    inv = np.float32(10000.0) ** (-np.arange(0, ROPE, 2, dtype=np.float32) / np.float32(ROPE))
    ang = (inv[:, None] * pos[None, :]).astype(np.float32)
    c, s = np.cos(ang), np.sin(ang)
    return (np.ascontiguousarray(np.concatenate([c, c, c, c]), np.float32),
            np.ascontiguousarray(np.concatenate([-s, s, -s, s]), np.float32))


def kernel(**inputs):
    import concourse.bacc as _bacc
    from concourse.bass_utils import run_bass_kernel_spmd as _run

    nc = _bacc.Bacc("TRN2", target_bir_lowering=False, num_devices=1)
    arrays, t = {}, {}
    for name in _INS:
        a = np.ascontiguousarray(inputs[name])
        arrays[f"in_{name}"] = a
        t[name] = nc.dram_tensor(f"in_{name}", a.shape, F32, kind="ExternalInput").ap()
    for name, a in zip(("rope_cos", "rope_sin"), rope_tables()):
        arrays[name] = a
        t[name] = nc.dram_tensor(name, a.shape, F32, kind="ExternalInput").ap()
    for name, shape in _OUTS:
        t[name] = nc.dram_tensor(f"out_{name}", shape, F32, kind="ExternalOutput").ap()
    build(nc, t)
    r = _run(nc, [arrays], core_ids=[0])
    return tuple(r.results[0][f"out_{name}"] for name, _ in _OUTS)
```

```python
from contextlib import ExitStack

import numpy as np
import concourse.bass as bass
from concourse import mybir

F32 = mybir.dt.float32
F32R = mybir.dt.float32r
ALU = mybir.AluOpType
ACT = mybir.ActivationFunctionType
AX = mybir.AxisListType
ds = bass.ds

P = 128
D = 1024
KD = D // P
T_PROMPT, T_SAMPLE, T_META = 512, 256, 16
META0 = T_PROMPT
SAMP0 = T_PROMPT + T_META
TK = T_PROMPT + T_META + T_SAMPLE
TQ = T_PROMPT + T_SAMPLE
NT = TQ // P
HEADS, NOPE, ROPE, VD = 8, 128, 64, 128
PAIRS = HEADS // 2
Q_LORA, KV_LORA = 512, 256
KQ, KKV = Q_LORA // P, KV_LORA // P
TAPS, PAD = 31, 15
FF = 4 * D
KF = FF // P
EPS = 1e-6
SCALE = float((NOPE + ROPE) ** -0.5)
HALF = 512

C_Q, C_KV = 0, Q_LORA
C_KR = C_KV + KV_LORA
C_A = C_KR + ROPE
C_B = C_A + D
C_GATE = C_B + D

U_QKV = 0
U_CONV = 8
U_GATE = U_CONV + 2 * KD
U_ATT = U_GATE + 2 * KD
U_O = U_ATT + 4 * PAIRS
U_CO = U_O + KD
U_OUT = U_CO + KD
U_IN = U_OUT + KD
U_FF = U_IN + KF
U_END = U_FF + KF

VEC = {}
for _name, _rows in (("norm_mix", KD), ("norm_q", KQ), ("norm_kv", KKV), ("b_gate", 2 * KD),
                     ("conv_b", KD), ("conv_ln_g", KD), ("conv_ln_b", KD), ("norm_mlp", KD)):
    VEC[_name] = (sum(r for _, r in VEC.values()), _rows)
NVEC = sum(r for _, r in VEC.values())

CS_PROMPT = T_META
CS_GAP = CS_PROMPT + T_PROMPT
CS_META2 = CS_GAP + PAD
CS_SAMPLE = CS_META2 + T_META
CS_END = CS_SAMPLE + T_SAMPLE
CS_ALL = 832
SPAN = CS_END - CS_PROMPT
ACC_SAMPLE = CS_SAMPLE - CS_PROMPT

X_ORDER = (6, 0, 1, 2, 3, 4, 5)

VTILES = [0, 128, 256, 384, SAMP0, SAMP0 + P]
PACK = (slice(0, T_META), slice(32, 32 + T_META), slice(64, 64 + T_META))
GROUPS = [
    dict(k0=0, nk=SAMP0, pieces=((0, SAMP0 // 2), (SAMP0 // 2, SAMP0 // 2)),
         tiles=((0, 0), (1, 128), (2, 256), (3, 384)), meta=T_PROMPT),
    dict(k0=META0, nk=TK - META0, pieces=((0, TK - META0),), tiles=((4, T_META), (5, T_META + P)), meta=0),
]

W_QR, W_QK, W_V = KQ * P, (KQ + KKV) * P, KKV * 2 * VD
EARLY_HEADS = 4
PAIR_TAPS = 8
FIRST_TAPS = 1

SB0 = 16512
Z0 = SB0 + 36352


def build(nc, t):
    with ExitStack() as ctx:
        def at(name, shape, dt, offset):
            return nc.alloc_sbuf_tensor_at(name, shape, dt, offset=offset)

        def sem(name):
            return ctx.enter_context(nc.semaphore(name))

        psum = ctx.enter_context(nc.psum_tensor("psum", [P, 4, 2 * HALF], F32))
        bank = psum[:].rearrange("p a (b n) -> p (a b) n", n=HALF)

        ident = at("ident", [P, P], F32, SB0)
        ones = at("ones", [P, P], F32, SB0 + 512)
        vec = at("vec", [P, NVEC], F32, SB0 + 1024)
        convw = at("convw", [P, KD, TAPS], F32, SB0 + 1280)
        eps = at("eps", [P, 1], F32, SB0 + 2272)
        sumsq = at("sumsq", [P, 8], F32, SB0 + 2336)
        root = at("root", [P, 8], F32, SB0 + 2368)
        rstd = at("rstd", [P, 8], F32, SB0 + 2400)
        negmax = at("negmax", [P, 4], F32, SB0 + 2432)
        psumexp = at("psumexp", [P, 4], F32, SB0 + 2464)
        rsum = at("rsum", [P, 4], F32, SB0 + 2496)
        halfsq = at("halfsq", [P, 2, 8], F32, SB0 + 2528)
        meansq = at("meansq", [P, 8], F32, SB0 + 2592)
        raw = at("raw", [P, 4, D], F32, SB0 + 3584)
        whi = at("whi", [P, 2, D], F32R, SB0 + 3584 + 16384)
        wlo = at("wlo", [P, 2, D], F32R, SB0 + 3584 + 24576)

        cs = at("cs", [P, KD, CS_ALL], F32, Z0)
        acc = at("acc", [P, 2, 800], F32, Z0 + 26624)
        lnsum = at("lnsum", [P, TQ], F32, Z0 + 33024)
        qhi = at("qhi", [P, KQ, TQ], F32R, Z0 + 36096)
        qlo = at("qlo", [P, KQ, TQ], F32R, Z0 + 48384)
        kvhi = at("kvhi", [P, KKV, TK], F32R, Z0 + 60672)
        kvlo = at("kvlo", [P, KKV, TK], F32R, Z0 + 66944)
        kra = at("kra", [P, TK], F32R, Z0 + 73216)
        krb = at("krb", [P, TK], F32R, Z0 + 76352)
        rcos = at("rcos", [P, TK], F32, Z0 + 79488)
        rsin = at("rsin", [P, TK], F32, Z0 + 82624)
        V0 = Z0 + 85760
        xt = at("xt", [P, 7, D], F32, Z0)
        vecrows = at("vecrows", [P, P], F32, V0 + 50176)
        tapsrows = at("tapsrows", [32, D], F32, V0 + 50176 + 512)
        junk0 = at("junk0", [P, D], F32, V0 + 50176 + 4608)
        uhi = at("uhi", [P, KD, TK], F32R, V0)
        ulo = at("ulo", [P, KD, TK], F32R, V0 + 25088)
        qraw = at("qraw", [P, KQ, TQ], F32, V0 + 50176)
        kvraw = at("kvraw", [P, KKV, TK], F32, V0 + 62464)
        sqacc = at("sqacc", [P, 2, TK], F32, V0 + 68736)
        sqt = at("sqt", [P, 2, TK], F32, V0 + 75008)
        krsw = at("krsw", [P, TK], F32, V0 + 81280)
        krt = at("krt", [P, TK], F32, V0 + 84416)
        sg = at("sg", [P, 2, TK], F32, V0 + 75008)
        gout = at("gout", [P, 2, TQ], F32, V0 + 62464)
        qnhi = at("qnhi", [P, TQ], F32R, V0)
        qnlo = at("qnlo", [P, TQ], F32R, V0 + 3072)
        knhi = at("knhi", [P, TK], F32R, V0 + 6144)
        knlo = at("knlo", [P, TK], F32R, V0 + 9280)
        qrs = [at(f"qrs{e}", [P, TQ], F32R, V0 + 12416 + 3072 * e) for e in range(2)]
        qsw = at("qsw", [P, TQ], F32, V0 + 18560)
        qt = at("qt", [P, TQ], F32, V0 + 21632)
        vhi = at("vhi", [P, 6, 2 * VD], F32R, V0 + 24704)
        vlo = at("vlo", [P, 6, 2 * VD], F32R, V0 + 32896)
        vmeta = at("vmeta", [P, 2 * VD], F32R, V0 + 39040)
        prob = at("prob", [P, 2, SAMP0], F32, V0 + 41088)
        pthi = at("pthi", [P, 2, 4, 2 * P], F32R, V0 + 45312)
        ptmeta = at("ptmeta", [P, 2, 2 * P], F32R, V0 + 53504)
        ptlo = at("ptlo", [P, 2, 4, 2 * P], F32R, V0 + 55552)
        oraw = at("oraw", [P, HEADS, TQ], F32, V0 + 65792)
        ohi = at("ohi", [P, KD, TQ], F32R, Z0 + 36096)
        olo = at("olo", [P, KD, TQ], F32R, Z0 + 60672)
        gin = at("gin", [P, 2, TQ], F32, Z0 + 26624)
        zacc = at("zacc", [P, KD, TQ], F32, Z0 + 85760)
        chi = at("chi", [P, KD, TQ], F32R, Z0 + 110336)
        clo = at("clo", [P, KD, TQ], F32R, Z0 + 151552)
        mu = at("mu", [P, TQ], F32, Z0 + 134912)
        lnr = at("lnr", [P, TQ], F32, Z0 + 137984)
        lnsq = at("lnsq", [P, 2, TQ], F32, Z0 + 141056)
        lnacc = at("lnacc", [P, TQ], F32, Z0 + 147200)
        gconv = at("gconv", [P, TQ], F32, Z0 + 134912)
        zhi = at("zhi", [P, KD, TQ], F32R, Z0 + 36096)
        zlo = at("zlo", [P, KD, TQ], F32R, Z0 + 60672)
        h1 = at("h1", [P, NT, D], F32, Z0)
        junk1 = at("junk1", [P, HALF], F32, Z0 + 110336)
        diag = at("diag", [P, NT, P], F32, Z0 + 119808)
        rbc = at("rbc", [P, TQ], F32, Z0 + 172032)
        hid = at("hid", [P, KF, TQ], F32, Z0 + 24576)
        u2hi = at("u2hi", [P, KD, TQ], F32R, Z0 + 122880)
        u2lo = at("u2lo", [P, KD, TQ], F32R, Z0 + 147456)
        hidhi = [at(f"hidhi{e}", [P, 2, TQ], F32R, Z0 + 122880 + 12288 * e) for e in range(2)]
        hidlo = [at(f"hidlo{e}", [P, 2, TQ], F32R, Z0 + 129024 + 12288 * e) for e in range(2)]
        yout = at("yout", [P, NT, D], F32, Z0 + 147456)
        gfinal = at("gfinal", [P, D], F32, Z0 + 172032)
        junk2 = at("junk2", [P, HALF], F32, Z0 + 24576)

        gates = nc.dram_tensor("gates", [2 * KD, P, TQ], F32, kind="Internal").ap()

        raw_landed = [sem(f"raw_landed{s}") for s in range(4)]
        hi_ready, lo_ready, unit_used = sem("hi_ready"), sem("lo_ready"), sem("unit_used")
        dup_landed = [sem(f"dup_landed{e}") for e in range(2)]
        kw_landed = [sem(f"kw_landed{e}") for e in range(2)]
        x_landed = [sem(f"x_landed{i}") for i in range(7)]
        consts_landed, taps_landed, tables_landed = sem("consts_landed"), sem("taps_landed"), sem("tables_landed")
        setup, vec_clear, vec_t, vec_ready = sem("setup"), sem("vec_clear"), sem("vec_t"), sem("vec_ready")
        x_sq, x_root, x_rstd, x_scaled = sem("x_sq"), sem("x_root"), sem("x_rstd"), sem("x_scaled")
        ut_ready, uhi_ready, ulo_ready = sem("ut_ready"), sem("uhi_ready"), sem("ulo_ready")
        raw_q, q_sq, sq_sum = sem("raw_q"), sem("q_sq"), sem("sq_sum")
        ss_mm, ss_root, ss_rstd = sem("ss_mm"), sem("ss_root"), sem("ss_rstd")
        qkv_scaled, qkv_hi, qkv_lo = sem("qkv_scaled"), sem("qkv_hi"), sem("qkv_lo")
        kr_sw, kr_cos, kr_sin, kr_rot, kr_hi, kr_lo = (sem("kr_sw"), sem("kr_cos"), sem("kr_sin"),
                                                       sem("kr_rot"), sem("kr_hi"), sem("kr_lo"))
        pads_zero, sg_ready, glu_ready = sem("pads_zero"), sem("sg_ready"), sem("glu_ready")
        tap_done, conv_done, lnsum_done = sem("tap_done"), sem("conv_done"), sem("lnsum_done")
        gate_ready = sem("gate_ready")
        gate_stored = [sem(f"gate_stored{e}") for e in range(2)]
        v_mm, v_hi, v_lo = sem("v_mm"), sem("v_hi"), sem("v_lo")
        qr_sw, qr_cos, qr_sin, qr_rot, qr_hi, qr_lo = (sem("qr_sw"), sem("qr_cos"), sem("qr_sin"),
                                                       sem("qr_rot"), sem("qr_hi"), sem("qr_lo"))
        qn_mm, qn_hi, qn_lo, kn_hi, kn_lo = sem("qn_mm"), sem("qn_hi"), sem("qn_lo"), sem("kn_hi"), sem("kn_lo")
        s_ready, max_ready, exp_ready, rsum_ready, p_ready = (sem("s_ready"), sem("max_ready"),
                                                              sem("exp_ready"), sem("rsum_ready"), sem("p_ready"))
        tail_hi, tail_hi_again, tail_lo = sem("tail_hi"), sem("tail_hi_again"), sem("tail_lo")
        packs_zero = sem("packs_zero")
        pt_mm, pt_hi, pt_lo, av_mm, o_ready = sem("pt_mm"), sem("pt_hi"), sem("pt_lo"), sem("av_mm"), sem("o_ready")
        o_hi, o_lo = sem("o_hi"), sem("o_lo")
        gin_landed = [sem(f"gin_landed{e}") for e in range(2)]
        mean_mm, mu_ready, centred, ln_sq, ln_sqsum = (sem("mean_mm"), sem("mu_ready"), sem("centred"),
                                                       sem("ln_sq"), sem("ln_sqsum"))
        var_mm, ln_root, ln_rstd, ln_scaled, c_silu, c_hi, c_lo = (
            sem("var_mm"), sem("ln_root"), sem("ln_rstd"), sem("ln_scaled"), sem("c_silu"), sem("c_hi"), sem("c_lo"))
        merged, gated, z_hi, z_lo = sem("merged"), sem("gated"), sem("z_hi"), sem("z_lo")
        h_landed, h_ready = [sem(f"h_landed{i}") for i in range(2)], sem("h_ready")
        h_sq, h_ms, h_root, h_rstd, diag_ready = sem("h_sq"), sem("h_ms"), sem("h_root"), sem("h_rstd"), sem("diag_ready")
        rbc_mm, rbc_ready = sem("rbc_mm"), sem("rbc_ready")
        out_tile, y_tile, u2_half_used = sem("out_tile"), sem("y_tile"), sem("u2_half_used")
        y_gain, y_ms, y_left = sem("y_gain"), sem("y_ms"), sem("y_left")
        u2t_ready, u2hi_ready, u2lo_ready = sem("u2t_ready"), sem("u2hi_ready"), sem("u2lo_ready")
        relu_ready, hid_ready = sem("relu_ready"), sem("hid_ready")
        hidhi_ready, hidlo_ready = sem("hidhi_ready"), sem("hidlo_ready")
        gfinal_landed, y_ready, y_sq, y_root, y_rstd, y_out, y_stored = (
            sem("gfinal_landed"), sem("y_ready"), sem("y_sq"), sem("y_root"), sem("y_rstd"), sem("y_out"), sem("y_stored"))

        waits_apart = sem("waits_apart")

        def wait(eng, s, value):
            if not isinstance(value, int) or value > 0:
                eng.wait_ge(s, value)

        def wait_apart(eng, s, value):
            wait(eng, s, value)
            if not isinstance(value, int):
                eng.sem_inc(waits_apart, 1)

        def rolled(eng, count, body, peel=1, last=0):
            for i in range(peel):
                body(i)
            if count - peel - last > 0:
                with eng.Fori(peel, count - last) as i:
                    body(i)
            for i in range(count - last, count):
                body(i)

        def hi_unit(act, base, i, c, w=D):
            act.wait_ge(raw_landed[c % 4], (i + (base // 4 + c // 4 + 1)) * 16)
            wait(act, unit_used, i * 4 + (base + c - 1))
            nc.scalar.activation(whi[:, c % 2, 0:w], raw[:, c % 4, 0:w], ACT.Copy).then_inc(hi_ready, 1)

        def lo_unit(gp, base, i, c, w=D):
            gp.wait_ge(hi_ready, i * 4 + (base + c + 1))
            gp.tensor_tensor(out=wlo[:, c % 2, 0:w], in0=raw[:, c % 4, 0:w], in1=whi[:, c % 2, 0:w].bitcast(F32),
                             op=ALU.subtract).then_inc(lo_ready, 1)

        def weights(s, k, m=P):
            return (whi[:, s, 0:k * m].rearrange("p (k m) -> p k m", k=k),
                    wlo[:, s, 0:k * m].rearrange("p (k m) -> p k m", k=k))

        def products(out, lhs, rhs, k, segments, first, last):
            (lh, ll), (rh, rl) = lhs, rhs
            mm = None
            for step, (a, b) in enumerate(((lh, rh), (lh, rl), (ll, rh))):
                for o0, c0, n in segments:
                    mm = nc.tensor.matmul(out[:, o0:o0 + n], a, b[:, k, c0:c0 + n],
                                          start=first and step == 0, stop=last and step == 2)
            return mm

        KSEG = ((0, 0, HALF), (HALF, HALF, TK - HALF))
        QSEG = ((0, 0, T_PROMPT), (T_PROMPT, SAMP0, T_SAMPLE))
        ZSEG = ((0, 0, HALF), (HALF, HALF, TQ - HALF))

        def vcol(name, k):
            r = VEC[name][0]
            return vec[:, ds(k + r, 1)] if not isinstance(k, int) else vec[:, r + k:r + k + 1]

        def qtile(q):
            return (GROUPS[0] if q < 4 else GROUPS[1]), q * P

        def u_part(k, seg):
            if seg == 0:
                return bank[:, k, 0:T_PROMPT], slice(0, T_PROMPT)
            return bank[:, 4 + k % 4, 0:TK - T_PROMPT], slice(T_PROMPT, TK)

        U2_PAIR = (0, 0, 0, 0, 1, 2, 3, 1)

        def main_tiles(q):
            return len(qtile(q)[0]["tiles"])

        def sum_squares(pe, a, w, count):
            pe.wait_ge(sq_sum, count)
            for c0, n in ((0, HALF), (HALF, w - HALF)):
                mm = nc.tensor.matmul(psum[:, 3, c0:c0 + n], ones[:, :], sqacc[:, a, c0:c0 + n], start=True, stop=True)
            mm.then_inc(ss_mm, 1)

        block = ctx.enter_context(nc.Block())

        @block.sync
        def _(sp):
            xs = [t["x_prompt"][0, i * P:(i + 1) * P, :] for i in range(4)]
            xs += [t["x_sample"][0, i * P:(i + 1) * P, :] for i in range(2)]
            win = t["w_in"][0].rearrange("(k p) n -> p k n", p=P)

            def columns(w, base, i, c, col):
                wait_apart(sp, lo_ready, i * 4 + (base + c - 3))
                sp.dma_start(raw[:, c].rearrange("p (k m) -> p k m", k=KD), w[:, :, col]) \
                  .then_inc(raw_landed[c], 16)

            def load_x(i):
                if i == 6:
                    sp.dma_start(xt[0:T_META, 6], t["meta_tokens"]).then_inc(x_landed[6], 16)
                else:
                    sp.dma_start(xt[:, i], xs[i]).then_inc(x_landed[i], 16)
            for i in X_ORDER[:4]:
                load_x(i)
            columns(win, 0, 0, 0, slice(0, P))
            sp.wait_ge(vec_clear, 1)
            for name, (r, n) in VEC.items():
                sp.dma_start(vecrows[r:r + n, :], t[name][0].rearrange("(k p) -> k p", p=P)).then_inc(consts_landed, 16)
            sp.dma_start(tapsrows[0:TAPS, :], t["conv_w"][0]).then_inc(taps_landed, 16)
            for i in X_ORDER[4:]:
                load_x(i)

            for n in range(1, 6):
                columns(win, 4 * (n // 4), 0, n % 4, slice(n * P, (n + 1) * P))
            sp.dma_start(rcos[:, :], t["rope_cos"]).then_inc(tables_landed, 16)
            sp.dma_start(rsin[:, :], t["rope_sin"]).then_inc(tables_landed, 16)
            for e in range(2):
                sp.wait_ge(lo_ready, 6 + e - 3)
                r = raw[:, 2 + e, 0:4 * P].rearrange("p (k m) -> p k m", k=4)
                w = win[:, 4 * e:4 * e + 4, C_KR:C_KR + ROPE]
                sp.dma_start(r[:, :, 0:ROPE], w).then_inc(raw_landed[2 + e], 16)
                sp.dma_start(r[:, :, ROPE:P], w).then_inc(dup_landed[e], 16)

            def conv_units(i):
                for c in range(4):
                    first = C_B if c % 2 == 0 else C_A
                    columns(win, U_CONV, i, c, ds(i * (2 * P) + (first + (c // 2) * P), P))
            rolled(sp, 4, conv_units, peel=0)

            def gate_units(i):
                for c in range(4):
                    columns(win, U_GATE, i, c, ds(i * (4 * P) + (C_GATE + c * P), P))
            rolled(sp, 4, gate_units, peel=0)

            uq = t["w_uq"][0].rearrange("(k p) (a h e) -> p k a h e", p=P, h=2, e=NOPE + ROPE)
            ukv = t["w_ukv"][0].rearrange("(k p) (a h v d) -> p k a h v d", p=P, h=2, v=2, d=VD)

            def pair_units(i):
                def head_halves(c, wait_value, dst, src, second):
                    wait_apart(sp, lo_ready, wait_value)
                    for h in range(2):
                        sp.dma_start(dst[:, :, h], src(h)).then_inc(raw_landed[c] if h == 0 else second, 16)

                def queries_keys(c, h, wait_value):
                    wait_apart(sp, lo_ready, wait_value)
                    sp.dma_start(raw[:, c, 0:KQ * P].rearrange("p (k m) -> p k m", k=KQ),
                                 uq[:, :, ds(i, 1), h, 0:NOPE].rearrange("p k a e -> p k (a e)")) \
                      .then_inc(raw_landed[c], 16)
                    sp.dma_start(raw[:, c, KQ * P:(KQ + KKV) * P].rearrange("p (k m) -> p k m", k=KKV),
                                 ukv[:, :, ds(i, 1), h, 0].rearrange("p k a d -> p k (a d)")) \
                      .then_inc(kw_landed[h], 16)
                head_halves(0, i * 4 + (U_ATT - 3), raw[:, 0, 0:W_QR].rearrange("p (k h e) -> p k h e", k=KQ, h=2),
                            lambda h: uq[:, :, ds(i, 1), h, NOPE:NOPE + ROPE].rearrange("p k a e -> p k (a e)"), dup_landed[0])
                queries_keys(1, 0, i * 4 + (U_ATT - 2))
                head_halves(2, i * 4 + (U_ATT - 1), raw[:, 2, 0:W_V].rearrange("p (k h d) -> p k h d", k=KKV, h=2),
                            lambda h: ukv[:, :, ds(i, 1), h, 1].rearrange("p k a d -> p k (a d)"), dup_landed[1])
                queries_keys(3, 1, i * 4 + U_ATT)
            rolled(sp, PAIRS, pair_units, peel=0)

            def gate_back(g):
                if g < 2:
                    sp.wait_ge(conv_done, KD)
                    for e in range(2):
                        sp.wait_ge(gate_stored[e], 16 * KD)
                wait(sp, merged, g - 1)
                sp.dma_start(gin[:, g % 2], gates[g]).then_inc(gin_landed[g % 2], 16)

            projections = [t[name][0].rearrange("(k p) n -> p k n", p=P) for name in ("w_o_attn", "w_conv_out")]
            def row_units(w, base, half):
                def body(i, cs=range(4)):
                    for c in cs:
                        wait_apart(sp, lo_ready, i * 4 + (base + c - 3))
                        sp.dma_start(raw[:, c].rearrange("p (k n) -> p k n", k=2),
                                     w[:, ds(i * 4 + c, 1), :, half * HALF:(half + 1) * HALF]
                                     .rearrange("p u k n -> p (u k) n")).then_inc(raw_landed[c], 16)
                return body
            wo = t["w_out"][0].rearrange("(u k p) n -> p u k n", k=2, p=P)
            for g in range(2 * KD + 3):
                m = g % KD
                if g == 2 * KD:
                    sp.wait_ge(c_lo, KD)
                    for e, (name, t0, nt) in enumerate((("x_prompt", 0, 4), ("x_sample", 4, 2))):
                        sp.dma_start(h1[:, t0:t0 + nt], t[name][0].rearrange("(t p) n -> p t n", p=P)) \
                          .then_inc(h_landed[e], 16)
                if g >= 2 * KD:
                    row_units(wo, U_OUT, 0)(0, [g - 2 * KD])
                if g < 2 * KD:
                    columns(projections[g // KD], U_O + g - g % 4, 0, g % 4, slice(m * P, (m + 1) * P))
                if g >= 3:
                    gate_back(g - 3)
            row_units(wo, U_OUT, 0)(0, [3])
            row_units(wo, U_OUT + 4, 1)(0)
            wi = t["w_mlp_in"][0].rearrange("(k p) n -> p k n", p=P)

            def in_units(i):
                for c in range(4):
                    columns(wi, U_IN, i, c, ds(i * (4 * P) + c * P, P))
            rolled(sp, KF // 4, in_units, peel=0)
            wm = t["w_mlp_out"][0].rearrange("(u k p) n -> p u k n", k=2, p=P)
            for half in range(2):
                rolled(sp, KF // 8, row_units(wm, U_FF + 16 * half, half), peel=0)
            sp.wait_ge(relu_ready, KF)
            sp.dma_start(gfinal[:, :], t["norm_final"].rearrange("(a n) -> a n", a=1).to_broadcast([P, D])) \
              .then_inc(gfinal_landed, 16)
            for i in range(NT):
                dst = t["y_prompt"][0, i * P:(i + 1) * P, :] if i < 4 else t["y_sample"][0, (i - 4) * P:(i - 3) * P, :]
                for made, c0 in ((y_left, 0), (y_out, HALF)):
                    sp.wait_ge(made, i + 1)
                    sp.dma_start(dst[:, c0:c0 + HALF], yout[:, i, c0:c0 + HALF]).then_inc(y_stored, 16)
            sp.wait_ge(y_stored, 2 * 16 * NT)

        @block.scalar
        def _(act):
            act.wait_ge(setup, 5)
            nc.scalar.activation(root[:, 7:8], eps[:, 0:1], ACT.Sqrt)

            def x_rms(j):
                i = X_ORDER[j]
                r = T_META if i == 6 else P
                act.wait_ge(x_landed[i], 16)
                wait(act, x_sq, j)
                nc.scalar.activation(junk0[0:r, :], xt[0:r, i], ACT.Square,
                                     accum_out=sumsq[0:r, i:i + 1]).then_inc(x_sq, 1)
                act.wait_ge(x_sq, j + 1)
                nc.scalar.activation(root[0:r, i:i + 1], sumsq[0:r, i:i + 1], ACT.Sqrt, bias=eps[0:r, 0:1],
                                     scale=1.0 / D).then_inc(x_root, 1)

            def u_hi(k, seg):
                src, cols = u_part(k, seg)
                act.wait_ge(ut_ready, KD * seg + k + 1)
                nc.scalar.activation(uhi[:, k, cols], src, ACT.Copy, scale=vcol("norm_mix", k)).then_inc(uhi_ready, 1)
            for j in range(4):
                x_rms(j)
            hi_unit(act, 0, 0, 0)
            x_rms(4)
            act.wait_ge(vec_ready, 1)
            u_hi(0, 0), u_hi(1, 0), u_hi(2, 0), u_hi(3, 0), x_rms(5)
            u_hi(4, 0), u_hi(5, 0), x_rms(6), u_hi(6, 0), u_hi(7, 0)
            for k in range(3):
                u_hi(k, 1)
            hi_unit(act, 0, 0, 1)
            for k in range(3, KD):
                u_hi(k, 1)

            for n in range(8):
                if n in (5, 6):
                    act.wait_ge(dup_landed[n - 5], 16)
                if n > 0:
                    hi_unit(act, 0, 0, n + 1) if n < 3 else hi_unit(act, 4, 0, n + 1 - 4)
                if n < 6:
                    act.wait_ge(raw_q, n + 1)
                    wait(act, sq_sum, n - 1)
                    src, w = (qraw[:, n], TQ) if n < 4 else (kvraw[:, n - 4], TK)
                    nc.scalar.activation(sqt[:, n % 2, 0:w], src, ACT.Square).then_inc(q_sq, 1)
                if n == 7:
                    act.wait_ge(unit_used, 8)
                    for b in range(4):
                        o = b ^ 1
                        ins = nc.scalar.activation(krsw[32 * o:32 * o + 32, :], psum[32 * b:32 * b + 32, 2, 0:TK], ACT.Copy)
                    ins.then_inc(kr_sw, 1)
            act.wait_ge(ss_mm, 1)
            nc.scalar.activation(sqacc[:, 0, 0:TQ], psum[:, 3, 0:TQ], ACT.Sqrt, bias=eps[:, 0:1],
                                 scale=1.0 / Q_LORA).then_inc(ss_root, 1)

            def kr_split():
                act.wait_ge(kr_rot, 1)
                nc.scalar.activation(kra[0:64, :], krt[0:64, :], ACT.Copy)
                nc.scalar.activation(krb[64:128, :], krt[64:128, :], ACT.Copy).then_inc(kr_hi, 1)

            def latent_hi(j):
                act.wait_ge(qkv_scaled, j + 1)
                dst, src = (qhi[:, j], qraw[:, j]) if j < 4 else (kvhi[:, j - 4], kvraw[:, j - 4])
                nc.scalar.activation(dst, src, ACT.Copy).then_inc(qkv_hi, 1)

            def conv_step(i):
                for c in range(4):
                    hi_unit(act, U_CONV, i, c + 1)
                    if c % 2 == 0:
                        j = i * 2 + c // 2
                        act.wait_ge(unit_used, i * 4 + (U_CONV + c + 1))
                        wait(act, glu_ready, i * 2 + (c // 2 - 1))
                        if isinstance(i, int) and i == 0 and c == 0:
                            act.wait_ge(sq_sum, 6)
                        nc.scalar.activation(sg[:, c // 2], psum[:, 0, 0:TK], ACT.Sigmoid).then_inc(sg_ready, 1)
                    if isinstance(i, int) and i == 0 and c == 0:
                        kr_split()
                    if isinstance(i, int) and i == 0 and c == 2:
                        kv_root(), latent_hi(0), latent_hi(1)
                    if isinstance(i, int) and i == 0 and c == 3:
                        latent_hi(2), latent_hi(3)
                    if isinstance(i, int) and i == 1 and c == 0:
                        latent_hi(4), latent_hi(5)

            def kv_root():
                act.wait_ge(ss_mm, 2)
                nc.scalar.activation(sqacc[:, 1, :], psum[:, 3, 0:TK], ACT.Sqrt, bias=eps[:, 0:1],
                                     scale=1.0 / KV_LORA).then_inc(ss_root, 1)
            conv_step(0)
            conv_step(1)
            with act.Fori(2, 4) as i:
                conv_step(i)

            def gate_step(i):
                for c in range(4):
                    end = isinstance(i, int) and i == 3 and c == 3
                    if end:
                        act.wait_ge(dup_landed[0], 32)
                    hi_unit(act, U_GATE, i, c + 1, W_QR if end else D)
                    act.wait_ge(unit_used, i * 4 + (U_GATE + c + 1))
                    wait(act, gate_stored[c % 2], i * 32 + 16 * (c // 2))
                    if isinstance(i, int) and i == 0 and c == 0:
                        act.wait_ge(qkv_lo, 6)
                    nc.scalar.activation(gout[:, c % 2], psum[:, c % 2, 0:TQ], ACT.Sigmoid,
                                         bias=vcol("b_gate", i * 4 + c)).then_inc(gate_ready, 1)
                    act.wait_ge(gate_ready, i * 4 + (c + 1))
                    dst = gates[ds(i * 4 + c, 1)].rearrange("a p n -> p (a n)") if not isinstance(i, int) else gates[i * 4 + c]
                    act.dma_start(dst, gout[:, c % 2]).then_inc(gate_stored[c % 2], 16)
            rolled(act, 4, gate_step, peel=1, last=1)

            def E(p, hh, q):
                g = p * 12 + (6 * hh + q)
                grp, _ = qtile(q)
                act.wait_ge(max_ready, g + 1)
                wait(act, pt_mm, g - 1)
                n = len(grp["pieces"])
                src = psum[:, q % 2, :].rearrange("p (b n) -> p b n", b=2)[:, 0:n, 0:grp["pieces"][0][1]]
                dst = prob[:, q % 2, 0:grp["nk"]].rearrange("p (b n) -> p b n", b=n)
                nc.scalar.activation(dst, src, ACT.Exp, bias=negmax[:, q % 4:q % 4 + 1],
                                     accum_out=psumexp[:, q % 4:q % 4 + 1]).then_inc(exp_ready, 1)

            def H(p, hh, q):
                g, b = p * 12 + (6 * hh + q), 3 * hh + q // 2
                act.wait_ge(pt_mm, g + 1)
                wait(act, av_mm, p * 6 + (b - 1))
                nc.scalar.activation(pthi[:, b % 2, 0:main_tiles(q), (q % 2) * P:(q % 2 + 1) * P],
                                     bank[:, 4 + q % 2, 0:main_tiles(q) * P].rearrange("p (t n) -> p t n", n=P),
                                     ACT.Copy).then_inc(pt_hi, 1)
                if q % 2 == 1:
                    act.wait_ge(tail_hi, p * 6 + (b + 1))
                    nc.scalar.activation(ptmeta[PACK[2], b % 2], ptmeta[PACK[0], b % 2].bitcast(F32), ACT.Copy) \
                      .then_inc(tail_hi_again, 1)

            def H_tails(p, hh, b):
                blk = 3 * hh + b
                act.wait_ge(pt_mm, p * 12 + (6 * hh + 2 * b + 2))
                wait(act, av_mm, p * 6 + (blk - 1))
                nc.scalar.activation(ptmeta[PACK[0], blk % 2], bank[0:T_META, 6, 0:2 * P], ACT.Copy).then_inc(tail_hi, 1)

            def o_split_hi(h):
                act.wait_ge(o_ready, 3 * h + 3)
                nc.scalar.activation(ohi[:, h], oraw[:, h], ACT.Copy).then_inc(o_hi, 1)

            def O(p, hh, b):
                act.wait_ge(av_mm, p * 6 + (3 * hh + b + 1))
                dst = oraw[:, ds(p * 2 + hh, 1), b * 2 * P:(b + 1) * 2 * P]
                nc.scalar.activation(dst, bank[:, 7, 0:2 * P].rearrange("p (a n) -> p a n", a=1), ACT.Copy) \
                  .then_inc(o_ready, 1)

            def q_hi(p, hh, pair):
                act.wait_ge(qn_mm, p * 2 + (hh + 1))
                nc.scalar.activation(qnhi[:, :], psum[:, pair, 0:TQ], ACT.Copy, scale=SCALE).then_inc(qn_hi, 1)

            def k_hi(p, hh, pair):
                act.wait_ge(unit_used, p * 4 + (U_ATT + 2 + 2 * hh))
                nc.scalar.activation(knhi[:, :], psum[:, pair, 0:TK], ACT.Copy).then_inc(kn_hi, 1)

            def rotary_swap(p):
                act.wait_ge(unit_used, p * 4 + (U_ATT + 1))
                for b in range(4):
                    o = b ^ 1
                    ins = nc.scalar.activation(qsw[32 * o:32 * o + 32, :], psum[32 * b:32 * b + 32, 0, 0:TQ], ACT.Copy)
                ins.then_inc(qr_sw, 1)

            def rotary_hi(p):
                act.wait_ge(qr_rot, p + 1)
                nc.scalar.activation(qrs[0][0:64, :], qt[0:64, :], ACT.Copy, scale=SCALE).then_inc(qr_hi, 1)
                nc.scalar.activation(qrs[1][64:128, :], qt[64:128, :], ACT.Copy, scale=SCALE).then_inc(qr_hi, 1)

            def v_hi_first(p):
                act.wait_ge(v_mm, p * 2 + 1)
                nc.scalar.activation(vhi[:, 0:4], psum[:, 2, :].rearrange("p (t n) -> p t n", t=4), ACT.Copy).then_inc(v_hi, 1)

            def v_hi_rest(p):
                act.wait_ge(v_mm, p * 2 + 2)
                nc.scalar.activation(vhi[:, 4:6], bank[:, 6].rearrange("p (t n) -> p t n", t=2), ACT.Copy).then_inc(v_hi, 1)
                act.wait_ge(unit_used, p * 4 + (U_ATT + 3))
                for part in PACK[0:2]:
                    ins = nc.scalar.activation(vmeta[part, :], bank[0:T_META, 7, 0:2 * VD], ACT.Copy)
                ins.then_inc(v_hi, 1)

            def start_pair(n, between=lambda step: None):
                rotary_swap(n)
                between(0)
                act.wait_ge(dup_landed[1], n * 16 + 32)
                hi_unit(act, U_ATT, n, 2, W_V)
                q_hi(n, 0, 1)
                between(1)
                rotary_hi(n)
                k_hi(n, 0, 0)
                act.wait_ge(kw_landed[1], n * 16 + 16)
                hi_unit(act, U_ATT, n, 3, W_QK)
                between(2)
                v_hi_first(n)

            def pair_step(p):
                final = isinstance(p, int) and p == PAIRS - 1
                for hh in range(2):
                    early = final and hh == 1
                    if hh == 0:
                        E(p, hh, 0), v_hi_rest(p), E(p, hh, 1)
                    else:
                        E(p, hh, 0), E(p, hh, 1), O(p, 0, 2)
                    E(p, hh, 2)
                    if isinstance(p, int) and p == 0 and hh == 0:
                        for e in range(2):
                            act.wait_ge(gate_stored[e], 16 * KD)
                    H(p, hh, 0)
                    H_tails(p, hh, 0), E(p, hh, 3), H(p, hh, 1)
                    E(p, hh, 4), H(p, hh, 2)
                    if hh == 0:
                        if not final:
                            act.wait_ge(dup_landed[0], p * 16 + 48)
                        hi_unit(act, U_ATT, p, 4, D if final else W_QR)
                    else:
                        if not final:
                            act.wait_ge(kw_landed[0], p * 16 + 32)
                        hi_unit(act, U_ATT, p, 5, D if final else W_QK)
                    if early:
                        o_split_hi(2)
                    E(p, hh, 5), H_tails(p, hh, 1), H(p, hh, 3), O(p, hh, 0), H(p, hh, 4)
                    if early:
                        o_split_hi(3)
                    if hh == 0:
                        q_hi(p, 1, 0), k_hi(p, 1, 1), H_tails(p, hh, 2), H(p, hh, 5), O(p, hh, 1)
                        if final:
                            o_split_hi(0), o_split_hi(1)
                    elif not final:
                        rest = (lambda: (H_tails(p, 1, 2), H(p, 1, 5)), lambda: O(p, 1, 1), lambda: O(p, 1, 2))
                        start_pair(p + 1, lambda step: rest[step]())
                    else:
                        H_tails(p, hh, 2), H(p, hh, 5), O(p, hh, 1), O(p, hh, 2)
            act.wait_ge(kw_landed[0], 16)
            hi_unit(act, U_ATT, 0, 1, W_QK)
            start_pair(0)
            act.wait_ge(packs_zero, 2)
            rolled(act, PAIRS, pair_step, peel=1, last=1)

            for h in range(EARLY_HEADS, HEADS):
                o_split_hi(h)
            hi_unit(act, U_O, 0, 2)
            act.wait_ge(mean_mm, 1)
            nc.scalar.activation(mu[:, :], psum[:, 2, 0:TQ], ACT.Copy, scale=1.0 / D).then_inc(mu_ready, 1)
            hi_unit(act, U_O, 0, 3)

            def ln_squares(js):
                for j in js:
                    act.wait_ge(centred, j + 1)
                    wait(act, ln_sqsum, j - 1)
                    nc.scalar.activation(lnsq[:, j % 2], cs[:, j, 0:TQ], ACT.Square).then_inc(ln_sq, 1)
            ln_squares(range(0, 3))
            hi_unit(act, U_O, 0, 4)
            ln_squares(range(3, 6))
            hi_unit(act, U_O, 1, 1)
            ln_squares(range(6, 8))
            hi_unit(act, U_O, 1, 2)
            act.wait_ge(var_mm, 1)
            nc.scalar.activation(lnacc[:, :], psum[:, 3, 0:TQ], ACT.Sqrt, bias=eps[:, 0:1],
                                 scale=1.0 / D).then_inc(ln_root, 1)
            hi_unit(act, U_O, 1, 3)
            for k in range(KD):
                act.wait_ge(ln_scaled, k + 1)
                nc.scalar.activation(cs[:, k, 0:TQ], cs[:, k, 0:TQ], ACT.Silu,
                                     bias=vcol("conv_ln_b", k)).then_inc(c_silu, 1)
                act.wait_ge(c_silu, k + 1)
                nc.scalar.activation(chi[:, k], cs[:, k, 0:TQ], ACT.Copy).then_inc(c_hi, 1)
                if k == 2:
                    hi_unit(act, U_O, 1, 4)
                if k == 6:
                    hi_unit(act, U_CO, 0, 1)

            for m in range(KD):
                if m > 0:
                    hi_unit(act, U_CO, m // 4, m % 4 + 1)
                act.wait_ge(merged, KD + m + 1)
                nc.scalar.activation(zhi[:, m], zacc[:, m], ACT.Copy).then_inc(z_hi, 1)
            def h_square(half, i):
                n = NT * half + i
                act.wait_ge(h_ready, n + 1)
                wait(act, h_sq, n)
                nc.scalar.activation(junk1[:, :], h1[:, i, half * HALF:(half + 1) * HALF], ACT.Square,
                                     accum_out=halfsq[:, half, i:i + 1]).then_inc(h_sq, 1)

            def u2_hi(k):
                act.wait_ge(u2t_ready, k + 1)
                nc.scalar.activation(u2hi[:, k], psum[:, U2_PAIR[k], 0:TQ], ACT.Copy, scale=vcol("norm_mlp", k)).then_inc(u2hi_ready, 1)
            for n in range(1, 6):
                hi_unit(act, U_OUT, 0, n)
            for i in range(NT):
                h_square(0, i)
            hi_unit(act, U_OUT, 0, 6)
            u2_hi(0), u2_hi(1)
            hi_unit(act, U_OUT, 0, 7)
            u2_hi(2), u2_hi(3)
            hi_unit(act, U_IN, 0, 0)
            h_square(1, 0), h_square(1, 1), h_square(1, 2)
            hi_unit(act, U_IN, 0, 1)
            u2_hi(4), h_square(1, 3), u2_hi(5), h_square(1, 4), u2_hi(6), h_square(1, 5), u2_hi(7)
            act.wait_ge(h_ms, 1)
            nc.scalar.activation(root[:, 0:NT], meansq[:, 0:NT], ACT.Sqrt, bias=eps[:, 0:1], scale=1.0 / D).then_inc(h_root, 1)

            def hid_hi(i, c, half):
                n = i * 4 + (U_FF + 16 * half + c)
                if isinstance(n, int) and n == U_FF:
                    act.wait_ge(u2_half_used, 1)
                    act.wait_ge(hid_ready, 2)
                else:
                    act.wait_ge(unit_used, n - 1)
                nc.scalar.activation(hidhi[c % 2][:, :, :], hid[:, ds(i * 8 + 2 * c, 2), :], ACT.Copy).then_inc(hidhi_ready, 1)

            def in_step(i):
                for c in range(4):
                    start = isinstance(i, int) and i == 0
                    if not start:
                        hi_unit(act, U_IN, i, c + 1)
                    elif c != 1:
                        hi_unit(act, U_IN, i, 2 if c == 0 else c + 1)
                    if isinstance(i, int) and i == KF // 4 - 1 and c == 3:
                        hid_hi(0, 0, 0)
                    act.wait_ge(relu_ready, i * 4 + (c + 1))
                    r = hid[:, ds(i * 4 + c, 1), :]
                    nc.scalar.activation(r, r, ACT.Square).then_inc(hid_ready, 1)
            rolled(act, KF // 4, in_step, peel=1, last=1)
            act.wait_ge(hid_ready, KF)

            def y_square(half, i):
                n = NT * half + i
                act.wait_ge(y_ready, n + 1)
                wait(act, y_sq, n)
                nc.scalar.activation(junk2[:, :], h1[:, i, half * HALF:(half + 1) * HALF], ACT.Square,
                                     accum_out=halfsq[:, half, i:i + 1]).then_inc(y_sq, 1)

            def ff_step(half):
                def body(i):
                    for c in range(4):
                        end = isinstance(i, int) and i == 3 and c == 3
                        if end and half == 1:
                            continue
                        hi_unit(act, U_FF + 16 * half, i, c + 1)
                        if end:
                            hid_hi(0, 0, 1)
                        elif c < 3:
                            hid_hi(i, c + 1, half)
                        else:
                            hid_hi(i + 1, 0, half)
                return body
            rolled(act, 4, ff_step(0), peel=0, last=1)
            rolled(act, 4, ff_step(1), peel=0, last=1)

            act.wait_ge(hidlo_ready, KF)
            for i in range(NT):
                y_square(0, i)
            act.wait_ge(y_ms, 1)
            for i in range(NT):
                y_square(1, i)
                act.wait_ge(y_sq, NT + i + 1)
                nc.scalar.activation(root[:, i:i + 1], halfsq[:, 1, i:i + 1], ACT.Sqrt, bias=meansq[:, i:i + 1],
                                     scale=1.0 / D).then_inc(y_root, 1)
                act.wait_ge(y_rstd, i + 1)
                act.wait_ge(y_gain, i + 1)
                nc.scalar.activation(yout[:, i, 0:HALF], yout[:, i, 0:HALF], ACT.Copy, scale=rstd[:, i:i + 1]).then_inc(y_left, 1)

        @block.vector
        def _(dve):
            def x_scale(j):
                i = X_ORDER[j]
                r = T_META if i == 6 else P
                dve.wait_ge(x_root, j + 1)
                nc.vector.reciprocal(rstd[0:r, i:i + 1], root[0:r, i:i + 1]).then_inc(x_rstd, 1)
                dve.wait_ge(x_rstd, j + 1)
                nc.vector.tensor_scalar(xt[0:r, i], xt[0:r, i], rstd[0:r, i:i + 1], None, ALU.mult).then_inc(x_scaled, 1)

            def u_lo(k, seg):
                src, cols = u_part(k, seg)
                dve.wait_ge(uhi_ready, KD * seg + k + 1)
                nc.vector.scalar_tensor_tensor(out=ulo[:, k, cols], in0=src, scalar=vcol("norm_mix", k),
                                               in1=uhi[:, k, cols].bitcast(F32), op0=ALU.mult, op1=ALU.subtract).then_inc(ulo_ready, 1)
            x_scale(0), x_scale(1), x_scale(2), x_scale(3)
            dve.wait_ge(vec_t, 1)
            nc.vector.tensor_copy(vec[:, :], bank[:, 6, 0:NVEC]).then_inc(vec_ready, 1)
            dve.wait_ge(vec_t, 2)
            nc.vector.tensor_copy(convw[:, :, :], bank[:, 7, 0:KD * 32].rearrange("p (k n) -> p k n", k=KD)[:, :, 0:TAPS]).then_inc(vec_ready, 1)
            x_scale(4)
            dve.wait_ge(vec_ready, 2)
            u_lo(0, 0), u_lo(1, 0), u_lo(2, 0), u_lo(3, 0), x_scale(5)
            u_lo(4, 0), u_lo(5, 0), x_scale(6), u_lo(6, 0), u_lo(7, 0)
            for k in range(KD):
                u_lo(k, 1)

            for n in range(6):
                dve.wait_ge(unit_used, n + 1)
                dst, w = (qraw[:, n], TQ) if n < 4 else (kvraw[:, n - 4], TK)
                nc.vector.tensor_copy(dst, psum[:, n % 2, 0:w]).then_inc(raw_q, 1)
            dve.wait_ge(tables_landed, 32)
            dve.wait_ge(kr_sw, 1)
            nc.vector.tensor_tensor(out=krt[:, :], in0=psum[:, 2, 0:TK], in1=rcos[:, :], op=ALU.mult).then_inc(kr_cos, 1)
            dve.wait_ge(kr_cos, 1)
            dve.wait_ge(kr_sin, 1)
            nc.vector.tensor_tensor(out=krt[:, :], in0=krt[:, :], in1=krsw[:, :], op=ALU.add).then_inc(kr_rot, 1)

            def kr_los():
                dve.wait_ge(kr_hi, 1)
                dve.wait_ge(kr_rot, 1)
                nc.vector.tensor_tensor(out=kra[64:128, :], in0=krt[64:128, :], in1=krb[64:128, :].bitcast(F32), op=ALU.subtract)
                nc.vector.tensor_tensor(out=krb[0:64, :], in0=krt[0:64, :], in1=kra[0:64, :].bitcast(F32), op=ALU.subtract).then_inc(kr_lo, 1)

            def recip_q():
                dve.wait_ge(ss_root, 1)
                nc.vector.reciprocal(sqacc[:, 0, 0:TQ], sqacc[:, 0, 0:TQ]).then_inc(ss_rstd, 1)

            def recip_kv():
                dve.wait_ge(ss_root, 2)
                nc.vector.reciprocal(sqacc[:, 1, :], sqacc[:, 1, :]).then_inc(ss_rstd, 1)

            def latent_scale(j):
                dve.wait_ge(ss_rstd, 1 if j < 4 else 2)
                src, g, r = ((qraw[:, j], vcol("norm_q", j), sqacc[:, 0, 0:TQ]) if j < 4 else
                             (kvraw[:, j - 4], vcol("norm_kv", j - 4), sqacc[:, 1, :]))
                nc.vector.scalar_tensor_tensor(out=src, in0=src, scalar=g, in1=r, op0=ALU.mult, op1=ALU.mult).then_inc(qkv_scaled, 1)

            def latent_lo(j):
                dve.wait_ge(qkv_hi, j + 1)
                dst, src, h = ((qlo[:, j], qraw[:, j], qhi[:, j]) if j < 4 else
                               (kvlo[:, j - 4], kvraw[:, j - 4], kvhi[:, j - 4]))
                nc.vector.tensor_tensor(out=dst, in0=src, in1=h.bitcast(F32), op=ALU.subtract).then_inc(qkv_lo, 1)

            def tap(tile, k, before, r=None):
                half = (k if isinstance(k, int) else r) % 2
                a = acc[:, half, 0:SPAN]
                j = tile if isinstance(tile, int) else None
                def pick(x, lo_, n_):
                    return x[:, ds(tile, 1), lo_:lo_ + n_] if j is None else x[:, j:j + 1, lo_:lo_ + n_]
                if isinstance(k, int):
                    src = pick(cs, 1 + k, SPAN).rearrange("p a n -> p (a n)")
                    w = pick(convw, k, 1).rearrange("p a n -> p (a n)")
                else:
                    src = cs[:, j, ds(k + 1, SPAN)]
                    w = convw[:, j, ds(k, 1)]
                if isinstance(k, int) and k == 0:
                    b = vcol("conv_b", tile)
                    ins = nc.vector.tensor_scalar(a, src, w, b, ALU.mult, ALU.add)
                elif isinstance(k, int) and k == 1:
                    ins = nc.vector.tensor_scalar(a, src, w, None, ALU.mult)
                else:
                    dve.wait_ge(tap_done, before - 1)
                    ins = nc.vector.scalar_tensor_tensor(out=a, in0=src, scalar=w, in1=a, op0=ALU.mult, op1=ALU.add)
                ins.then_inc(tap_done, 1)

            def combine(tile, done):
                dve.wait_ge(tap_done, done)
                def out(lo_, n_):
                    return (cs[:, ds(tile, 1), lo_:lo_ + n_].rearrange("p a n -> p (a n)") if not isinstance(tile, int)
                            else cs[:, tile, lo_:lo_ + n_])
                nc.vector.tensor_tensor(out=out(0, T_PROMPT), in0=acc[:, 0, 0:T_PROMPT], in1=acc[:, 1, 0:T_PROMPT], op=ALU.add)
                nc.vector.tensor_tensor(out=out(T_PROMPT, T_SAMPLE), in0=acc[:, 0, ACC_SAMPLE:ACC_SAMPLE + T_SAMPLE],
                                        in1=acc[:, 1, ACC_SAMPLE:ACC_SAMPLE + T_SAMPLE], op=ALU.add).then_inc(conv_done, 1)

            def conv_part(tile, c):
                if c == 0:
                    wait(dve, conv_done, tile)
                for k in range(8 * c, min(8 * c + 8, TAPS)):
                    tap(tile, k, tile * TAPS + k)
                if c == 3:
                    combine(tile, tile * TAPS + TAPS)

            def glu(i, c):
                j = i * 2 + c // 2
                dve.wait_ge(sg_ready, i * 2 + (c // 2 + 1))
                dve.wait_ge(unit_used, i * 4 + (U_CONV + c + 1))
                def dst(lo_, n_):
                    return cs[:, ds(j, 1), lo_:lo_ + n_].rearrange("p a n -> p (a n)") if not isinstance(j, int) else cs[:, j, lo_:lo_ + n_]
                s = sg[:, c // 2]
                for o, c0, n in ((CS_PROMPT, 0, T_PROMPT), (CS_META2, META0, T_META + T_SAMPLE), (0, META0, T_META)):
                    ins = nc.vector.tensor_tensor(out=dst(o, n), in0=psum[:, 1, c0:c0 + n], in1=s[:, c0:c0 + n], op=ALU.mult)
                ins.then_inc(glu_ready, 1)

            dve.wait_ge(pads_zero, 2)
            kr_los(), recip_q()
            glu(0, 1)
            for j in range(KQ):
                latent_scale(j)
            latent_lo(0)
            glu(0, 3)
            latent_lo(1), latent_lo(2), latent_lo(3)
            recip_kv(), latent_scale(4), latent_scale(5)
            dve.wait_ge(glu_ready, 1)
            conv_part(0, 0)

            def conv_step(i, order):
                dve.wait_ge(glu_ready, i * 2)
                for what in order:
                    if isinstance(what, str):
                        glu(i, 1 if what == "first glu" else 3)
                    else:
                        conv_part(i - 1, what)
            conv_step(1, ("first glu", 1, 2, "second glu", 3))
            latent_lo(4)
            latent_lo(5)
            with dve.Fori(2, 4) as i:
                conv_step(i, (0, "first glu", 1, 2, "second glu", 3))

            dve.wait_ge(glu_ready, KD)
            with dve.Fori(3, 6) as tile:
                for c in range(4):
                    conv_part(tile, c)
            for c in range(3):
                conv_part(6, c)
            for k in range(24, 28):
                tap(6, k, 6 * TAPS + k)

            LAST = KD - 1

            def conv_handover():
                for k in range(29, TAPS):
                    tap(6, k, 6 * TAPS + k)
                combine(6, LAST * TAPS)
                dve.wait_ge(conv_done, LAST)
                for k in range(FIRST_TAPS):
                    tap(LAST, k, LAST * TAPS + k)

            def M(p, hh, q):
                g = p * 12 + (6 * hh + q)
                grp, _ = qtile(q)
                n = len(grp["pieces"])
                dve.wait_ge(s_ready, g + 1)
                src = psum[:, q % 2, :].rearrange("p (b n) -> p b n", b=2)[:, 0:n, 0:grp["pieces"][0][1]]
                nc.vector.tensor_reduce(out=negmax[:, q % 4:q % 4 + 1], in_=src, axis=AX.XY, op=ALU.max,
                                        negate=True).then_inc(max_ready, 1)

            def R(p, hh, q):
                g = p * 12 + (6 * hh + q)
                dve.wait_ge(exp_ready, g + 1)
                nc.vector.reciprocal(rsum[:, q % 4:q % 4 + 1], psumexp[:, q % 4:q % 4 + 1]).then_inc(rsum_ready, 1)

            def L(p, hh, q):
                g, b = p * 12 + (6 * hh + q), 3 * hh + q // 2
                dve.wait_ge(pt_hi, g + 1)
                sl = (slice(None), b % 2, slice(0, main_tiles(q)), slice((q % 2) * P, (q % 2 + 1) * P))
                nc.vector.tensor_tensor(out=ptlo[sl], in0=bank[:, 4 + q % 2, 0:main_tiles(q) * P].rearrange("p (t n) -> p t n", n=P),
                                        in1=pthi[sl].bitcast(F32), op=ALU.subtract).then_inc(pt_lo, 1)

            def L_tails(p, hh, b):
                slot = (3 * hh + b) % 2
                dve.wait_ge(tail_hi, p * 6 + (3 * hh + b + 1))
                nc.vector.tensor_tensor(out=ptmeta[PACK[1], slot], in0=bank[0:T_META, 6, 0:2 * P],
                                        in1=ptmeta[PACK[0], slot].bitcast(F32), op=ALU.subtract).then_inc(tail_lo, 1)

            def q_lo(p, hh, pair):
                dve.wait_ge(qn_hi, p * 2 + (hh + 1))
                nc.vector.scalar_tensor_tensor(out=qnlo[:, :], in0=psum[:, pair, 0:TQ], scalar=SCALE, in1=qnhi[:, :].bitcast(F32),
                                               op0=ALU.mult, op1=ALU.subtract).then_inc(qn_lo, 1)

            def k_lo(p, hh, pair):
                dve.wait_ge(kn_hi, p * 2 + (hh + 1))
                nc.vector.tensor_tensor(out=knlo[:, :], in0=psum[:, pair, 0:TK], in1=knhi[:, :].bitcast(F32),
                                        op=ALU.subtract).then_inc(kn_lo, 1)

            def rotary_cos(p):
                dve.wait_ge(qr_sw, p + 1)
                nc.vector.tensor_tensor(out=qt[:, 0:T_PROMPT], in0=psum[:, 0, 0:T_PROMPT], in1=rcos[:, 0:T_PROMPT], op=ALU.mult)
                nc.vector.tensor_tensor(out=qt[:, T_PROMPT:TQ], in0=psum[:, 0, T_PROMPT:TQ], in1=rcos[:, SAMP0:TK], op=ALU.mult).then_inc(qr_cos, 1)

            def rotary_sum_lo(p, between=lambda step: None):
                dve.wait_ge(qr_cos, p + 1)
                dve.wait_ge(qr_sin, p + 1)
                nc.vector.tensor_tensor(out=qt[:, :], in0=qt[:, :], in1=qsw[:, :], op=ALU.add).then_inc(qr_rot, 1)
                between(0)
                dve.wait_ge(qr_hi, p * 2 + 1)
                dve.wait_ge(qr_rot, p + 1)
                nc.vector.scalar_tensor_tensor(out=qrs[0][64:128, :], in0=qt[0:64, :], scalar=SCALE, in1=qrs[0][0:64, :].bitcast(F32),
                                               op0=ALU.mult, op1=ALU.subtract)
                dve.wait_ge(qr_hi, p * 2 + 2)
                nc.vector.scalar_tensor_tensor(out=qrs[1][0:64, :], in0=qt[64:128, :], scalar=SCALE, in1=qrs[1][64:128, :].bitcast(F32),
                                               op0=ALU.mult, op1=ALU.subtract).then_inc(qr_lo, 1)

            def v_lo_first(p):
                dve.wait_ge(v_hi, p * 3 + 1)
                nc.vector.tensor_tensor(out=vlo[:, 0:4], in0=psum[:, 2, :].rearrange("p (t n) -> p t n", t=4),
                                        in1=vhi[:, 0:4].bitcast(F32), op=ALU.subtract).then_inc(v_lo, 1)

            def v_lo_rest(p, e):
                dve.wait_ge(v_hi, p * 3 + (2 + e))
                if e == 0:
                    nc.vector.tensor_tensor(out=vlo[:, 4:6], in0=bank[:, 6].rearrange("p (t n) -> p t n", t=2),
                                            in1=vhi[:, 4:6].bitcast(F32), op=ALU.subtract).then_inc(v_lo, 1)
                else:
                    nc.vector.tensor_tensor(out=vmeta[PACK[2], :], in0=bank[0:T_META, 7, 0:2 * VD],
                                            in1=vmeta[PACK[0], :].bitcast(F32), op=ALU.subtract).then_inc(v_lo, 1)

            def start_pair(n, between=lambda step: None):
                rotary_cos(n)
                between(0)
                if isinstance(n, int) and n == 0:
                    rotary_sum_lo(n, lambda step: q_lo(n, 0, 1))
                else:
                    q_lo(n, 0, 1)
                    rotary_sum_lo(n)
                k_lo(n, 0, 0)
                between(1)
                v_lo_first(n)

            def o_split_lo(h):
                dve.wait_ge(o_hi, h + 1)
                nc.vector.tensor_tensor(out=olo[:, h], in0=oraw[:, h], in1=ohi[:, h].bitcast(F32), op=ALU.subtract).then_inc(o_lo, 1)

            def pair_step(p):
                final = isinstance(p, int) and p == PAIRS - 1

                def taps(a, b):
                    for r in range(a, b):
                        tap(LAST, p * PAIR_TAPS + (FIRST_TAPS + r), p * PAIR_TAPS + (LAST * TAPS + FIRST_TAPS + r), FIRST_TAPS + r)
                for hh in range(2):
                    if hh == 0:
                        M(p, hh, 0), R(p, hh, 0), M(p, hh, 1), v_lo_rest(p, 0), R(p, hh, 1), M(p, hh, 2), v_lo_rest(p, 1)
                    else:
                        M(p, hh, 0), M(p, hh, 1), R(p, hh, 0), R(p, hh, 1), M(p, hh, 2)
                    R(p, hh, 2), M(p, hh, 3), L(p, hh, 0)
                    L_tails(p, hh, 0), R(p, hh, 3), M(p, hh, 4), L(p, hh, 1)
                    R(p, hh, 4), M(p, hh, 5), L(p, hh, 2)
                    if final and hh == 1:
                        o_split_lo(0)
                    L_tails(p, hh, 1), R(p, hh, 5), L(p, hh, 3), L(p, hh, 4)
                    first = isinstance(p, int) and p == 0
                    if first and hh == 0:
                        conv_handover()
                    taps(*(((0, 2), (2, 2)) if final else ((0, 1), (2, 8)) if first else ((0, 3), (3, 8)))[hh])
                    if hh == 0:
                        q_lo(p, 1, 0), k_lo(p, 1, 1), L_tails(p, hh, 2), L(p, hh, 5)
                        if first:
                            taps(1, 2)
                    elif not final:
                        rest = (lambda: (L_tails(p, 1, 2), L(p, 1, 5)), lambda: None)
                        start_pair(p + 1, lambda step: rest[step]())
                    else:
                        o_split_lo(1), L_tails(p, hh, 2), L(p, hh, 5)
                        taps(2, 3)
            start_pair(0, lambda step: tap(6, 28, 6 * TAPS + 28) if step == 1 else None)
            rolled(dve, PAIRS, pair_step, peel=1, last=1)

            for h in range(2, HEADS):
                o_split_lo(h)
                if 3 <= h < 6:
                    tap(LAST, TAPS - 6 + h, LAST * TAPS + TAPS - 6 + h)
            combine(LAST, KD * TAPS)

            def gate_attn(m):
                dve.wait_ge(unit_used, U_O + m + 1)
                dve.wait_ge(gin_landed[m % 2], 16 * (m // 2 + 1))
                nc.vector.tensor_tensor(out=zacc[:, m], in0=psum[:, m % 2, 0:TQ], in1=gin[:, m % 2], op=ALU.mult).then_inc(merged, 1)

            def centre(js):
                dve.wait_ge(mu_ready, 1)
                for j in js:
                    dve.wait_ge(conv_done, KD)
                    nc.vector.tensor_tensor(out=cs[:, j, 0:TQ], in0=cs[:, j, 0:TQ], in1=mu[:, :], op=ALU.subtract).then_inc(centred, 1)

            def ln_scale(k):
                dve.wait_ge(ln_rstd, 1)
                nc.vector.scalar_tensor_tensor(out=cs[:, k, 0:TQ], in0=cs[:, k, 0:TQ], scalar=vcol("conv_ln_g", k), in1=lnr[:, :],
                                               op0=ALU.mult, op1=ALU.mult).then_inc(ln_scaled, 1)

            def c_low(k):
                dve.wait_ge(c_hi, k + 1)
                nc.vector.tensor_tensor(out=clo[:, k], in0=cs[:, k, 0:TQ], in1=chi[:, k].bitcast(F32), op=ALU.subtract).then_inc(c_lo, 1)
            gate_attn(0)
            centre(range(0, 5))
            gate_attn(1)
            centre(range(5, 8))
            gate_attn(2), gate_attn(3), gate_attn(4)
            dve.wait_ge(ln_root, 1)
            dve.wait_ge(centred, KD)
            nc.vector.reciprocal(lnr[:, :], lnacc[:, :]).then_inc(ln_rstd, 1)
            gate_attn(5)
            ln_scale(0), ln_scale(1), c_low(0), ln_scale(2), c_low(1), ln_scale(3), c_low(2)
            gate_attn(6)
            ln_scale(4), c_low(3), ln_scale(5), c_low(4), ln_scale(6), c_low(5), ln_scale(7), c_low(6)
            gate_attn(7)
            c_low(7)

            for m in range(KD):
                dve.wait_ge(unit_used, U_CO + m + 1)
                dve.wait_ge(gin_landed[m % 2], 16 * ((KD + m) // 2 + 1))
                nc.vector.tensor_tensor(out=gconv[:, :], in0=psum[:, m % 2, 0:TQ], in1=gin[:, m % 2], op=ALU.mult).then_inc(gated, 1)
                dve.wait_ge(gated, m + 1)
                dve.wait_ge(merged, KD + m)
                nc.vector.tensor_tensor(out=zacc[:, m], in0=zacc[:, m], in1=gconv[:, :], op=ALU.add).then_inc(merged, 1)
                dve.wait_ge(z_hi, m + 1)
                nc.vector.tensor_tensor(out=zlo[:, m], in0=zacc[:, m], in1=zhi[:, m].bitcast(F32), op=ALU.subtract).then_inc(z_lo, 1)

            def tile_made(s, units, half, i):
                if i < NT - 1:
                    dve.wait_ge(s, (NT - 1) * half + i + 1)
                else:
                    dve.wait_ge(unit_used, units)

            def h_add(half):
                for i in range(NT):
                    tile_made(out_tile, U_OUT + 4 * (half + 1), half, i)
                    dve.wait_ge(h_landed[0 if i < 4 else 1], 16)
                    hx = h1[:, i, half * HALF:(half + 1) * HALF]
                    nc.vector.tensor_tensor(out=hx, in0=bank[:, (4 + 6 * half + i) % 8], in1=hx, op=ALU.add).then_inc(h_ready, 1)

            def u2_lo(k):
                dve.wait_ge(u2hi_ready, k + 1)
                nc.vector.scalar_tensor_tensor(out=u2lo[:, k], in0=psum[:, U2_PAIR[k], 0:TQ], scalar=vcol("norm_mlp", k),
                                               in1=u2hi[:, k].bitcast(F32), op0=ALU.mult, op1=ALU.subtract).then_inc(u2lo_ready, 1)
            h_add(0)
            u2_lo(0), u2_lo(1), u2_lo(2), u2_lo(3)
            h_add(1)
            u2_lo(4), u2_lo(5), u2_lo(6)
            dve.wait_ge(h_sq, 2 * NT)
            nc.vector.tensor_tensor(out=meansq[:, 0:NT], in0=halfsq[:, 0, 0:NT], in1=halfsq[:, 1, 0:NT], op=ALU.add).then_inc(h_ms, 1)
            u2_lo(7)
            dve.wait_ge(h_root, 1)
            nc.vector.reciprocal(rstd[:, 0:NT], root[:, 0:NT]).then_inc(h_rstd, 1)
            dve.wait_ge(h_rstd, 1)
            for i in range(NT):
                nc.vector.tensor_scalar(diag[:, i], ident[:, :], rstd[:, i:i + 1], None, ALU.mult).then_inc(diag_ready, 1)
            dve.wait_ge(rbc_mm, 1)
            nc.vector.tensor_copy(rbc[:, :], psum[:, 2, 0:TQ]).then_inc(rbc_ready, 1)
            dve.wait_ge(rbc_ready, 1)

            def hid_lo(i, c, half):
                dve.wait_ge(hidhi_ready, i * 4 + (16 * half + c + 1))
                nc.vector.tensor_tensor(out=hidlo[c % 2][:, :, :], in0=hid[:, ds(i * 8 + 2 * c, 2), :],
                                        in1=hidhi[c % 2][:, :, :].bitcast(F32), op=ALU.subtract).then_inc(hidlo_ready, 1)

            def in_step(i):
                for c in range(4):
                    if isinstance(i, int) and i == KF // 4 - 1 and c == 3:
                        hid_lo(0, 0, 0)
                    dve.wait_ge(unit_used, i * 4 + (U_IN + c + 1))
                    pair = c % 2
                    nc.vector.scalar_tensor_tensor(out=hid[:, ds(i * 4 + c, 1), :], in0=psum[:, pair:pair + 1, 0:TQ], scalar=0.0,
                                                   in1=rbc[:, :].rearrange("p (a n) -> p a n", a=1), op0=ALU.max, op1=ALU.mult).then_inc(relu_ready, 1)
            rolled(dve, KF // 4, in_step, peel=1, last=1)

            def y_add(half, i):
                tile_made(y_tile, U_FF + 16 * (half + 1), half, i)
                hx = h1[:, i, half * HALF:(half + 1) * HALF]
                nc.vector.tensor_tensor(out=hx, in0=bank[:, (4 + 6 * half + i) % 8], in1=hx, op=ALU.add).then_inc(y_ready, 1)

            for half in range(2):
                def ff_step(i):
                    for c in range(4):
                        if not (isinstance(i, int) and half == 0 and c == 0):
                            hid_lo(i, c, half)
                        if half == 1 and c == 0 and isinstance(i, int):
                            for tt in range(NT):
                                y_add(0, tt)
                rolled(dve, 4, ff_step, peel=1)
            dve.wait_ge(y_sq, NT)
            nc.vector.tensor_scalar(meansq[:, 0:NT], halfsq[:, 0, 0:NT], 1.0 / D, EPS, ALU.mult, ALU.add).then_inc(y_ms, 1)
            dve.wait_ge(gfinal_landed, 16)

            def y_finish(i):
                dve.wait_ge(y_root, i + 1)
                nc.vector.reciprocal(rstd[:, i:i + 1], root[:, i:i + 1]).then_inc(y_rstd, 1)
                dve.wait_ge(y_rstd, i + 1)
                dve.wait_ge(y_ready, NT + i + 1)
                nc.vector.scalar_tensor_tensor(out=yout[:, i, HALF:D], in0=h1[:, i, HALF:D], scalar=rstd[:, i:i + 1],
                                               in1=gfinal[:, HALF:D], op0=ALU.mult, op1=ALU.mult).then_inc(y_out, 1)
            for i in range(NT):
                y_add(1, i)
                if i > 0:
                    y_finish(i - 1)
            y_finish(NT - 1)

        @block.gpsimd
        def _(gp):
            gp.memset(tapsrows[:, :], 0.0).then_inc(vec_clear, 1)
            gp.memset(sumsq[:, :], 1.0).then_inc(setup, 1)
            gp.memset(ident[:, :], 0.0).then_inc(setup, 1)
            gp.memset(ones[:, :], 1.0).then_inc(setup, 1)
            gp.memset(eps[:, :], EPS).then_inc(setup, 1)
            gp.wait_ge(setup, 4)
            gp.affine_select(out=ident[:, :], in_=ident[:, :], compare_op=ALU.not_equal, fill=1.0, base=0,
                             pattern=[[-1, P]], channel_multiplier=1).then_inc(setup, 1)
            gp.memset(lnsum[:, :], 0.0).then_inc(lnsum_done, 1)
            lo_unit(gp, 0, 0, 0)
            lo_unit(gp, 0, 0, 1)
            gp.wait_ge(ut_ready, 2 * KD)
            gp.memset(cs[:, :, CS_GAP:CS_META2], 0.0).then_inc(pads_zero, 1)
            gp.memset(cs[:, :, CS_END:CS_END + PAD], 0.0).then_inc(pads_zero, 1)

            for n in range(8):
                if n > 0:
                    lo_unit(gp, 0, 0, n + 1) if n < 3 else lo_unit(gp, 4, 0, n + 1 - 4)
                if n < 6:
                    gp.wait_ge(q_sq, n + 1)
                    w, a = (TQ, 0) if n < 4 else (TK, 1)
                    if n in (0, 4):
                        gp.tensor_scalar(sqacc[:, a, 0:w], sqt[:, n % 2, 0:w], 1.0, 1.0, ALU.mult, ALU.mult).then_inc(sq_sum, 1)
                    else:
                        gp.wait_ge(sq_sum, n)
                        gp.tensor_tensor(out=sqacc[:, a, 0:w], in0=sqacc[:, a, 0:w], in1=sqt[:, n % 2, 0:w], op=ALU.add).then_inc(sq_sum, 1)
            gp.wait_ge(kr_sw, 1)
            gp.wait_ge(tables_landed, 32)
            gp.tensor_tensor(out=krsw[:, :], in0=krsw[:, :], in1=rsin[:, :], op=ALU.mult).then_inc(kr_sin, 1)

            def conv_step(i):
                for c in range(4):
                    lo_unit(gp, U_CONV, i, c + 1)
            rolled(gp, 4, conv_step, peel=0)

            def ln_add(tile):
                gp.wait_ge(conv_done, tile + 1)
                gp.wait_ge(lnsum_done, tile + 1)
                src = cs[:, ds(tile, 1), 0:TQ].rearrange("p a n -> p (a n)") if not isinstance(tile, int) else cs[:, tile, 0:TQ]
                gp.tensor_tensor(out=lnsum[:, :], in0=lnsum[:, :], in1=src, op=ALU.add).then_inc(lnsum_done, 1)

            def gate_step(i):
                for c in range(4):
                    lo_unit(gp, U_GATE, i, c + 1, W_QR if isinstance(i, int) and i == 3 and c == 3 else D)
                    if c == 1 and not (isinstance(i, int) and i == 0):
                        ln_add(i - 1)
            rolled(gp, 4, gate_step, peel=1, last=1)

            def start_pair(n):
                gp.wait_ge(qr_sw, n + 1)
                gp.tensor_tensor(out=qsw[:, 0:T_PROMPT], in0=qsw[:, 0:T_PROMPT], in1=rsin[:, 0:T_PROMPT], op=ALU.mult)
                gp.tensor_tensor(out=qsw[:, T_PROMPT:TQ], in0=qsw[:, T_PROMPT:TQ], in1=rsin[:, SAMP0:TK], op=ALU.mult).then_inc(qr_sin, 1)
                lo_unit(gp, U_ATT, n, 2, W_V)
                lo_unit(gp, U_ATT, n, 3, W_QK)

            def pair_step(p):
                final = isinstance(p, int) and p == PAIRS - 1
                for hh in range(2):
                    for q in range(6):
                        g = p * 12 + (6 * hh + q)
                        n = qtile(q)[0]["nk"]
                        wait_apart(gp, rsum_ready, g + 1)
                        gp.tensor_scalar(prob[:, q % 2, 0:n], prob[:, q % 2, 0:n], rsum[:, q % 4:q % 4 + 1], 1.0,
                                         ALU.mult, ALU.mult).then_inc(p_ready, 1)
                    lo_unit(gp, U_ATT, p, 4 + hh, D if final else (W_QR, W_QK)[hh])
                    if hh == 0:
                        ln_add(p + 3)
                if not final:
                    start_pair(p + 1)
            lo_unit(gp, U_ATT, 0, 1, W_QK)
            gp.wait_ge(unit_used, U_ATT)
            gp.memset(vmeta[:, :].bitcast(F32), 0.0).then_inc(packs_zero, 1)
            gp.memset(ptmeta[:, :, :].bitcast(F32), 0.0).then_inc(packs_zero, 1)
            start_pair(0)
            rolled(gp, PAIRS, pair_step, peel=1, last=1)

            ln_add(KD - 1)
            lo_unit(gp, U_O, 0, 2)
            lo_unit(gp, U_O, 0, 3)

            def ln_sq_add(js):
                for j in js:
                    gp.wait_ge(ln_sq, j + 1)
                    if j == 0:
                        gp.tensor_scalar(lnacc[:, :], lnsq[:, 0], 1.0, 1.0, ALU.mult, ALU.mult).then_inc(ln_sqsum, 1)
                    else:
                        gp.wait_ge(ln_sqsum, j)
                        gp.tensor_tensor(out=lnacc[:, :], in0=lnacc[:, :], in1=lnsq[:, j % 2], op=ALU.add).then_inc(ln_sqsum, 1)
            ln_sq_add(range(0, 3))
            lo_unit(gp, U_O, 0, 4)
            ln_sq_add(range(3, 6))
            lo_unit(gp, U_O, 1, 1)
            ln_sq_add(range(6, 8))
            lo_unit(gp, U_O, 1, 2)
            lo_unit(gp, U_O, 1, 3)
            for n in range(U_O + KD, U_IN + 1):
                lo_unit(gp, n - n % 4, 0, n % 4)

            def in_step(i):
                for c in range(4):
                    lo_unit(gp, U_IN, i, c + 1)
            rolled(gp, KF // 4, in_step, peel=0)
            with gp.Fori(0, 7) as i:
                for c in range(4):
                    lo_unit(gp, U_FF, i, c + 1)
            for c in range(3):
                lo_unit(gp, U_FF, 7, c + 1)
            gp.wait_ge(gfinal_landed, 16)
            gp.wait_ge(unit_used, U_FF)
            for i in range(NT):
                gp.wait_ge(y_ready, i + 1)
                gp.tensor_tensor(out=yout[:, i, 0:HALF], in0=h1[:, i, 0:HALF], in1=gfinal[:, 0:HALF], op=ALU.mult).then_inc(y_gain, 1)

        @block.tensor
        def _(pe):
            def x_transpose(k, i):
                r = T_META if i == 6 else P
                out, col = (bank[:, k], i * P) if i < 4 else (bank[:, 4 + k % 4], (T_META + (i - 4) * P) if i < 6 else 0)
                return nc.tensor.transpose(out[:, col:col + r], xt[0:r, i, k * P:(k + 1) * P], ident[0:r, 0:r])
            pe.wait_ge(setup, 5)
            for i in range(4):
                pe.wait_ge(x_scaled, i + 2)
                for k in range(6):
                    mm = x_transpose(k, i)
                    if i == 3:
                        mm.then_inc(ut_ready, 1)
                if i == 2:
                    pe.wait_ge(consts_landed, 16 * len(VEC))
                    nc.tensor.transpose(bank[:, 6, 0:NVEC], vecrows[0:NVEC, :], ident[0:NVEC, 0:NVEC]).then_inc(vec_t, 1)
                    pe.wait_ge(taps_landed, 16)
                    for k in range(KD):
                        mm = nc.tensor.transpose(bank[:, 7, k * 32:(k + 1) * 32], tapsrows[:, k * P:(k + 1) * P], ident[0:32, 0:32])
                    mm.then_inc(vec_t, 1)
            pe.wait_ge(vec_ready, 2)
            for k in (6, 7):
                for i in range(4):
                    mm = x_transpose(k, i)
                mm.then_inc(ut_ready, 1)

            def sample_transposes(ks):
                for k in ks:
                    pe.wait_ge(ulo_ready, k + (5 if k < 4 else KD - 3))
                    for i in (4, 5, 6):
                        mm = x_transpose(k, i)
                    mm.then_inc(ut_ready, 1)

            def first_units(n, seg, ks):
                wh, wl = weights(n, KD)
                c0, w = ((0, T_PROMPT), (SAMP0, T_SAMPLE))[seg]
                for k in ks:
                    pe.wait_ge(ulo_ready, KD * seg + k + 1)
                    for step, (a, b) in enumerate(((wh, uhi), (wh, ulo), (wl, uhi))):
                        mm = nc.tensor.matmul(bank[:, 2 * n + seg, 0:w], a[:, k], b[:, k, c0:c0 + w],
                                              start=k == 0 and step == 0, stop=k == KD - 1 and step == 2)
                if seg == 1 and ks[-1] == KD - 1:
                    mm.then_inc(unit_used, 1)
            pe.wait_ge(lo_ready, 1)
            first_units(0, 0, range(KD))
            pe.wait_ge(x_scaled, 7)
            sample_transposes(range(4))
            first_units(0, 1, range(4))
            sample_transposes(range(4, KD))
            first_units(0, 1, range(4, KD))
            pe.wait_ge(lo_ready, 2)
            first_units(1, 0, range(KD))
            first_units(1, 1, range(KD))

            u = (uhi, ulo)

            def unit(base, i, c, pair, rhs, segments, k_tiles=range(KD), first=True, last=True, rhs_ready=None,
                     after=lambda k, mm: None):
                pe.wait_ge(lo_ready, i * 4 + (base + c + 1))
                wh, wl = weights(c % 2, len(k_tiles))
                for j, k in enumerate(k_tiles):
                    if rhs_ready is not None:
                        rhs_ready(k)
                    mm = products(psum[:, pair], (wh[:, j], wl[:, j]), rhs, k, segments,
                                  first and j == 0, last and j == len(k_tiles) - 1)
                    after(k, mm)
                mm.then_inc(unit_used, 1)

            for n in range(2, 6):
                pe.wait_ge(raw_q, n - 1)
                unit(4 * (n // 4), 0, n % 4, n % 2, u, QSEG if n < 4 else KSEG)
            for e in range(2):
                unit(4, 0, 2 + e, 2, u, KSEG, k_tiles=range(4 * e, 4 * e + 4), first=e == 0, last=e == 1)
                if e == 0:
                    sum_squares(pe, 0, TQ, 4)
            pe.wait_ge(raw_q, 6)

            def conv_step(i):
                for c in range(4):
                    if c % 2 == 0:
                        wait(pe, sg_ready, i * 2 + c // 2)
                    else:
                        wait(pe, glu_ready, i * 2 + c // 2)
                    unit(U_CONV, i, c, c % 2, u, KSEG)
                    if isinstance(i, int) and i == 0 and c == 0:
                        pe.wait_ge(ss_root, 1)
                        sum_squares(pe, 1, TK, 6)
            rolled(pe, 4, conv_step, peel=1)

            def gate_step(i):
                for c in range(4):
                    if isinstance(i, int) and i == 0 and c < 2:
                        pe.wait_ge(sg_ready if c == 0 else glu_ready, KD)
                    wait(pe, gate_ready, i * 4 + (c - 1))
                    unit(U_GATE, i, c, c % 2, u, QSEG)
            rolled(pe, 4, gate_step, peel=1)

            pe.wait_ge(qkv_lo, KQ + KKV)
            pe.wait_ge(kr_lo, 1)
            pe.wait_ge(kr_rot, 1)

            def values(p, js):
                pe.wait_ge(lo_ready, p * 4 + (U_ATT + 3))
                wh, wl = weights(0, KKV, 2 * VD)
                for j in js:
                    out = bank[:, 4 + j // 2, (j % 2) * 2 * VD:(j % 2 + 1) * 2 * VD]
                    if j == 0:
                        wait(pe, pt_lo, p * 12)
                    if j == 4:
                        wait(pe, tail_lo, p * 6)
                    for k in range(KKV):
                        for step, (a, b) in enumerate(((kvhi, wh), (kvlo, wh), (kvhi, wl))):
                            mm = nc.tensor.matmul(out, a[:, k, VTILES[j]:VTILES[j] + P], b[:, k, :],
                                                  start=k == 0 and step == 0, stop=k == KKV - 1 and step == 2)
                    if j in (3, 5):
                        mm.then_inc(v_mm, 1)
                if js[-1] == 5:
                    wait(pe, o_ready, p * 6)
                    for k in range(KKV):
                        for step, (a, b) in enumerate(((kvhi, wh), (kvlo, wh), (kvhi, wl))):
                            mm = nc.tensor.matmul(bank[0:T_META, 7, 0:2 * VD], a[:, k, META0:META0 + T_META], b[:, k, :],
                                                  start=k == 0 and step == 0, stop=k == KKV - 1 and step == 2)
                    mm.then_inc(unit_used, 1)

            def rotary_queries(p):
                unit(U_ATT, p, 0, 0, (qhi, qlo), ZSEG, k_tiles=range(KQ))

            def queries(p, hh, pair):
                pe.wait_ge(lo_ready, p * 4 + (U_ATT + 2 + 2 * hh))
                wh, wl = weights(1, KQ + KKV)
                for k in range(KQ):
                    mm = products(psum[:, pair], (wh[:, k], wl[:, k]), (qhi, qlo), k, ZSEG, k == 0, k == KQ - 1)
                mm.then_inc(qn_mm, 1)

            def keys(hh, pair):
                wh, wl = weights(1, KQ + KKV)
                for k in range(KKV):
                    mm = products(psum[:, pair], (wh[:, KQ + k], wl[:, KQ + k]), (kvhi, kvlo), k, KSEG, k == 0, k == KKV - 1)
                mm.then_inc(unit_used, 1)

            def S(p, hh, q):
                g = p * 12 + (6 * hh + q)
                grp, c0 = qtile(q)
                wait(pe, exp_ready, g - 1)
                ops = [(qnhi, knhi), (qnhi, knlo), (qnlo, knhi), (qrs[hh], kra), (qrs[hh], krb)]
                for step, (a, b) in enumerate(ops):
                    for e, (k0, n) in enumerate(grp["pieces"]):
                        mm = nc.tensor.matmul(psum[:, q % 2, e * HALF:e * HALF + n], a[:, c0:c0 + P],
                                              b[:, grp["k0"] + k0:grp["k0"] + k0 + n],
                                              start=step == 0, stop=step == len(ops) - 1)
                mm.then_inc(s_ready, 1)

            def T(p, hh, q):
                g = p * 12 + (6 * hh + q)
                pe.wait_ge(p_ready, g + 1)
                wait(pe, pt_lo, g - 1)
                if hh == 0 and q == 0:
                    pe.wait_ge(v_lo, p * 3 + 2)
                for e, (_, k0) in enumerate(qtile(q)[0]["tiles"]):
                    nc.tensor.transpose(bank[:, 4 + q % 2, e * P:(e + 1) * P], prob[:, q % 2, k0:k0 + P], ident[:, :])
                if q % 2 == 0:
                    wait(pe, tail_lo, p * 6 + (3 * hh + q // 2))
                m0 = qtile(q)[0]["meta"]
                nc.tensor.transpose(bank[0:T_META, 6, (q % 2) * P:(q % 2 + 1) * P], prob[:, q % 2, m0:m0 + T_META],
                                    ident[:, :]).then_inc(pt_mm, 1)

            def A(p, hh, b):
                blk = 3 * hh + b
                pe.wait_ge(pt_lo, p * 12 + (6 * hh + 2 * b + 2))
                pe.wait_ge(tail_lo, p * 6 + (blk + 1))
                pe.wait_ge(tail_hi_again, p * 6 + (blk + 1))
                if hh == 0 and b == 0:
                    pe.wait_ge(v_lo, p * 3 + 3)
                wait(pe, o_ready, p * 6 + blk)
                tiles = qtile(2 * b)[0]["tiles"]
                for e, (vt, _) in enumerate(tiles):
                    for step, (a, r) in enumerate(((vhi, pthi), (vhi, ptlo), (vlo, pthi))):
                        mm = nc.tensor.matmul(bank[:, 7, 0:2 * P], a[:, vt, hh * VD:(hh + 1) * VD], r[:, blk % 2, e, :],
                                              start=e == 0 and step == 0, stop=False)
                nc.tensor.matmul(bank[:, 7, 0:2 * P], vmeta[:, hh * VD:(hh + 1) * VD], ptmeta[:, blk % 2],
                                 start=False, stop=True).then_inc(av_mm, 1)

            def pair_step(p):
                final = isinstance(p, int) and p == PAIRS - 1
                pe.wait_ge(qr_lo, p + 1)
                for hh in range(2):
                    pe.wait_ge(qn_lo, p * 2 + (hh + 1))
                    pe.wait_ge(kn_lo, p * 2 + (hh + 1))
                    if hh == 0:
                        S(p, hh, 0), values(p, range(4, 6)), S(p, hh, 1)
                    else:
                        S(p, hh, 0), S(p, hh, 1), A(p, 0, 2)
                    S(p, hh, 2), T(p, hh, 0), S(p, hh, 3), T(p, hh, 1), S(p, hh, 4), T(p, hh, 2), S(p, hh, 5)
                    T(p, hh, 3), A(p, hh, 0), T(p, hh, 4)
                    done = p * 12 + 6 * hh
                    if hh == 0:
                        pe.wait_ge(exp_ready, done + 5)
                        queries(p, 1, 0)
                        pe.wait_ge(exp_ready, done + 6)
                        keys(1, 1)
                        T(p, hh, 5)
                        A(p, hh, 1)
                    elif not final:
                        pe.wait_ge(exp_ready, done + 5)
                        rotary_queries(p + 1)
                        T(p, hh, 5)
                        pe.wait_ge(exp_ready, done + 6)
                        queries(p + 1, 0, 1)
                        A(p, hh, 1)
                        pe.wait_ge(qr_cos, p + 2)
                        keys(0, 0)
                        A(p, hh, 2)
                        values(p + 1, range(4))
                    else:
                        T(p, hh, 5), A(p, hh, 1), A(p, hh, 2)
            pe.wait_ge(gate_ready, 2 * KD - 1)
            rotary_queries(0)
            pe.wait_ge(gate_ready, 2 * KD)
            queries(0, 0, 1)
            pe.wait_ge(qr_cos, 1)
            keys(0, 0)
            values(0, range(4))
            rolled(pe, PAIRS, pair_step, peel=1, last=1)

            o = (ohi, olo)

            def column_sums(k):
                if k == 2:
                    pe.wait_ge(lnsum_done, KD + 1)
                    for c0, n in ((0, HALF), (HALF, TQ - HALF)):
                        mm = nc.tensor.matmul(psum[:, 2, c0:c0 + n], ones[:, :], lnsum[:, c0:c0 + n], start=True, stop=True)
                    mm.then_inc(mean_mm, 1)
            for m in range(KD):
                wait(pe, merged, m - 1)
                unit(U_O, m // 4, m % 4, m % 2, o, ZSEG,
                     rhs_ready=(lambda k: pe.wait_ge(o_lo, k + 1)) if m == 0 else (column_sums if m == 1 else None))
                if m == 4:
                    pe.wait_ge(ln_sqsum, KD)
                    for c0, n in ((0, HALF), (HALF, TQ - HALF)):
                        mm = nc.tensor.matmul(psum[:, 3, c0:c0 + n], ones[:, :], lnacc[:, c0:c0 + n], start=True, stop=True)
                    mm.then_inc(var_mm, 1)
            for m in range(KD):
                pe.wait_ge(merged, KD + m - 1)
                unit(U_CO, m // 4, m % 4, m % 2, (chi, clo), ZSEG,
                     rhs_ready=(lambda k: pe.wait_ge(c_lo, k + 1)) if m == 0 else None)

            def token_major(base, bank0, i, units, lhs, lhs_ready, tile_done, free=lambda tt: None,
                            between=lambda c, kk: None):
                for c in range(4):
                    first_unit = isinstance(i, int) and i == 0 and c == 0
                    last_unit = isinstance(i, int) and i == units // 4 - 1 and c == 3
                    pe.wait_ge(lo_ready, i * 4 + (base + c + 1))
                    wh, wl = weights(c % 2, 2, HALF)
                    lhs_ready(i, c)
                    by_tile = first_unit or last_unit
                    order = [(kk, tt) for tt in range(NT) for kk in range(2)] if by_tile else \
                            [(kk, tt) for kk in range(2) for tt in range(NT)]
                    for kk, tt in order:
                        first, last = first_unit and kk == 0, last_unit and kk == 1
                        if not by_tile and tt == 0:
                            between(c, kk)
                        if first:
                            free(tt)
                        out = bank[:, (bank0 + tt) % 8]
                        a_hi, a_lo = lhs(i, c, kk, tt)
                        for step, (a, b) in enumerate(((a_hi, wh), (a_hi, wl), (a_lo, wh))):
                            mm = nc.tensor.matmul(out, a, b[:, kk, :], start=first and step == 0, stop=last and step == 2)
                        if last and tt < NT - 1:
                            mm.then_inc(tile_done, 1)
                    mm.then_inc(unit_used, 1)
            def h_transpose(k):
                wait(pe, u2lo_ready, k if k < 4 else (0 if k < 7 else 5))
                for i in range(NT):
                    mm = nc.tensor.transpose(psum[:, U2_PAIR[k], i * P:(i + 1) * P], h1[:, i, k * P:(k + 1) * P], ident[:, :])
                mm.then_inc(u2t_ready, 1)

            z = lambda i, c, kk, tt: (zhi[:, 2 * c + kk, tt * P:(tt + 1) * P], zlo[:, 2 * c + kk, tt * P:(tt + 1) * P])

            def left_half(c, kk):
                if c in (1, 2):
                    if c == 1 and kk == 0:
                        pe.wait_ge(h_ready, NT)
                    h_transpose(2 * (c - 1) + kk)

            def out_bank_free(half, tt):
                if half == 0 and tt >= 4:
                    pe.wait_ge(merged, 2 * KD - 1)
                elif half == 1 and tt == 0:
                    pe.wait_ge(merged, 2 * KD)
                elif half == 1:
                    wait(pe, h_ready, tt - 1)
            token_major(U_OUT, 4, 0, 4, z, lambda i, c: pe.wait_ge(z_lo, 2 * c + 2), out_tile,
                        free=lambda tt: out_bank_free(0, tt))
            token_major(U_OUT + 4, 10, 0, 4, z, lambda i, c: None, out_tile,
                        free=lambda tt: out_bank_free(1, tt), between=left_half)

            def h_follow(k):
                if k == 1:
                    pe.wait_ge(h_ready, 2 * NT)
                if 1 <= k < 4:
                    h_transpose(k + 3)
                pe.wait_ge(u2lo_ready, max(k + 1, 4))
                if k == 4:
                    h_transpose(7)

            def spread_rms(k):
                if k == 4:
                    pe.wait_ge(diag_ready, NT)
                    for tt in range(NT):
                        mm = nc.tensor.matmul(psum[:, 2, tt * P:(tt + 1) * P], ones[:, :], diag[:, tt], start=True, stop=True)
                    mm.then_inc(rbc_mm, 1)

            def in_step(i):
                for c in range(4):
                    start = isinstance(i, int) and i == 0
                    if start and c == 1:
                        pe.wait_ge(u2lo_ready, KD)
                    wait(pe, relu_ready, i * 4 + (c - 1))
                    if isinstance(i, int) and i == KF // 4 - 1 and c == 3:
                        unit(U_IN, i, c, 1, (u2hi, u2lo), ZSEG, after=lambda k, mm: mm.then_inc(u2_half_used, 1) if k == KD // 2 - 1 else None)
                    elif start and c < 2:
                        unit(U_IN, i, c, c, (u2hi, u2lo), ZSEG, rhs_ready=(h_follow, spread_rms)[c])
                    else:
                        unit(U_IN, i, c, c % 2, (u2hi, u2lo), ZSEG)
            rolled(pe, KF // 4, in_step, peel=1, last=1)

            def ff_bank_free(half, tt):
                if half == 0 and tt >= 4:
                    pe.wait_ge(relu_ready, KF - 1)
                elif half == 1 and tt == 0:
                    pe.wait_ge(relu_ready, KF)
                elif half == 1:
                    wait(pe, y_ready, tt - 1)
            for half in range(2):
                rolled(pe, 4, lambda i: token_major(
                    U_FF + 16 * half, 4 + 6 * half, i, 16,
                    lambda i, c, kk, tt: (hidhi[c % 2][:, kk, tt * P:(tt + 1) * P], hidlo[c % 2][:, kk, tt * P:(tt + 1) * P]),
                    lambda i, c: pe.wait_ge(hidlo_ready, i * 4 + (16 * half + c + 1)), y_tile,
                    free=lambda tt: ff_bank_free(half, tt)), peel=1, last=1)


_INS = ["x_prompt", "x_sample", "meta_tokens", "norm_mix", "w_in", "b_gate", "norm_q", "w_uq", "norm_kv", "w_ukv",
        "w_o_attn", "conv_w", "conv_b", "conv_ln_g", "conv_ln_b", "w_conv_out", "w_out", "norm_mlp", "w_mlp_in",
        "w_mlp_out", "norm_final"]
_OUTS = [("y_prompt", (1, T_PROMPT, D)), ("y_sample", (1, T_SAMPLE, D))]


def rope_tables():
    pos = np.concatenate([T_META + np.arange(T_PROMPT), np.arange(T_META), T_META + np.arange(T_SAMPLE)]).astype(np.float32)
    inv = np.float32(10000.0) ** (-np.arange(0, ROPE, 2, dtype=np.float32) / np.float32(ROPE))
    ang = (inv[:, None] * pos[None, :]).astype(np.float32)
    c, s = np.cos(ang), np.sin(ang)
    return (np.ascontiguousarray(np.concatenate([c, c, c, c]), np.float32),
            np.ascontiguousarray(np.concatenate([-s, s, -s, s]), np.float32))


def kernel(**inputs):
    import concourse.bacc as _bacc
    from concourse.bass_utils import run_bass_kernel_spmd as _run

    nc = _bacc.Bacc("TRN2", target_bir_lowering=False, num_devices=1)
    arrays, t = {}, {}
    for name in _INS:
        a = np.ascontiguousarray(inputs[name])
        arrays[f"in_{name}"] = a
        t[name] = nc.dram_tensor(f"in_{name}", a.shape, F32, kind="ExternalInput").ap()
    for name, a in zip(("rope_cos", "rope_sin"), rope_tables()):
        arrays[name] = a
        t[name] = nc.dram_tensor(name, a.shape, F32, kind="ExternalInput").ap()
    for name, shape in _OUTS:
        t[name] = nc.dram_tensor(f"out_{name}", shape, F32, kind="ExternalOutput").ap()
    build(nc, t)
    r = _run(nc, [arrays], core_ids=[0])
    return tuple(r.results[0][f"out_{name}"] for name, _ in _OUTS)
```
